# Optimizing a Trainium2 kernel written in Bass

```python
import jax, jax.numpy as jnp
from jax import lax
import numpy as np
import math

D_MODEL = 1024
BATCH = 1
SEQ = 512
DEPTH = 1

CHUNK = 64
LEFT_CHUNKS = 8
BAND = (LEFT_CHUNKS + 1) * CHUNK
Q_BLOCK = 128
MLA_HEADS = 8
MLA_Q_RANK = 256
MLA_KV_RANK = 128
MLA_NOPE = 64
MLA_ROPE = 32
MLA_QK = MLA_NOPE + MLA_ROPE
MLA_V = 64
ROPE_THETA = 10000.0
CA_HEADS = 8
CA_HEAD_DIM = 64
REL_CLIP = 128
D_MIX = MLA_HEADS * MLA_V + CA_HEADS * CA_HEAD_DIM
D_IN = MLA_Q_RANK + MLA_KV_RANK + MLA_ROPE + 3 * CA_HEADS * CA_HEAD_DIM
D_FF = 2816
CONV_WIDTH = 3
N_MOD = 6
EPS = 1e-6
NEG_INF = -1e30


def rmsnorm(x, g):
    xf = x.astype(jnp.float32)
    y = xf * lax.rsqrt(jnp.mean(xf * xf, axis=-1, keepdims=True) + EPS)
    return (y * g.astype(jnp.float32)).astype(x.dtype)

def modulate(h, shift, scale):
    return h * (1 + scale[:, None, :]) + shift[:, None, :]

def rope(x, positions):
    half = x.shape[-1] // 2
    inv = jnp.power(ROPE_THETA, -jnp.arange(half, dtype=jnp.float32) / half)
    ang = positions.astype(jnp.float32)[..., None] * inv
    cos = jnp.cos(ang)[:, :, None, :]
    sin = jnp.sin(ang)[:, :, None, :]
    xf = x.astype(jnp.float32)
    x1, x2 = xf[..., :half], xf[..., half:]
    out = jnp.concatenate([x1 * cos - x2 * sin, x2 * cos + x1 * sin], axis=-1)
    return out.astype(x.dtype)

def mla_attention(q, k, v):
    B, S, H, Dq = q.shape
    nqb = S // Q_BLOCK
    scale = Dq ** -0.5
    key_chunk = jnp.arange(S) // CHUNK
    qb = q.reshape(B, nqb, Q_BLOCK, H, Dq).swapaxes(0, 1)

    def block(args):
        qi, i = args
        s = jnp.einsum('bqhd,bkhd->bhqk', qi, k,
                       preferred_element_type=jnp.float32) * scale
        q_chunk = (i * Q_BLOCK + jnp.arange(Q_BLOCK)) // CHUNK
        mask = key_chunk[None, :] <= q_chunk[:, None]
        s = jnp.where(mask[None, None], s, NEG_INF)
        p = jax.nn.softmax(s, axis=-1).astype(v.dtype)
        return jnp.einsum('bhqk,bkhd->bqhd', p, v)

    o = lax.map(block, (qb, jnp.arange(nqb)))
    return o.swapaxes(0, 1).reshape(B, S, H * v.shape[-1])

def chunk_attention(q, k, v, rel_bias):
    B, S, H, D = q.shape
    nc = S // CHUNK
    pad = LEFT_CHUNKS * CHUNK
    scale = D ** -0.5
    k_pad = jnp.pad(k, ((0, 0), (pad, 0), (0, 0), (0, 0)))
    v_pad = jnp.pad(v, ((0, 0), (pad, 0), (0, 0), (0, 0)))
    qi = jnp.arange(CHUNK)
    kj = jnp.arange(BAND)
    rel = (pad + qi[:, None]) - kj[None, :]
    bias = rel_bias[:, jnp.clip(rel, -REL_CLIP, REL_CLIP) + REL_CLIP].astype(jnp.float32)
    qc = q.reshape(B, nc, CHUNK, H, D).swapaxes(0, 1)

    def one_chunk(args):
        qch, ci = args
        kb = lax.dynamic_slice_in_dim(k_pad, ci * CHUNK, BAND, axis=1)
        vb = lax.dynamic_slice_in_dim(v_pad, ci * CHUNK, BAND, axis=1)
        s = jnp.einsum('bqhd,bkhd->bhqk', qch, kb,
                       preferred_element_type=jnp.float32) * scale + bias[None]
        valid = kj >= (LEFT_CHUNKS - ci) * CHUNK
        s = jnp.where(valid[None, None, None, :], s, NEG_INF)
        p = jax.nn.softmax(s, axis=-1).astype(vb.dtype)
        return jnp.einsum('bhqk,bkhd->bqhd', p, vb)

    o = lax.map(one_chunk, (qc, jnp.arange(nc)))
    return o.swapaxes(0, 1).reshape(B, S, H * D)

def causal_dwconv(u, w, b):
    S = u.shape[1]
    up = jnp.pad(u, ((0, 0), (CONV_WIDTH - 1, 0), (0, 0)))
    out = up[:, 0:S] * w[0]
    for j in range(1, CONV_WIDTH):
        out = out + up[:, j:j + S] * w[j]
    return out + b

def first_inputs(seed: int = 0) -> dict:
    key = jax.random.key(seed)
    ks = jax.random.split(key, 24)
    f32 = jnp.float32

    def nrm(k, shape, fan_in):
        return jax.random.normal(k, shape, f32) * (fan_in ** -0.5)

    def gain(k, shape):
        return 1.0 + 0.05 * jax.random.normal(k, shape, f32)

    L = DEPTH
    x = jax.random.normal(ks[0], (BATCH, SEQ, D_MODEL), f32)
    c = jax.random.normal(ks[1], (BATCH, D_MODEL), f32)
    offsets = jax.random.randint(ks[2], (BATCH, 1), 0, 4096, dtype=jnp.int32)
    positions = (offsets + jnp.arange(SEQ, dtype=jnp.int32)[None, :]).astype(jnp.int32)
    return {
        "x": x,
        "c": c,
        "positions": positions,
        "w_ada": nrm(ks[3], (L, D_MODEL, N_MOD * D_MODEL), D_MODEL),
        "b_ada": 0.02 * jax.random.normal(ks[4], (L, N_MOD * D_MODEL), f32),
        "g_attn_norm": gain(ks[5], (L, D_MODEL)),
        "w_in": nrm(ks[6], (L, D_MODEL, D_IN), D_MODEL),
        "g_q_latent": gain(ks[7], (L, MLA_Q_RANK)),
        "g_kv_latent": gain(ks[8], (L, MLA_KV_RANK)),
        "w_q_up": nrm(ks[9], (L, MLA_Q_RANK, MLA_HEADS * MLA_QK), MLA_Q_RANK),
        "w_kv_up": nrm(ks[10], (L, MLA_KV_RANK, MLA_HEADS * (MLA_NOPE + MLA_V)), MLA_KV_RANK),
        "g_mla_q": gain(ks[11], (L, MLA_QK)),
        "g_mla_k": gain(ks[12], (L, MLA_QK)),
        "g_ca_q": gain(ks[13], (L, CA_HEAD_DIM)),
        "g_ca_k": gain(ks[14], (L, CA_HEAD_DIM)),
        "rel_bias": 0.5 * jax.random.normal(ks[15], (L, CA_HEADS, 2 * REL_CLIP + 1), f32),
        "w_out": nrm(ks[16], (L, D_MIX, D_MODEL), D_MIX),
        "g_mlp_norm": gain(ks[17], (L, D_MODEL)),
        "w_up": nrm(ks[18], (L, D_MODEL, 2 * D_FF), D_MODEL),
        "conv_w": nrm(ks[19], (L, CONV_WIDTH, 2 * D_FF), CONV_WIDTH),
        "conv_b": 0.02 * jax.random.normal(ks[20], (L, 2 * D_FF), f32),
        "w_down": nrm(ks[21], (L, D_FF, D_MODEL), D_FF),
    }

def first_block(x, c, positions, w_ada, b_ada, g_attn_norm, w_in, g_q_latent, g_kv_latent,
              w_q_up, w_kv_up, g_mla_q, g_mla_k, g_ca_q, g_ca_k, rel_bias, w_out,
              g_mlp_norm, w_up, conv_w, conv_b, w_down):
    B, S, _ = x.shape
    split_pts = [MLA_Q_RANK, MLA_Q_RANK + MLA_KV_RANK, MLA_Q_RANK + MLA_KV_RANK + MLA_ROPE]
    for l in range(DEPTH):
        mod = jnp.dot(jax.nn.silu(c), w_ada[l]) + b_ada[l]
        sh_a, sc_a, g_a, sh_m, sc_m, g_m = jnp.split(mod, N_MOD, axis=-1)

        h = modulate(rmsnorm(x, g_attn_norm[l]), sh_a, sc_a)
        proj = jnp.dot(h, w_in[l])
        q_lat, kv_lat, k_rope, ca_qkv = jnp.split(proj, split_pts, axis=-1)

        q = jnp.dot(rmsnorm(q_lat, g_q_latent[l]), w_q_up[l]).reshape(B, S, MLA_HEADS, MLA_QK)
        kv = jnp.dot(rmsnorm(kv_lat, g_kv_latent[l]), w_kv_up[l]).reshape(B, S, MLA_HEADS, MLA_NOPE + MLA_V)
        k_nope, v = kv[..., :MLA_NOPE], kv[..., MLA_NOPE:]
        k = jnp.concatenate(
            [k_nope, jnp.broadcast_to(k_rope[:, :, None, :], (B, S, MLA_HEADS, MLA_ROPE))], axis=-1)
        q = rmsnorm(q, g_mla_q[l])
        k = rmsnorm(k, g_mla_k[l])
        q = jnp.concatenate([q[..., :MLA_NOPE], rope(q[..., MLA_NOPE:], positions)], axis=-1)
        k = jnp.concatenate([k[..., :MLA_NOPE], rope(k[..., MLA_NOPE:], positions)], axis=-1)
        o_mla = mla_attention(q, k, v)

        ca = ca_qkv.reshape(B, S, 3, CA_HEADS, CA_HEAD_DIM)
        cq = rmsnorm(ca[:, :, 0], g_ca_q[l])
        ck = rmsnorm(ca[:, :, 1], g_ca_k[l])
        cv = ca[:, :, 2]
        o_ca = chunk_attention(cq, ck, cv, rel_bias[l])

        mixed = jnp.dot(jnp.concatenate([o_mla, o_ca], axis=-1), w_out[l])
        x = x + g_a[:, None, :] * mixed

        h = modulate(rmsnorm(x, g_mlp_norm[l]), sh_m, sc_m)
        u = causal_dwconv(jnp.dot(h, w_up[l]), conv_w[l], conv_b[l])
        gate, val = jnp.split(u, 2, axis=-1)
        x = x + g_m[:, None, :] * jnp.dot(jax.nn.silu(gate) * val, w_down[l])
    return x


PLE_DIM = 256
HEAD_DIM = 64
D_MIX_2 = D_MODEL
SB_HEADS = D_MIX_2 // 2 // HEAD_DIM
RET_HEADS = D_MIX_2 // 2 // HEAD_DIM
SB_WIDTH = SB_HEADS * HEAD_DIM
RET_WIDTH = RET_HEADS * HEAD_DIM
D_IN_2 = 3 * SB_WIDTH + 4 * RET_WIDTH
RET_CHUNK = 128
ROPE_BASE = 10000.0
N_EXPERTS = 32
TOP_K = 4
D_EXPERT = D_MODEL
SWIGLU_LIMIT = 7.0
SWIGLU_ALPHA = 1.702
MOE_BLOCK = 128


def _rmsnorm(x, g):
    xf = x.astype(jnp.float32)
    y = xf * lax.rsqrt(jnp.mean(xf * xf, axis=-1, keepdims=True) + EPS)
    return (y * g.astype(jnp.float32)).astype(x.dtype)

def _heads(t, n_heads):
    b, s, _ = t.shape
    return t.reshape(b, s, n_heads, HEAD_DIM).transpose(0, 2, 1, 3)

def _rope(t, positions):
    half = HEAD_DIM // 2
    inv_freq = ROPE_BASE ** (-jnp.arange(half, dtype=jnp.float32) / half)
    ang = positions.astype(jnp.float32)[:, None, :, None] * inv_freq
    cos, sin = jnp.cos(ang), jnp.sin(ang)
    tf = t.astype(jnp.float32)
    t1, t2 = tf[..., :half], tf[..., half:]
    return jnp.concatenate([t1 * cos - t2 * sin, t2 * cos + t1 * sin], axis=-1).astype(t.dtype)

def _stick_breaking(q, k, v):
    b, h, s, d = q.shape
    nqb = s // Q_BLOCK
    scale = 1.0 / math.sqrt(d)
    qs = q.reshape(b, h, nqb, Q_BLOCK, d).transpose(2, 0, 1, 3, 4)
    t0s = jnp.arange(nqb, dtype=jnp.int32) * Q_BLOCK
    kpos = jnp.arange(s, dtype=jnp.int32)

    def block(args):
        qb, t0 = args
        z = jnp.einsum('bhqd,bhkd->bhqk', qb, k).astype(jnp.float32) * scale
        qpos = t0 + jnp.arange(Q_BLOCK, dtype=jnp.int32)
        mask = kpos[None, :] < qpos[:, None]
        lneg = jnp.where(mask, jax.nn.log_sigmoid(-z), 0.0)
        tail = lax.cumsum(lneg, axis=3, reverse=True) - lneg
        w = jnp.where(mask, jnp.exp(jax.nn.log_sigmoid(z) + tail), 0.0)
        return jnp.einsum('bhqk,bhkd->bhqd', w.astype(v.dtype), v)

    out = lax.map(block, (qs, t0s))
    return out.transpose(1, 2, 0, 3, 4).reshape(b, h, s, d)

def _retention(q, k, v):
    b, h, s, d = q.shape
    n = s // RET_CHUNK
    c = RET_CHUNK
    log_g = jnp.log(1.0 - 2.0 ** (-5.0 - jnp.arange(h, dtype=jnp.float32)))
    idx = jnp.arange(c, dtype=jnp.float32)
    diff = idx[:, None] - idx[None, :]
    dmat = jnp.where(diff >= 0, jnp.exp(log_g[:, None, None] * jnp.maximum(diff, 0.0)), 0.0)
    k_dec = jnp.exp(log_g[:, None] * (c - 1 - idx)[None, :])
    q_dec = jnp.exp(log_g[:, None] * (idx + 1.0)[None, :])
    g_chunk = jnp.exp(log_g * c)
    qc = q.reshape(b, h, n, c, d)
    kc = k.reshape(b, h, n, c, d)
    vc = v.reshape(b, h, n, c, d)
    dt = q.dtype
    scores = jnp.einsum('bhnid,bhnjd->bhnij', qc, kc) * dmat[None, :, None].astype(dt)
    inner = jnp.einsum('bhnij,bhnjd->bhnid', scores, vc)
    kv = jnp.einsum('bhnjd,bhnje->bhnde', kc * k_dec[None, :, None, :, None].astype(dt), vc)

    def step(state, kv_n):
        return g_chunk[:, None, None].astype(state.dtype) * state + kv_n, state

    init = jnp.zeros((b, h, d, d), dtype=kv.dtype)
    _, prev = lax.scan(step, init, jnp.moveaxis(kv, 2, 0))
    prev = jnp.moveaxis(prev, 0, 2)
    cross = jnp.einsum('bhnid,bhnde->bhnie', qc, prev) * q_dec[None, :, None, :, None].astype(dt)
    return (inner + cross).reshape(b, h, s, d)

def _group_norm(y, gain, bias):
    yf = y.astype(jnp.float32)
    mu = jnp.mean(yf, axis=-1, keepdims=True)
    var = jnp.mean((yf - mu) ** 2, axis=-1, keepdims=True)
    yn = (yf - mu) * lax.rsqrt(var + EPS)
    b, h, s, d = y.shape
    yn = yn.transpose(0, 2, 1, 3).reshape(b, s, h * d)
    return (yn * gain.astype(jnp.float32) + bias.astype(jnp.float32)).astype(y.dtype)

def _moe(xt, w_router, b_router, w_up_gate, b_up_gate, w_down, b_down):
    t, d = xt.shape
    logits = (xt @ w_router + b_router).astype(jnp.float32)
    top_vals, top_idx = lax.top_k(logits, TOP_K)
    gates = jax.nn.softmax(top_vals, axis=-1)
    a = t * TOP_K
    flat_e = top_idx.reshape(a).astype(jnp.int32)
    flat_tok = jnp.arange(a, dtype=jnp.int32) // TOP_K
    flat_gate = gates.reshape(a)
    order = jnp.argsort(flat_e)
    sorted_e = flat_e[order]
    counts = jnp.zeros((N_EXPERTS,), jnp.int32).at[flat_e].add(1)
    padded = ((counts + MOE_BLOCK - 1) // MOE_BLOCK) * MOE_BLOCK
    pad_end = jnp.cumsum(padded)
    pad_start = pad_end - padded
    start = jnp.cumsum(counts) - counts
    rank = jnp.arange(a, dtype=jnp.int32) - start[sorted_e]
    dest = pad_start[sorted_e] + rank
    n_slots = a + N_EXPERTS * MOE_BLOCK
    n_blocks = n_slots // MOE_BLOCK
    slot_tok = jnp.zeros((n_slots,), jnp.int32).at[dest].set(flat_tok[order])
    slot_gate = jnp.zeros((n_slots,), jnp.float32).at[dest].set(flat_gate[order])
    block_e = jnp.clip(jnp.searchsorted(pad_end, jnp.arange(n_blocks, dtype=jnp.int32) * MOE_BLOCK, side='right'), 0, N_EXPERTS - 1)
    xs = xt[slot_tok].reshape(n_blocks, MOE_BLOCK, d)

    def expert_block(args):
        xb, e = args
        hgu = xb @ w_up_gate[e] + b_up_gate[e]
        x_glu = jnp.minimum(hgu[:, :D_EXPERT], SWIGLU_LIMIT)
        x_lin = jnp.clip(hgu[:, D_EXPERT:], -SWIGLU_LIMIT, SWIGLU_LIMIT)
        hact = x_glu * jax.nn.sigmoid(SWIGLU_ALPHA * x_glu) * (x_lin + 1.0)
        return hact @ w_down[e] + b_down[e]

    ys = lax.map(expert_block, (xs, block_e)).reshape(n_slots, d)
    return jnp.zeros((t, d), xt.dtype).at[slot_tok].add(ys * slot_gate[:, None].astype(xt.dtype))

def second_inputs(seed: int = 0) -> dict:
    key = jax.random.key(seed)
    ks = jax.random.split(key, 24)
    nrm = lambda k, shape, s: jax.random.normal(k, shape, jnp.float32) * s
    L = DEPTH
    return {
        "x": nrm(ks[0], (BATCH, SEQ, D_MODEL), 1.0),
        "p": nrm(ks[1], (DEPTH, BATCH, SEQ, PLE_DIM), 1.0),
        "positions": jnp.broadcast_to(jnp.arange(SEQ, dtype=jnp.int32), (BATCH, SEQ)),
        "g_mix_norm": 1.0 + nrm(ks[2], (L, D_MODEL), 0.02),
        "w_in": nrm(ks[3], (L, D_MODEL, D_IN_2), D_MODEL ** -0.5),
        "sb_q_gain": 1.0 + nrm(ks[4], (L, HEAD_DIM), 0.02),
        "sb_k_gain": 1.0 + nrm(ks[5], (L, HEAD_DIM), 0.02),
        "ret_q_gain": 1.0 + nrm(ks[6], (L, HEAD_DIM), 0.02),
        "ret_k_gain": 1.0 + nrm(ks[7], (L, HEAD_DIM), 0.02),
        "ret_gn_gain": 1.0 + nrm(ks[8], (L, RET_WIDTH), 0.02),
        "ret_gn_bias": nrm(ks[9], (L, RET_WIDTH), 0.02),
        "w_out": nrm(ks[10], (L, D_MIX_2, D_MODEL), D_MIX_2 ** -0.5),
        "g_ffn_norm": 1.0 + nrm(ks[11], (L, D_MODEL), 0.02),
        "w_router": nrm(ks[12], (L, D_MODEL, N_EXPERTS), D_MODEL ** -0.5),
        "b_router": nrm(ks[13], (L, N_EXPERTS), 0.01),
        "w_up_gate": nrm(ks[14], (L, N_EXPERTS, D_MODEL, 2 * D_EXPERT), D_MODEL ** -0.5),
        "b_up_gate": nrm(ks[15], (L, N_EXPERTS, 2 * D_EXPERT), 0.02),
        "w_down": nrm(ks[16], (L, N_EXPERTS, D_EXPERT, D_MODEL), D_EXPERT ** -0.5),
        "b_down": nrm(ks[17], (L, N_EXPERTS, D_MODEL), 0.02),
        "g_ple_norm": 1.0 + nrm(ks[18], (L, D_MODEL), 0.02),
        "w_ple_gate": nrm(ks[19], (L, D_MODEL, D_MODEL), D_MODEL ** -0.5),
        "w_ple_proj": nrm(ks[20], (L, PLE_DIM, D_MODEL), PLE_DIM ** -0.5),
    }

def second_block(x, p, positions, g_mix_norm, w_in, sb_q_gain, sb_k_gain, ret_q_gain, ret_k_gain,
              ret_gn_gain, ret_gn_bias, w_out, g_ffn_norm, w_router, b_router, w_up_gate, b_up_gate,
              w_down, b_down, g_ple_norm, w_ple_gate, w_ple_proj):
    b, s, d = x.shape
    for i in range(DEPTH):
        xn = _rmsnorm(x, g_mix_norm[i])
        proj = xn @ w_in[i]
        o = 0
        sb_q = proj[..., o:o + SB_WIDTH]; o += SB_WIDTH
        sb_k = proj[..., o:o + SB_WIDTH]; o += SB_WIDTH
        sb_v = proj[..., o:o + SB_WIDTH]; o += SB_WIDTH
        r_q = proj[..., o:o + RET_WIDTH]; o += RET_WIDTH
        r_k = proj[..., o:o + RET_WIDTH]; o += RET_WIDTH
        r_v = proj[..., o:o + RET_WIDTH]; o += RET_WIDTH
        r_g = proj[..., o:o + RET_WIDTH]
        q_a = _rmsnorm(_heads(sb_q, SB_HEADS), sb_q_gain[i])
        k_a = _rmsnorm(_heads(sb_k, SB_HEADS), sb_k_gain[i])
        y_a = _stick_breaking(q_a, k_a, _heads(sb_v, SB_HEADS))
        y_a = y_a.transpose(0, 2, 1, 3).reshape(b, s, SB_WIDTH)
        q_b = _rope(_rmsnorm(_heads(r_q, RET_HEADS), ret_q_gain[i]), positions)
        k_b = _rope(_rmsnorm(_heads(r_k, RET_HEADS), ret_k_gain[i]), positions) * (HEAD_DIM ** -0.5)
        y_b = _retention(q_b, k_b, _heads(r_v, RET_HEADS))
        y_b = _group_norm(y_b, ret_gn_gain[i], ret_gn_bias[i]) * jax.nn.silu(r_g)
        x = x + jnp.concatenate([y_a, y_b], axis=-1) @ w_out[i]
        hn = _rmsnorm(x, g_ffn_norm[i]).reshape(b * s, d)
        x = x + _moe(hn, w_router[i], b_router[i], w_up_gate[i], b_up_gate[i], w_down[i], b_down[i]).reshape(b, s, d)
        gate = jax.nn.sigmoid(_rmsnorm(x, g_ple_norm[i]) @ w_ple_gate[i])
        x = x + (p[i] @ w_ple_proj[i]) * gate
    return x


def setup_inputs(seed=0):
    out = dict(first_inputs(seed))
    for name, value in second_inputs(seed + 1).items():
        if name != "x":
            out[name + "_2"] = value
    return out


def reference(
    x, c, positions, w_ada, b_ada, g_attn_norm, w_in, g_q_latent, g_kv_latent, w_q_up, w_kv_up,
    g_mla_q, g_mla_k, g_ca_q, g_ca_k, rel_bias, w_out, g_mlp_norm, w_up, conv_w, conv_b, w_down,
    p_2, positions_2, g_mix_norm_2, w_in_2, sb_q_gain_2, sb_k_gain_2, ret_q_gain_2,
    ret_k_gain_2, ret_gn_gain_2, ret_gn_bias_2, w_out_2, g_ffn_norm_2, w_router_2, b_router_2,
    w_up_gate_2, b_up_gate_2, w_down_2, b_down_2, g_ple_norm_2, w_ple_gate_2, w_ple_proj_2,
):
    x = first_block(
        x, c, positions, w_ada, b_ada, g_attn_norm, w_in, g_q_latent, g_kv_latent, w_q_up,
        w_kv_up, g_mla_q, g_mla_k, g_ca_q, g_ca_k, rel_bias, w_out, g_mlp_norm, w_up, conv_w,
        conv_b, w_down,
    )
    return second_block(
        x, p_2, positions_2, g_mix_norm_2, w_in_2, sb_q_gain_2, sb_k_gain_2, ret_q_gain_2,
        ret_k_gain_2, ret_gn_gain_2, ret_gn_bias_2, w_out_2, g_ffn_norm_2, w_router_2,
        b_router_2, w_up_gate_2, b_up_gate_2, w_down_2, b_down_2, g_ple_norm_2, w_ple_gate_2,
        w_ple_proj_2,
    )


_drawn_inputs = setup_inputs


def setup_inputs(seed=0):
    import zlib

    import numpy as np

    out = dict(_drawn_inputs(seed))
    spreads = {}
    factors = {'g_q_latent': 5.261,
     'g_mla_q': 4.086,
     'g_mla_k': 5.913,
     'g_ca_q': 3.649,
     'g_ca_k': 4.397,
     'sb_q_gain_2': 4.136,
     'sb_k_gain_2': 4.453,
     'ret_q_gain_2': 3.098,
     'ret_k_gain_2': 3.193,
     'ret_gn_gain_2': 3.277,
     'ret_gn_bias_2': 8.282,
     'b_up_gate_2': 7.199,
     'b_down_2': 8.0,
     'g_ple_norm_2': 200.0,
     'b_router_2': 3.619}
    for name, (base, spread) in spreads.items():
        noise = np.random.default_rng([zlib.crc32(name.encode()), seed]).standard_normal(out[name].shape)
        drawn = base * np.exp(spread * noise) if base else spread * noise
        out[name] = __import__('jax').numpy.asarray(drawn.astype(out[name].dtype))
    for name, factor in factors.items():
        out[name] = (out[name] * factor).astype(out[name].dtype)
    return out
```

```python
import numpy as np
import concourse.bass as bass
from concourse import mybir

FP = mybir.dt.float32
BF = mybir.dt.bfloat16
I32 = mybir.dt.int32
U32 = mybir.dt.uint32
ALU = mybir.AluOpType
ACT = mybir.ActivationFunctionType
AX = mybir.AxisListType.X

P = 128
S = 512
NT = S // P
D = 1024
KT = D // P
H = 8
HD = 64
QK = 96
NOPE, ROPE = 64, 32
QR, KVR = 256, 128
LAT = QR + KVR + ROPE
FF = 2816
FB = FF // P
EPS = 1e-6
NEG = -1e30
NE = 32
MAXSLOT = 50
TRASH = S
CW = 512
CHUNK = KT * CW
RING_D = 4
RING_E = 6

VC, VGA, VGM, VG2, VGF, VGP, VQL, VKL, VCQ, VCK, VSQ, VSK, VCB = 0, 8, 16, 24, 32, 40, 48, 50, 51, 52, 53, 54, 55
NV = VCB + 2 * FB
CWA = 2 * 2 * FB
VEC1, VEC2 = P, 256
VBA = VEC2 + 2 * FB


def constants():
    p = np.arange(P, dtype=np.float64)
    half1, half2 = ROPE // 2, HD // 2
    inv1 = 10000.0 ** (-np.arange(half1) / half1)
    inv2 = 10000.0 ** (-np.arange(half2) / half2)
    log_g = np.log(1.0 - 2.0 ** (-5.0 - np.arange(H)))
    diff = p[None, :] - p[:, None]
    dmat = np.where(diff[:, None] >= 0, np.exp(log_g[None, :, None] * np.maximum(diff, 0)[:, None]), 0.0)
    qdec = np.zeros((P, H // 2, P))
    gch = np.zeros((P, H // 2))
    for par in range(2):
        for pair in range(H // 2):
            qdec[par * HD:(par + 1) * HD, pair] = np.exp(log_g[2 * pair + par] * (p + 1.0))[None]
            gch[par * HD:(par + 1) * HD, pair] = np.exp(log_g[2 * pair + par] * P)
    kdec = np.exp(log_g[None, :] * (P - 1 - p)[:, None])
    parts = [
        ("a", [("ident", np.eye(P)), ("inv1", np.tile(inv1, (P, 1))), ("inv2", np.tile(inv2, (P, 1)))]),
        ("b", [("strict", (p[None, :] < p[:, None]) * 1.0), ("negm", np.where(p[None, :] < p[:, None], 0.0, NEG)),
               ("dmat", dmat.reshape(P, -1)), ("qdec", qdec.reshape(P, -1)), ("kdec", kdec), ("gch", gch)]),
        ("c", [("tri", (p[:, None] <= p[None, :]) * 1.0), ("iota", np.tile(np.arange(S), (P, 1))),
               ("slots", np.tile(np.arange(MAXSLOT), (P, 1))), ("tok", p[:, None] + P * np.arange(NT)[None, :]),
               ("trash", TRASH + p[:, None]), ("pmod", np.tile((p % 32)[:, None], (1, P)))]),
    ]
    where, cols, packs = {}, [], {}
    at = 0
    for pack, entries in parts:
        start = at
        for name, a in entries:
            where[name] = (at - start, a.shape[1])
            at += a.shape[1]
            cols.append(a)
        packs[pack] = (start, at - start)
    return where, packs, np.concatenate(cols, axis=1).astype(np.float32)


def program(nc, g, out):
    where, packs, _ = constants()

    BASE = 16512
    KB = 1024
    names = [0]

    def at(off, shape, dt=FP, name=None):
        names[0] += 1
        return nc.alloc_sbuf_tensor_at(f"{name or 't'}_{names[0]}", shape, dt, offset=BASE + int(off))

    ring = [at(s * 16 * KB, [P, CHUNK], name=f"ring{s}") for s in range(RING_D)]
    x = at(64 * KB, [P, NT, D], name="x")
    hT = at(80 * KB, [P, KT, S], name="hT")
    gate_a = at(96 * KB, [P, D], name="gate_a")
    gate_m = at(100 * KB, [P, D], name="gate_m")
    C = [104 * KB]

    def take_C(shape, dt=FP, name=None):
        t = at(C[0], shape, dt, name)
        C[0] += -(-int(np.prod(shape[1:])) * 4 // 32) * 32
        return t
    cona = take_C([P, packs["a"][1]], name="cona")
    vec = take_C([P, 352], name="vec")
    mod = take_C([P, 48], name="mod")
    stat = take_C([P, 96], name="stat")
    trig1 = take_C([P, NT, 2, ROPE // 2], name="trig1")
    trig2 = take_C([P, NT, 2, HD // 2], name="trig2")
    soft = take_C([P, 64], name="soft")
    hs = take_C([P, 416], name="hs")
    krope = take_C([P, NT, ROPE], name="krope")
    den = take_C([P, 8], name="den")
    cvec = take_C([P, 8], name="cvec")
    eps = take_C([P, 1], name="eps")
    one = take_C([P, 1], name="one")
    qs = take_C([P, 1], name="qs")
    assert C[0] <= 112 * KB, C[0]
    R = 112 * KB
    ident = cona[:, where["ident"][0]:where["ident"][0] + P]
    inv1 = cona[:, where["inv1"][0]:where["inv1"][0] + ROPE // 2]
    inv2 = cona[:, where["inv2"][0]:where["inv2"][0] + HD // 2]


    srep = at(R, [P, KT, P], name="srep")
    vrow = [at(R + 4 * KB, [NV, P], name="vrow0"), at(R + 5 * KB, [CWA, P], name="vrow1"),
            at(R + 6 * KB, [2 * FB + 48, P], name="vrow2")]
    modrow = [at(R + 8 * KB, [P, CW], name="modrow0"), at(R + 10 * KB, [P, CW], name="modrow1")]
    ang = [at(R + 16 * KB, [P, NT, 2, ROPE // 2], name="ang0"), at(R + 20 * KB, [P, NT, 2, HD // 2], name="ang1")]
    angk = at(R + 17 * KB, [P, NT, 2, HD // 2], name="angk")
    posi = at(R + 19 * KB, [P, 2, NT], I32, name="posi")
    posf = at(R + 19 * KB + 64, [P, 2, NT], name="posf")
    junk = at(R + 66 * KB, [P, D], name="junk")
    xn = [at(R + 70 * KB, [P, D], name="xn0"), at(R + 74 * KB, [P, D], name="xn1")]
    caq = at(R, [P, NT, CW], name="caq")
    cak = at(R + 8 * KB, [P, NT, CW], name="cak")
    caT = [at(R + 16 * KB, [P, NT, S], name="caqT"), at(R + 24 * KB, [P, NT, S], name="cakT")]
    cav = at(R + 32 * KB, [P, NT, CW], name="cav")
    bias = at(R + 40 * KB, [P, H, 2 * P], name="bias")
    biasr = at(R + 78 * KB, [P, H, 2 * P], name="biasr")
    lat = at(R + 48 * KB, [P, NT, LAT], name="lat")
    latT = at(R + 55 * KB, [P, 3, S], name="latT")
    kv = at(R + 62 * KB, [P, NT, H, 2 * HD], name="kv")
    tmp = at(R + 78 * KB, [P, NT * CW], name="tmp")
    mq = at(R, [P, NT, H, QK], name="mq")
    mk = at(R + 78 * KB, [P, NT, H, QK], name="mk")
    tmpm = at(R + 90 * KB, [P, H, QK], name="tmpm")
    mT = [at(R + 16 * KB, [QK, H, S], name="mqT"), at(R + 32 * KB, [QK, H, S], name="mkT")]
    PR1 = [at(R + (48 + 2 * i) * KB, [P, S], name=f"probs1_{i}") for i in range(3)]
    PT1 = [at(R + (54 + 2 * i) * KB, [P, NT, P], name=f"probsT1_{i}") for i in range(2)]
    o1 = [at(R + (58 + 2 * i) * KB, [P, H, HD], name=f"o1_{i}") for i in range(2)]
    farb = at(R + 94 * KB, [P, H], name="farb")
    grow1 = at(R + 94 * KB + 64, [P, 2, QK], name="grow1")
    grow2 = at(R + 94 * KB + 64 + 768, [P, 2, HD], name="grow2")
    modrow2 = [at(R + 12 * KB, [P, CW], name="modrow2"), at(R + 14 * KB, [P, CW], name="modrow3")]
    srep2 = at(R + 16 * KB, [P, KT, P], name="srep2")
    gbias = at(R, [P, 2, D], name="gbias")
    act = at(R, [P, FB, S], name="act")
    cgate = [at(R + (44 + 4 * i) * KB, [P, S], name=f"cgate{i}") for i in range(2)]
    cval = [at(R + (46 + 4 * i) * KB, [P, S], name=f"cval{i}") for i in range(2)]
    cgs = [at(R + (52 + 2 * i) * KB, [P, S], name=f"cgs{i}") for i in range(2)]
    conb = at(96 * KB, [P, packs["b"][1]], name="conb")
    def cb(n):
        return conb[:, where[n][0]:where[n][0] + where[n][1]]
    sbq = at(R, [P, NT, CW], name="sbq")
    sbk = at(R + 8 * KB, [P, NT, CW], name="sbk")
    sbT = [at(R + 16 * KB, [P, NT, S], name="sbqT"), at(R + 24 * KB, [P, NT, S], name="sbkT")]
    sbv = at(R + 32 * KB, [P, NT, CW], name="sbv")
    rq = at(R + 40 * KB, [P, NT, CW], name="rq")
    rk = at(R + 48 * KB, [P, NT, CW], name="rk")
    rv = at(R + 56 * KB, [P, NT, CW], name="rv")
    rg = at(R + 64 * KB, [P, NT, CW], name="rg")
    rT = [at(R, [P, NT, S], name="rqT"), at(R + 8 * KB, [P, NT, S], name="rkT")]
    rqdT = at(R + 72 * KB, [P, NT, S], name="rqdT")
    tmp2 = at(R + 72 * KB, [P, NT * CW], name="tmp2")
    tmpr = at(R + 80 * KB, [P, NT * CW], name="tmpr")
    PR2 = [at(R + (80 + 2 * i) * KB, [P, S], name=f"probs2_{i}") for i in range(3)]
    PT2 = [at(R + (86 + 2 * i) * KB, [P, NT, P], name=f"probsT2_{i}") for i in range(2)]
    o2 = [at(R + (90 + 2 * i) * KB, [P, H, HD], name=f"o2_{i}") for i in range(2)]
    sbw = [at((88 + 2 * i) * KB, [P, S], name=f"sbw{i}") for i in range(4)]
    rS = at(R + 80 * KB, [P, H, P], name="rS")
    state = at(R + 84 * KB, [P, H // 2, 2 * HD], name="state")
    gy = at(R + 86 * KB, [P, H, HD], name="gy")
    gsq = at(R + 88 * KB, [P, H, HD], name="gsq")
    gnrow = at(R + 16 * KB, [P, 2, CW], name="gnrow")
    wrt = at(R + 80 * KB, [P, KT, NE], name="wrt")
    ptok = at(R + 48 * KB, [P, NT, 256], name="ptok")
    pT = at(R + 52 * KB, [P, 2, S], name="pT")
    grow_f = at(R + 84 * KB, [P, D], name="grow_f")
    pp = at(R + 32 * KB, [P, NT, D], name="pp")
    bsum = at(R, [NE, 3 * D], name="bsum")
    brem = at(R + 12 * KB, [NE, 3 * D], name="brem")
    btmp = at(64 * KB, [NE, 3 * D], name="btmp")
    tmpx = at(R + 62 * KB, [P, CW], name="tmpx")
    zero = at(R + 62 * KB, [P, D], name="zero")
    ring += [at(R + (16 * i) * KB, [P, CHUNK], name=f"ring{4 + i}") for i in range(2)]
    rows = at(R + 48 * KB, [P, D], name="rows")
    xeT = at(R + 52 * KB, [P, KT, P], name="xeT")
    ea = at(R + 56 * KB, [P, D], name="ea")
    eaT = at(R + 60 * KB, [P, KT, P], name="eaT")
    ey = at(R + 64 * KB, [P, D], name="ey")
    eg = [at(R + (68 + 6 * i) * KB, [P, CW], name=f"eg{i}") for i in range(2)]
    es = [at(R + (70 + 6 * i) * KB, [P, CW], name=f"es{i}") for i in range(2)]
    el = [at(R + (72 + 6 * i) * KB, [P, CW], name=f"el{i}") for i in range(2)]
    pick = at(R + 80 * KB, [P, NT, P], name="pick")
    bias3 = at(R + 82 * KB, [3 * NE, 3 * D], BF, name="bias3")
    conc = at(R + 88 * KB, [P, packs["c"][1]], name="conc")
    def cc(n):
        return conc[:, where[n][0]:where[n][0] + where[n][1]]
    T = [96 * KB]

    def take_T(shape, dt=FP, name=None):
        t = at(T[0], shape, dt, name)
        T[0] += -(-int(np.prod(shape[1:])) * (2 if dt == BF else 4) // 32) * 32
        return t

    logits = take_T([P, NT, NE], name="logits")
    top8 = take_T([P, NT, 8], name="top8")
    topi = take_T([P, NT, 8], U32, name="topi")
    topf = take_T([P, NT, 8], name="topf")
    gate4 = take_T([P, NT, 4], name="gate4")
    chosen = take_T([P, NT, NE], name="chosen")
    route = take_T([P, NT, 2 + NE], name="route")
    rank = take_T([P, NT, NE], name="rank")
    eqk = take_T([P, NT, NE], name="eqk")
    nblk = take_T([P, 4, NE], name="nblk")
    ends = take_T([P, NE], name="ends")
    slot_f = take_T([P, 3, MAXSLOT], name="slot_f")
    slot_i = take_T([P, 3, MAXSLOT], I32, name="slot_i")
    cmp = at(R + 56 * KB, [P, MAXSLOT, NE], name="cmp")
    picked = take_T([P, 2 + NE], name="picked")
    gates = take_T([P, MAXSLOT], name="gates")
    idx_f = take_T([P, 4], name="idx_f")
    idx_all = take_T([P, MAXSLOT], I32, name="idx_all")
    idx_in = take_T([P, 1], I32, name="idx_in")
    idx_out = take_T([P, 1], I32, name="idx_out")
    hot = [take_T([3 * NE, P], BF, name=f"hot{i}") for i in range(2)]
    nb_i = take_T([P, 1], I32, name="nb_i")
    ones = take_T([P, P], name="ones")
    cntp = take_T([P, NE], name="cntp")
    brt = take_T([P, NE], name="brt")
    assert T[0] <= 104 * KB, T[0]

    bank = [nc.alloc_psum_tensor(f"bank{i}", [P, 512], FP) for i in range(8)]
    xo = [at(R + (48 + 4 * i) * KB, [P, D], name=f"xo{i}") for i in range(2)]
    fgate = [at(R + (56 + 4 * i) * KB, [P, D], name=f"fgate{i}") for i in range(2)]
    hn_d = nc.dram_tensor("hn_rows", [S + P, D], FP).ap()
    acc_d = nc.dram_tensor("moe_sum", [S + P, D], FP).ap()
    ext_d = nc.dram_tensor("rel_bias_ext", [H, 3 * P], FP).ap()

    def cols(w, c0, n, k0=0, kn=None):
        kn = kn or w.shape[0] // P
        return w[k0 * P:(k0 + kn) * P, c0:c0 + n].rearrange("(k p) n -> p k n", p=P)

    w = {n: g[n].rearrange("l a b -> (l a) b") for n in
         ("w_ada", "w_in", "w_q_up", "w_kv_up", "w_out", "w_up", "w_down", "w_in_2", "w_out_2", "w_router_2",
          "w_ple_gate_2", "w_ple_proj_2")}
    chunks = []

    def chunk(label, *parts):
        chunks.append((label, parts))

    for c in range(4):
        chunk(("ada", c), (0, KT, CW, cols(w["w_ada"], c * CW, CW)))
    for c, (c0, n) in enumerate([(0, LAT), (LAT, CW), (LAT + CW, CW), (LAT + 2 * CW, CW)]):
        chunk(("win", c), (0, KT, n, cols(w["w_in"], c0, n)))
    chunk(("mlaup",), (0, 2, H * QK, cols(w["w_q_up"], 0, H * QK)), (2 * H * QK, 1, H * 2 * HD, cols(w["w_kv_up"], 0, H * 2 * HD)))
    for c in range(4, 12):
        chunk(("ada", c), (0, KT, CW, cols(w["w_ada"], c * CW, CW)))
    for n in range(2):
        chunk(("wout", n), (0, KT, CW, cols(w["w_out"], n * CW, CW)))
    for c in range(FB // 2):
        chunk(("up", c), (0, KT, 2 * P, cols(w["w_up"], c * 2 * P, 2 * P)), (KT * 2 * P, KT, 2 * P, cols(w["w_up"], FF + c * 2 * P, 2 * P)))
    DK = [(0, 8), (8, 8), (16, 6)]
    for n in range(2):
        for j, (k0, kn) in enumerate(DK):
            chunk(("down", n, j), (0, kn, CW, cols(w["w_down"], n * CW, CW, k0, kn)))
    IN2 = [0, 1, 3, 4, 2, 5, 6]
    for c in range(7):
        chunk(("win2", c), (0, KT, CW, cols(w["w_in_2"], IN2[c] * CW, CW)))
    for n in range(2):
        chunk(("wout2", n), (0, KT, CW, cols(w["w_out_2"], n * CW, CW)))
    chunk(("ple",), (0, 2, D, cols(w["w_ple_proj_2"], 0, D)))
    number = {c[0]: i for i, c in enumerate(chunks)}
    ND = len(chunks)
    N_VROW = 9 + 8 + 3
    fills = [0] * RING_E
    arrives = {}
    for i, (label, parts) in enumerate(chunks):
        fills[i % RING_D] += len(parts)
        arrives[label] = (i % RING_D, 16 * fills[i % RING_D])

    def last_product(label):
        kind = label[0]
        if kind == "up":
            return (*label, 1, 1)
        if kind == "down":
            return ("down", label[1], NT - 1) if label[2] == 2 else 2 * label[1] + label[2] + 1
        return {"ada": label, "mlaup": ("kvup", NT - 1, 1), "ple": ("ple", NT - 1, 1)}.get(kind) or (*label, NT - 1)

    def part(slot, off, k, n):
        return ring[slot][:, off:off + k * n].rearrange("p (k n) -> p k n", k=k)

    order = []
    rot = [0]

    def product(label, b=None):
        if b is None:
            b = rot[0] % 8
            rot[0] += 1
        order.append((label, b))

    OT_LAG = 6

    def attention_order(kind):
        for s in range(4 * H + OT_LAG + 1):
            if s < 4 * H:
                product(("S", kind, s), s % 3)
            if 0 <= s - 2 < 4 * H:
                product(("T", kind, s - 2), 3 + s % 2)
            if 0 <= s - 3 < 4 * H and (s - 3) % H == 0:
                product(("O", kind, (s - 3) // H), 5 + (s - 3) // H % 2)
            if s >= H + OT_LAG and (s - OT_LAG) % H == 0:
                product(("oT", kind, (s - OT_LAG) // H - 1), 7)

    def norm_order(nz):
        for t in range(NT):
            for j in range(2):
                product(("xT", nz, t, j))

    product(("vecs",))
    for c in range(4):
        product(("ada", c))
        if c:
            product(("adaT", c - 1))
    product(("adaT", 3))
    norm_order(0)
    for c in range(3):
        for t in range(NT):
            product(("win", c, t))
    for t in range(NT):
        product(("latT", t))
    for t in range(NT):
        product(("win", 3, t))
    for qk in range(2):
        for t in range(NT):
            product(("caT", qk, t))
    for t in range(NT):
        for n in range(2):
            product(("qup", t, n))
    for t in range(NT):
        for n in range(2):
            product(("kvup", t, n))
    attention_order(0)
    ADAT = (6, 7, 8, 9)
    for c in range(4, 12):
        product(("ada", c))
        if c - 1 in ADAT:
            product(("adaT", c - 1))
    for qk in range(2):
        for h in range(H):
            product(("mT", qk, h))
    attention_order(1)
    for n in range(2):
        for t in range(NT):
            product(("wout", n, t))
    norm_order(1)
    for c in range(FB // 2):
        for b in range(2):
            for gv in range(2):
                product(("up", c, b, gv))
    for n in range(2):
        for t in range(NT):
            product(("down", n, t))
    norm_order(2)
    for c in range(7):
        for t in range(NT):
            product(("win2", c, t))
        if c == 3:
            for qk in range(2):
                for t in range(NT):
                    product(("sbT", qk, t))
    for qk in range(2):
        for t in range(NT):
            product(("rT", qk, t))
    attention_order(2)
    for n in range(NT):
        product(("rS", n, 0), 0); product(("rS", n, 1), 1)
        product(("rO", n), 2 + n % 2)
        if n < NT - 1:
            product(("rkv", n), 4)
        if n:
            product(("oT", 3, n - 1), 7)
    product(("oT", 3, NT - 1), 7)
    for n in range(2):
        for t in range(NT):
            product(("wout2", n, t))
    norm_order(3)
    product(("router",))
    product(("pT", 0)); product(("pT", 1)); product(("pT", 2)); product(("pT", 3))
    product(("rank",))
    for t in range(NT):
        for n in range(2):
            product(("ple", t, n))
    uses = [0] * 8
    told = [0] * 8
    bank_of = {}
    for label, b in order:
        assert label not in bank_of, label
        uses[b] += 1
        told[b] += label[0] != "O"
        bank_of[label] = (b, uses[b], told[b])
    FU, TK = list(told), list(uses)
    late, late_uses = [], [0] * 8
    for t in range(NT):
        for j in range(2):
            late.append((("xT", 4, t, j), (2 * t + j) % 8))
    for t in range(NT):
        for n in range(2):
            late.append((("gate", t, n), (2 * t + n) % 8))
    for label, b in late:
        late_uses[b] += 1
        bank_of[label] = (b, late_uses[b], late_uses[b])
    late = {label for label, _ in late}

    sem = nc.alloc_semaphore
    ring_in = [sem(f"ring_in{i}") for i in range(RING_E)]
    w_used = sem("w_used")
    bank_full = [sem(f"bank_full{i}") for i in range(8)]
    bank_taken = [sem(f"bank_taken{i}") for i in range(8)]
    s_lin, s_empty, s_row, s_gate = sem("linear_part"), sem("empty_places"), sem("row_numbers"), sem("gates_and_rows")
    late_full = [sem(f"late_full{i}") for i in range(8)]
    late_taken = [sem(f"late_taken{i}") for i in range(8)]
    s_mset, s_bias, s_taps, s_qs, s_top, s_ge, s_ix = (sem(n) for n in (
        "constants_set", "bias_windows", "conv_taps", "stick_q_gain", "top_values", "gate_exp", "scatter_index"))
    s_con, s_vrow, s_x, s_pos, s_rows1, s_ext, s_biasr, s_far = (sem(n) for n in (
        "consts_in", "vectors_in", "x_in", "positions_in", "gain_rows_in", "bias_ext_in", "bias_windows_in", "far_bias_in"))
    s_ext2, s_gb, s_conb, s_gn, s_grf, s_wrt, s_ptok, s_conc, s_bsum = (sem(n) for n in (
        "bias_ext_out", "gate_bias_in", "consts_b_in", "group_norm_rows_in", "ffn_gain_row_in", "router_in", "p_in",
        "consts_c_in", "expert_bias_in"))
    s_ang, s_trig, s_silu, s_srep = sem("angles"), sem("trig"), sem("silu_c"), sem("silu_c_rep")
    s_mod, s_sq, s_xn, s_hTv = sem("modulation"), sem("x_rms"), sem("x_normed"), sem("hT_vector")
    s_ms, s_rt, s_nrm = sem("head_mean_square"), sem("head_rms"), sem("head_normed")
    s_max, s_P, s_pv = sem("row_max"), sem("probs"), sem("pv_done")
    s_ln, s_arg, s_o = sem("log1p"), sem("log_weight"), sem("attention_out")
    s_conv, s_cg, s_act, s_xr = sem("conv_done"), sem("gate_silu"), sem("mlp_act"), sem("x_updated")
    s_rqd, s_kd, s_rS, s_st, s_sg = sem("rqd"), sem("k_decayed"), sem("ret_scores"), sem("ret_state"), sem("ret_gate")
    s_zero, s_zd, s_acc = sem("zeros"), sem("zeros_out"), sem("moe_sum_init")
    s_hn = [sem(f"hn_rows_out{i}") for i in range(2)]
    s_route, s_slots, s_b3 = sem("routes"), sem("slot_table"), sem("expert_bias_split")
    s_pick, s_idx, s_got, s_ea, s_hotu, s_hotd = (sem(n) for n in (
        "pick_built", "gather_index", "rows_gathered", "expert_act", "hot_up", "hot_down"))
    s_sig, s_scat, s_back = sem("glu_sigmoid"), sem("scattered"), sem("sum_back")
    s_out = sem("final_rows")
    s_held = sem("held")
    s_stored = [sem(f"out_stored{i}") for i in range(2)]
    chain_v, chain_a, chain_g = sem("vector_chain"), sem("scalar_chain"), sem("gpsimd_chain")

    def norm_cols(nz, k):
        if nz < 2:
            s0, s1 = ((0, 8), (24, 32))[nz]
            return mod[:, s1 + k:s1 + k + 1], mod[:, s0 + k:s0 + k + 1]
        v = {2: VG2, 4: VGP}[nz]
        return vec[:, v + k:v + k + 1], None

    SM_CA, SM_MLA = HD ** -0.5, QK ** -0.5
    UP_ORDER = (0, 2, 1, 3)

    class Chain:
        def __init__(self, eng, s):
            self.eng, self.s, self.n = eng, s, 0

        def __call__(self, ins):
            self.n += 1
            ins.then_inc(self.s, 1)
            self.eng.wait_ge(self.s, self.n)

    def full(eng, label):
        b, n, m = bank_of[label]
        eng.wait_ge((late_full if label in late else bank_full)[b], m)
        return bank[b]

    def taken(eng, label):
        b, n, m = bank_of[label]
        eng.wait_ge((late_taken if label in late else bank_taken)[b], n)

    def take(ins, label):
        ins.then_inc((late_taken if label in late else bank_taken)[bank_of[label][0]], 1)

    def win_dst(c, t):
        return lat[:, t, :] if c == 0 else (caq, cak, cav)[c - 1][:, t, :]

    def win2_dst(c, t):
        return (sbq, sbk, rq, rk, sbv, rv, rg)[c][:, t, :]

    def blk3(ap, n=4):
        return ap.rearrange("p (a b) -> p a b", a=n)

    def bc(ap, axis, shape):
        return ap.unsqueeze(axis).broadcast_to(shape)

    def row_bcast(ap1d, n, parts=P):
        return bass.AP(tensor=ap1d.tensor, offset=ap1d.offset, ap=[[0, parts], [1, n]])

    def slot_reg(eng, row, s, hi):
        return eng.value_load(slot_i[0:1, row, slot_at(s)],
                              min_val=0, max_val=hi)

    def slot_at(i):
        return slice(i, i + 1) if isinstance(i, int) else bass.ds(i, 1)

    def n_slots(eng):
        return eng.value_load(nb_i[0:1, 0:1], min_val=NE, max_val=47)

    with nc.Block() as block:
        @block.sync
        def _(sp):
            v = g
            sp.dma_start(cona[:, :], v["consts"][:, packs["a"][0]:packs["a"][0] + packs["a"][1]]).then_inc(s_con, 16)
            packed = [("c", VC), ("g_attn_norm", VGA), ("g_mlp_norm", VGM), ("g_mix_norm_2", VG2), ("g_ffn_norm_2", VGF),
                      ("g_ple_norm_2", VGP), ("g_q_latent", VQL), ("g_kv_latent", VKL), ("conv_b", VCB)]
            for name, r0 in packed:
                n = v[name].shape[1] // P
                sp.dma_start(vrow[0][r0:r0 + n, :], v[name].rearrange("a (r p) -> (a r) p", p=P)).then_inc(s_vrow, 16)
            for name, r0 in (("g_ca_q", VCQ), ("g_ca_k", VCK), ("sb_q_gain_2", VSQ), ("sb_k_gain_2", VSK)):
                for half in range(2):
                    sp.dma_start(vrow[0][r0:r0 + 1, half * HD:(half + 1) * HD], v[name]).then_inc(s_vrow, 16)
            sp.dma_start(vrow[1][:, :], v["conv_w"][0, 0:2, :].rearrange("j (r p) -> (j r) p", p=P)).then_inc(s_vrow, 16)
            sp.dma_start(vrow[2][0:2 * FB, :], v["conv_w"][0, 2:3, :].rearrange("j (r p) -> (j r) p", p=P)).then_inc(s_vrow, 16)
            sp.dma_start(vrow[2][2 * FB:, :], v["b_ada"].rearrange("a (r p) -> (a r) p", p=P)).then_inc(s_vrow, 16)

            def used(i):
                last = last_product(chunks[i][0])
                if isinstance(last, int):
                    sp.wait_ge(w_used, last)
                else:
                    full(sp, last)

            def load(i):
                label, parts = chunks[i]
                if i >= RING_D:
                    used(i - RING_D)
                slot = i % RING_D
                for off, k, n, src in parts:
                    sp.dma_start(part(slot, off, k, n), src).then_inc(ring_in[slot], 16)

            for i in range(RING_D):
                load(i)
            for t in range(NT):
                sp.dma_start(x[:, t, :], v["x"][0, t * P:(t + 1) * P, :]).then_inc(s_x, 16)
            for i in range(RING_D, number[("wout", 0)]):
                load(i)
            full(sp, ("mT", 1, H - 1))
            for n, c in enumerate((2, 5)):
                src = v["b_ada"][0, c * D:(c + 1) * D]
                sp.dma_start(gbias[:, n, :], row_bcast(src, D)).then_inc(s_gb, 16)
            for i in range(number[("wout", 0)], number[("win2", 0)]):
                load(i)
            sp.wait_ge(s_xr, 3 * NT)
            sp.dma_start(conb[:, :], v["consts"][:, packs["b"][0]:packs["b"][0] + packs["b"][1]]).then_inc(s_conb, 16)
            for i in range(number[("win2", 0)], number[("wout2", 0)]):
                load(i)
            full(sp, ("S", 2, 4 * H - 1))
            sp.dma_start(gnrow[:, 0, :], row_bcast(v["ret_gn_gain_2"][0, :], CW)).then_inc(s_gn, 16)
            sp.dma_start(gnrow[:, 1, :], row_bcast(v["ret_gn_bias_2"][0, :], CW)).then_inc(s_gn, 16)
            for i in range(number[("wout2", 0)], ND):
                load(i)
            full(sp, ("oT", 3, NT - 1))
            sp.dma_start(grow_f[:, :], row_bcast(v["g_ffn_norm_2"][0, :], D)).then_inc(s_grf, 16)
            sp.dma_start(wrt[:, :, :], w["w_router_2"].rearrange("(k p) n -> p k n", p=P)).then_inc(s_wrt, 16)
            sp.dma_start(brt[:, :], row_bcast(v["b_router_2"][0, :], NE)).then_inc(s_wrt, 16)
            sp.dma_start(ptok[:, :, :], v["p_2"][0, 0].rearrange("(t p) n -> p t n", p=P)).then_inc(s_ptok, 16)
            sp.dma_start(conc[:, :], v["consts"][:, packs["c"][0]:packs["c"][0] + packs["c"][1]]).then_inc(s_conc, 16)
            sp.dma_start(bsum[:, 0:2 * D], v["b_up_gate_2"][0]).then_inc(s_bsum, 16)
            sp.dma_start(bsum[:, 2 * D:], v["b_down_2"][0]).then_inc(s_bsum, 16)

            def expert(q, e, down, c):
                slot = q % RING_E
                if down:
                    src = v["w_down_2"][0, bass.ds(e, 1), :, c * CW:(c + 1) * CW]
                else:
                    src = v["w_up_gate_2"][0, bass.ds(e, 1), :, c * CW:(c + 1) * CW]
                sp.dma_start(part(slot, 0, KT, CW), src.rearrange("e (k p) n -> p (e k) n", p=P)).then_inc(ring_in[slot], 16)

            for q, c in enumerate(UP_ORDER):
                used(max(i for i in range(ND) if i % RING_D == q))
                expert(q, 0, False, c)
            sp.wait_ge(s_slots, 1)
            sp.wait_ge(s_b3, 1)
            nb = n_slots(sp)

            def round_(i, e, d, first=False):
                for j in range(RING_E):
                    if first and j >= 2:
                        sp.wait_ge(bank_full[UP_ORDER[j - 2]], FU[UP_ORDER[j - 2]] + 1)
                    elif not first and j < 4:
                        sp.wait_ge(bank_full[UP_ORDER[j]], FU[UP_ORDER[j]] + i)
                    elif not first:
                        sp.wait_ge(bank_full[j], FU[j] - 1 + i)
                    if j < 4:
                        expert(4 + j, e, False, UP_ORDER[j])
                    else:
                        expert(4 + j, d, True, j - 4)

            round_(1, slot_reg(sp, 0, 1, NE - 1), 0, first=True)
            with sp.Fori(2, nb) as i:
                round_(i, slot_reg(sp, 0, i, NE - 1), slot_reg(sp, 0, i - 1, NE - 1))
            d = slot_reg(sp, 0, nb - 1, NE - 1)
            for j in range(2):
                sp.wait_ge(bank_full[UP_ORDER[j]], FU[UP_ORDER[j]] + nb)
                expert(4 + j, d, True, j)
            for j in range(2):
                sp.wait_ge(bank_full[UP_ORDER[2 + j]], FU[UP_ORDER[2 + j]] + nb)
                sp.dma_start(part(j, 0, KT, CW), cols(w["w_ple_gate_2"], j * CW, CW)).then_inc(ring_in[j], 16)
            for t in range(NT):
                sp.wait_ge(s_out, t + 1)
                sp.dma_start(out[0, t * P:(t + 1) * P, :], xo[t % 2][:, :]).then_inc(s_stored[t % 2], 16)
            for parity in range(2):
                sp.wait_ge(s_stored[parity], 16 * NT // 2)

        @block.gpsimd
        def _(pool):
            link = Chain(pool, chain_g)
            v = g
            pool.dma_start(posi[:, 0, :].unsqueeze(2), v["positions"].rearrange("a (t p) -> p t a", p=P), allow_slow_non_contiguous=True).then_inc(s_pos, 16)
            pool.dma_start(posi[:, 1, :].unsqueeze(2), v["positions_2"].rearrange("a (t p) -> p t a", p=P), allow_slow_non_contiguous=True).then_inc(s_pos, 16)
            rb = v["rel_bias"]
            nrel = rb.shape[2]
            pool.dma_start(ext_d[:, 0:nrel], rb[0]).then_inc(s_ext, 16)
            last = bass.AP(tensor=rb.tensor, offset=rb.offset + nrel - 1, ap=[[nrel, H], [0, 3 * P - nrel], [1, 1]])
            pool.dma_start(ext_d[:, nrel:].unsqueeze(2), last, allow_slow_non_contiguous=True).then_inc(s_ext, 16)
            pool.wait_ge(s_ext, 32)
            window = bass.AP(tensor=ext_d.tensor, offset=ext_d.offset + 1, ap=[[1, P], [3 * P, H], [1, 2 * P]])
            pool.dma_start(biasr[:, :, :], window).then_inc(s_biasr, 16)
            far = bass.AP(tensor=rb.tensor, offset=rb.offset + nrel - 1, ap=[[0, P], [nrel, H], [1, 1]])
            pool.dma_start(farb[:, :].unsqueeze(2), far, allow_slow_non_contiguous=True).then_inc(s_far, 16)
            for j, name in enumerate(("g_mla_q", "g_mla_k")):
                pool.dma_start(grow1[:, j, :], row_bcast(v[name][0, :], QK)).then_inc(s_rows1, 16)
            for j, name in enumerate(("ret_q_gain_2", "ret_k_gain_2")):
                pool.dma_start(grow2[:, j, :], row_bcast(v[name][0, :], HD)).then_inc(s_rows1, 16)
            pool.wait_ge(s_zero, 1)
            pool.dma_start(hn_d[S:, :], zero[:, :]).then_inc(s_zd, 16)
            pool.dma_start(acc_d[S:, :], zero[:, :]).then_inc(s_scat, 16)
            for t in range(NT):
                pool.wait_ge(s_xr, 3 * NT + t + 1)
                pool.dma_start(acc_d[t * P:(t + 1) * P, :], x[:, t, :]).then_inc(s_acc, 16)
            for t in range(NT):
                pool.wait_ge(s_xn, 3 * NT + t + 1)
                pool.dma_start(hn_d[t * P:(t + 1) * P, :], xn[t % 2][:, :]).then_inc(s_hn[t % 2], 16)
            pool.wait_ge(s_zd, 16)
            pool.wait_ge(s_scat, 16)
            for parity in range(2):
                pool.wait_ge(s_hn[parity], 16 * NT // 2)
            pool.wait_ge(s_acc, 16 * NT)

            def gather():
                pool.indirect_dma_start(out=rows[:, :], out_offset=None, in_=hn_d[:, :],
                                        in_offset=bass.IndirectOffsetOnAxis(ap=idx_in[:, 0:1], axis=0)).then_inc(s_got, 16)

            def scatter():
                pool.indirect_dma_start(out=acc_d[:, :], out_offset=bass.IndirectOffsetOnAxis(ap=idx_out[:, 0:1], axis=0),
                                        in_=ey[:, :], in_offset=None, compute_op=ALU.add).then_inc(s_scat, 16)

            def output_stands(i):
                pool.wait_ge(bank_taken[4], TK[4] + 1 + i)
                pool.wait_ge(bank_taken[5], TK[5] + 1 + i)
                pool.wait_ge(s_ix, i + 1)
                pool.nop().then_inc(s_held, 1)

            for i in range(2):
                pool.wait_ge(s_idx, i + 1)
                gather()
            pool.wait_ge(s_slots, 1)
            nb = n_slots(pool)
            with pool.Fori(1, nb) as i:
                pool.wait_ge(s_idx, i + 2)
                pool.nop().then_inc(s_held, 1)
                gather()
                output_stands(i - 1)
                scatter()
            output_stands(nb - 1)
            scatter()
            pool.wait_ge(s_scat, nb * 16 + 16)
            pool.nop().then_inc(s_held, 1)
            for t in range(NT):
                pool.dma_start(x[:, t, :], acc_d[t * P:(t + 1) * P, :]).then_inc(s_back, 16)
            pool.wait_ge(s_back, 16 * NT)

        @block.scalar
        def _(act_e):
            link = Chain(act_e, chain_a)
            fn = nc.scalar.activation

            def copy_out(dst, label, src=None, scale=None):
                b = full(act_e, label)
                src = b[:, 0:dst.shape[-1]] if src is None else src(b)
                if scale is None:
                    take(fn(dst, src, ACT.Copy), label)
                else:
                    take(fn(dst, src, ACT.Copy, scale=scale), label)

            def norm(nz):
                for t in range(NT):
                    if nz == 0:
                        act_e.wait_ge(s_x, 16 * NT)
                    elif nz == 4:
                        act_e.wait_ge(s_back, 16 * NT)
                    else:
                        act_e.wait_ge(s_xr, nz * NT + t + 1)
                    k = nz * NT + t
                    link(fn(junk[:, :], x[:, t, :], ACT.Square, accum_out=stat[:, k:k + 1]))
                    fn(stat[:, 20 + k:21 + k], stat[:, k:k + 1], ACT.Sqrt, scale=1.0 / D, bias=eps[:, 0:1]).then_inc(s_sq, 1)
                for t in range(NT):
                    label = ("xT", nz, t, 0)
                    b = full(act_e, label)
                    if nz == 3:
                        take(fn(hT[:, 0:4, t * P:(t + 1) * P], blk3(b[:, :]), ACT.Copy), label)
                        continue
                    for k in range(4):
                        a, sh = norm_cols(nz, k)
                        o, i = hT[:, k, t * P:(t + 1) * P], b[:, k * P:(k + 1) * P]
                        ins = fn(o, i, ACT.Identity, scale=a, bias=sh) if sh is not None else fn(o, i, ACT.Copy, scale=a)
                    take(ins, label)

            def roots(r):
                act_e.wait_ge(s_ms, r + 1)
                fn(hs[:, r * 32:r * 32 + 32], hs[:, r * 32:r * 32 + 32], ACT.Sqrt).then_inc(s_rt, 1)

            def attention(kind, PR, PT):
                base = {0: 0, 1: 1, 2: 0}[kind] * 4 * H
                for s in range(4 * H + OT_LAG + 1):
                    if s < 4 * H:
                        t, h = divmod(s, H)
                        n = (t + 1) * P
                        if kind == 2:
                            W1 = sbw[s % 2]
                            b = full(act_e, ("S", 2, s))
                            if s >= 2:
                                taken(act_e, ("S", 2, s - 2))
                            link(fn(W1[:, 0:n], b[:, 0:n], ACT.Abs))
                            link(fn(W1[:, 0:n], W1[:, 0:n], ACT.Exp, scale=-1.0))
                            fn(W1[:, 0:n], W1[:, 0:n], ACT.Ln, bias=one[:, 0:1]).then_inc(s_ln, 1)
                        else:
                            i = kind * 4 * H + s
                            if t >= 2 and h == 0:
                                act_e.wait_ge(s_o, kind * NT + t - 1)
                            act_e.wait_ge(s_max, i + 1)
                            c = soft[:, s % 8:s % 8 + 1]
                            total = soft[:, 16 + 8 * (t % 2) + h:17 + 8 * (t % 2) + h]
                            Pb = PR[s % 3]
                            if kind == 0:
                                fn(Pb[:, 0:n], Pb[:, 0:n], ACT.Exp, bias=c, accum_out=total).then_inc(s_P, 1)
                            else:
                                if s >= 3:
                                    full(act_e, ("T", 1, s - 3))
                                b = full(act_e, ("S", 1, s))
                                take(fn(Pb[:, 0:n], b[:, 0:n], ACT.Exp, bias=c, scale=SM_MLA, accum_out=total), ("S", 1, s))
                    if kind == 2 and 0 <= s - 1 < 4 * H:
                        i = s - 1
                        n = (i // H + 1) * P
                        act_e.wait_ge(s_arg, i + 1)
                        if i >= 3:
                            full(act_e, ("T", 2, i - 3))
                        fn(PR[i % 3][:, 0:n], sbw[2 + i % 2][:, 0:n], ACT.Exp).then_inc(s_P, 1)
                    i = s - 2
                    if kind < 2 and 0 <= i < 4 * H:
                        n = (i // H + 1) * P
                        b = full(act_e, ("T", kind, i))
                        if i >= 2:
                            act_e.wait_ge(s_pv, kind * 4 * H + i - 1)
                        take(fn(PT[i % 2][:, 0:i // H + 1, :], b[:, 0:n].rearrange("p (a b) -> p a b", b=P), ACT.Copy), ("T", kind, i))
                    if s >= H + OT_LAG and (s - OT_LAG) % H == 0:
                        t = (s - OT_LAG) // H - 1
                        out_T(kind, t)

            def out_T(kind, t):
                label = ("oT", kind, t)
                k0 = {0: 4, 1: 0, 2: 0, 3: 4}[kind]
                b = full(act_e, label)
                take(fn(hT[:, k0:k0 + 4, t * P:(t + 1) * P], blk3(b[:, :]), ACT.Copy), label)

            act_e.wait_ge(s_mset, 2)
            b = full(act_e, ("vecs",))
            link(fn(vec[:, 0:NV], b[:, 0:NV], ACT.Copy))
            link(fn(vec[:, VEC1:VEC1 + CWA], b[:, VEC1:VEC1 + CWA], ACT.Copy))
            take(fn(vec[:, VEC2:VEC2 + 2 * FB + 48], b[:, VEC2:VEC2 + 2 * FB + 48], ACT.Copy), ("vecs",))
            taken(act_e, ("vecs",))
            fn(cvec[:, :], vec[:, VC:VC + 8], ACT.Silu).then_inc(s_silu, 1)
            for j, (a, dst) in enumerate(zip(ang, (trig1, trig2))):
                act_e.wait_ge(s_ang, j + 1)
                fn(dst[:, :, :, :], a[:, :, :, :], ACT.Sin).then_inc(s_trig, 1)
            norm(0)
            for c in range(3):
                for t in range(NT):
                    copy_out(win_dst(c, t), ("win", c, t))
                if c == 0:
                    roots(0)
            for t in range(NT):
                label = ("latT", t)
                b = full(act_e, label)
                for j in range(3):
                    ins = fn(latT[:, j, t * P:(t + 1) * P], b[:, j * P:(j + 1) * P], ACT.Copy, scale=vec[:, VQL + j:VQL + j + 1])
                take(ins, label)
            for t in range(NT):
                copy_out(win_dst(3, t), ("win", 3, t))
                if t < 2:
                    roots(1 + t)
            for qk in range(2):
                for t in range(NT):
                    copy_out(caT[qk][:, :, t * P:(t + 1) * P], ("caT", qk, t), lambda b: blk3(b[:, :]), vec[:, VCQ + qk:VCQ + qk + 1])
            for t in range(NT):
                for n in range(2):
                    copy_out(mq[:, t, 4 * n:4 * n + 4, :], ("qup", t, n), lambda b: blk3(b[:, 0:4 * QK]))
            act_e.wait_ge(s_bias, 1)
            for t in range(NT):
                for n in range(2):
                    copy_out(kv[:, t, 4 * n:4 * n + 4, :], ("kvup", t, n), lambda b: blk3(b[:, :]))
            attention(0, PR1, PT1)
            for c in range(4, 12):
                dst = {4: gate_a, 5: gate_a, 10: gate_m, 11: gate_m}.get(c)
                if dst is not None:
                    copy_out(dst[:, c % 2 * CW:(c % 2 + 1) * CW], ("ada", c))
                else:
                    if c == 8 or c == 9:
                        full(act_e, ("adaT", c - 2))
                    copy_out(modrow2[c % 2][:, :], ("ada", c))
                if c in (5, 7):
                    roots(3 + (c - 5) // 2)
                if c - 1 in ADAT:
                    copy_out(mod[:, 4 * (c - 1):4 * c], ("adaT", c - 1), lambda b: blk3(b[:, :])[:, :, 0])
            for h in range(H):
                copy_out(mT[0][:, h, :], ("mT", 0, h), lambda b: b[0:QK, :])
            attention(1, PR1, PT1)
            norm(1)
            for i in range(FB + 1):
                c, b2 = divmod(i, 2)
                if i < FB:
                    for gv, dst in ((0, cgate), (1, cval)):
                        label = ("up", c, b2, gv)
                        b = full(act_e, label)
                        j = gv * FB + i
                        if gv == 0 and i >= 2:
                            act_e.wait_ge(s_act, i - 1)
                        fn(dst[i % 2][:, :], b[:, :], ACT.Identity, scale=vec[:, VEC2 + j:VEC2 + j + 1],
                           bias=vec[:, VCB + j:VCB + j + 1]).then_inc(s_conv, 1)
                if i >= 1:
                    k = i - 1
                    act_e.wait_ge(s_taps, k + 1)
                    fn(cgs[k % 2][:, :], cgate[k % 2][:, :], ACT.Silu).then_inc(s_cg, 1)
            norm(2)
            for c in range(7):
                for t in range(NT):
                    copy_out(win2_dst(c, t), ("win2", c, t))
                if c in (1, 2):
                    roots(4 + c)
                if c == 3:
                    act_e.wait_ge(s_qs, 1)
                    for qk in range(2):
                        for t in range(NT):
                            copy_out(sbT[qk][:, :, t * P:(t + 1) * P], ("sbT", qk, t), lambda b: blk3(b[:, :]),
                                     qs[:, 0:1] if qk == 0 else vec[:, VSK:VSK + 1])
                if c in (4, 5):
                    roots(3 + c)
            for qk in range(2):
                for t in range(NT):
                    copy_out(rT[qk][:, :, t * P:(t + 1) * P], ("rT", qk, t), lambda b: blk3(b[:, :]))
            fn(rg[:, :, :], rg[:, :, :], ACT.Silu).then_inc(s_sg, 1)
            attention(2, PR2, PT2)
            for n in range(NT):
                roots(9 + n)
                if n:
                    out_T(3, n - 1)
            out_T(3, NT - 1)
            norm(3)
            for t in range(NT):
                label = ("pT", t)
                b = full(act_e, label)
                take(fn(pT[:, :, t * P:(t + 1) * P], blk3(b[:, 0:2 * P], 2), ACT.Copy), label)
            act_e.wait_ge(s_top, 1)
            fn(gate4[:, :, :], gate4[:, :, :], ACT.Exp).then_inc(s_ge, 1)
            for t in range(NT):
                for n in range(2):
                    copy_out(pp[:, t, n * CW:(n + 1) * CW], ("ple", t, n))
            def tiles_T(dst, k6, k7):
                for j, (b, k) in enumerate(((6, k6), (7, k7))):
                    act_e.wait_ge(bank_full[b], k)
                    fn(dst[:, 4 * j:4 * j + 4, :], blk3(bank[b][:, :]), ACT.Copy).then_inc(bank_taken[b], 1)

            def sigmoids(i):
                for j in range(2):
                    act_e.wait_ge(bank_taken[j], TK[j] + 1 + i)
                    fn(es[j][:, :], eg[j][:, :], ACT.Sigmoid, scale=1.702).then_inc(s_sig, 1)

            def outputs(i, scattered):
                act_e.wait_ge(s_scat, scattered)
                act_e.wait_ge(s_gate, 2 * i + 2)
                for n in range(2):
                    act_e.wait_ge(bank_full[4 + n], FU[4 + n] + 1 + i)
                    act_e.nop().then_inc(s_held, 1)
                    fn(ey[:, n * CW:(n + 1) * CW], bank[4 + n][:, :], ACT.Copy,
                       scale=gates[:, bass.ds(i, 1)]).then_inc(bank_taken[4 + n], 1)

            tiles_T(xeT, FU[6] + 1, FU[7] + 2)
            sigmoids(0)
            tiles_T(xeT, FU[6] + 2, FU[7] + 4)
            act_e.wait_ge(s_slots, 1)
            nb = n_slots(act_e)
            with act_e.Fori(1, nb) as i:
                tiles_T(eaT, 2 * i + (FU[6] + 1), 3 * i + (FU[7] + 3))
                sigmoids(i)
                tiles_T(xeT, 2 * i + (FU[6] + 2), 3 * i + (FU[7] + 4))
                outputs(i - 1, 16 * i)
            tiles_T(eaT, 2 * nb + (FU[6] + 1), 3 * nb + (FU[7] + 2))
            outputs(nb - 1, 16 * nb)
            norm(4)
            for t in range(NT):
                for n in range(2):
                    label = ("gate", t, n)
                    b = full(act_e, label)
                    if t >= 2 and n == 0:
                        act_e.wait_ge(s_out, t - 1)
                    take(fn(fgate[t % 2][:, n * CW:(n + 1) * CW], b[:, :], ACT.Sigmoid), label)


        @block.tensor
        def _(pe):
            mm = nc.tensor.matmul

            def acquire(label):
                b, n, m = bank_of[label]
                if n > 1:
                    pe.wait_ge((late_taken if label in late else bank_taken)[b], n - 1)
                return bank[b]

            def publish(ins, label):
                ins.then_inc((late_full if label in late else bank_full)[bank_of[label][0]], 1)

            def arrived(label):
                slot, value = arrives[label]
                pe.wait_ge(ring_in[slot], value)
                return slot

            def tr(dst, src):
                return nc.tensor.transpose(dst, src, ident)

            def norm(nz):
                for t in range(NT):
                    pe.wait_ge(s_xn, nz * NT + t + 1)
                    for j in range(2):
                        b = acquire(("xT", nz, t, j))
                        for k in range(4):
                            ins = tr(b[:, k * P:(k + 1) * P], xn[t % 2][:, (4 * j + k) * P:(4 * j + k + 1) * P])
                        publish(ins, ("xT", nz, t, j))

            def hT_stands(nz, t):
                taken(pe, ("xT", nz, t, 0))
                taken(pe, ("xT", nz, t, 1))

            def project(chunk_label, label, n, nz=None):
                slot = arrived(chunk_label)
                wv = part(slot, 0, KT, n)
                for t in range(NT):
                    if nz is not None:
                        hT_stands(nz, t)
                    b = acquire(label(t))
                    for k in range(KT):
                        ins = mm(b[:, 0:n], hT[:, k, t * P:(t + 1) * P], wv[:, k, :], start=k == 0, stop=k == KT - 1)
                    publish(ins, label(t))

            def ada(c):
                slot = arrived(("ada", c))
                wv = part(slot, 0, KT, CW)
                b = acquire(("ada", c))
                for k in range(KT):
                    ins = mm(b[:, :], srep[:, k, :] if c < 4 else srep2[:, k, :], wv[:, k, :], start=k == 0, stop=k == KT - 1)
                publish(ins, ("ada", c))

            def ada_T(c, rows_):
                taken(pe, ("ada", c))
                b = acquire(("adaT", c))
                for j in range(4):
                    ins = tr(b[:, j * P:(j + 1) * P], rows_[c % 2][:, j * P:(j + 1) * P])
                publish(ins, ("adaT", c))

            def pairs_T(name, qk, src):
                for t in range(NT):
                    b = acquire((name, qk, t))
                    for j in range(4):
                        ins = tr(b[:, j * P:(j + 1) * P], src[:, t, j * P:(j + 1) * P])
                    publish(ins, (name, qk, t))

            def out_T(kind, t, o):
                pe.wait_ge(s_o, kind * NT + t + 1)
                b = acquire(("oT", kind, t))
                for j in range(4):
                    ins = tr(b[:, j * P:(j + 1) * P], o[t % 2][:, 2 * j:2 * j + 2, :].rearrange("p a b -> p (a b)"))
                publish(ins, ("oT", kind, t))

            def attention(kind, q_of, k_of, v_of, PR, PT, o):
                for s in range(4 * H + OT_LAG + 1):
                    if s < 4 * H:
                        t, h = divmod(s, H)
                        n = (t + 1) * P
                        b = acquire(("S", kind, s))
                        publish(mm(b[:, 0:n], q_of(h, t), k_of(h, n), start=True, stop=True), ("S", kind, s))
                    i = s - 2
                    if 0 <= i < 4 * H:
                        t = i // H
                        if kind == 1:
                            taken(pe, ("S", 1, i))
                        else:
                            pe.wait_ge(s_P, (0 if kind == 0 else 4 * H) + i + 1)
                        b = acquire(("T", kind, i))
                        for j in range(t + 1):
                            ins = tr(b[:, j * P:(j + 1) * P], PR[i % 3][:, j * P:(j + 1) * P])
                        publish(ins, ("T", kind, i))
                    i = s - 3
                    if 0 <= i < 4 * H:
                        t, h = divmod(i, H)
                        taken(pe, ("T", kind, i))
                        b = acquire(("O", kind, t)) if h == 0 else bank[bank_of[("O", kind, t)][0]]
                        for j in range(t + 1):
                            ins = mm(b[:, h * HD:(h + 1) * HD], PT[i % 2][:, j, :], v_of(h, j), start=j == 0, stop=j == t)
                        ins.then_inc(s_pv, 1)
                    if s >= H + OT_LAG and (s - OT_LAG) % H == 0:
                        out_T(kind, (s - OT_LAG) // H - 1, o)

            pe.wait_ge(s_con, 16)
            pe.wait_ge(s_vrow, 16 * N_VROW)
            b = acquire(("vecs",))
            nc.tensor.transpose(b[:, 0:NV], vrow[0][:, :], cona[0:NV, 0:NV])
            nc.tensor.transpose(b[:, VEC1:VEC1 + CWA], vrow[1][:, :], cona[0:CWA, 0:CWA])
            n = 2 * FB + 48
            publish(nc.tensor.transpose(b[:, VEC2:VEC2 + n], vrow[2][:, :], cona[0:n, 0:n]), ("vecs",))
            pe.wait_ge(s_srep, 1)
            for c in range(4):
                ada(c)
                if c:
                    ada_T(c - 1, modrow)
            ada_T(3, modrow)
            norm(0)
            for c in range(3):
                project(("win", c), lambda t: ("win", c, t), LAT if c == 0 else CW, 0 if c == 0 else None)
            pe.wait_ge(s_nrm, 1)
            for t in range(NT):
                b = acquire(("latT", t))
                for j in range(3):
                    ins = tr(b[:, j * P:(j + 1) * P], lat[:, t, j * P:(j + 1) * P])
                publish(ins, ("latT", t))
            project(("win", 3), lambda t: ("win", 3, t), CW)
            for qk, src in enumerate((caq, cak)):
                pe.wait_ge(s_nrm, 2 + qk)
                pairs_T("caT", qk, src)
            slot = arrived(("mlaup",))
            wq = part(slot, 0, 2, H * QK)
            wkv = ring[slot][:, 2 * H * QK:2 * H * QK + H * 2 * HD]
            for t in range(NT):
                taken(pe, ("latT", t))
                for n in range(2):
                    b = acquire(("qup", t, n))
                    for k in range(2):
                        ins = mm(b[:, 0:4 * QK], latT[:, k, t * P:(t + 1) * P], wq[:, k, n * 4 * QK:(n + 1) * 4 * QK], start=k == 0, stop=k == 1)
                    publish(ins, ("qup", t, n))
            for t in range(NT):
                for n in range(2):
                    b = acquire(("kvup", t, n))
                    publish(mm(b[:, :], latT[:, 2, t * P:(t + 1) * P], wkv[:, n * CW:(n + 1) * CW], start=True, stop=True), ("kvup", t, n))
            for qk in range(2):
                for t in range(NT):
                    taken(pe, ("caT", qk, t))

            def half(a, h, c0, n):
                return a[h % 2 * HD:(h % 2 + 1) * HD, h // 2, c0:c0 + n]

            attention(0, lambda h, t: half(caT[0], h, t * P, P), lambda h, n: half(caT[1], h, 0, n),
                      lambda h, j: cav[:, j, h * HD:(h + 1) * HD], PR1, PT1, o1)
            pe.wait_ge(s_srep, 2)
            for c in range(4, 12):
                ada(c)
                if c - 1 in ADAT:
                    ada_T(c - 1, modrow2)
            for qk, src in enumerate((mq, mk)):
                pe.wait_ge(s_nrm, 4 + qk)
                for h in range(H):
                    b = acquire(("mT", qk, h))
                    for t in range(NT):
                        ins = tr(b[0:QK, t * P:(t + 1) * P], src[:, t, h, :])
                    publish(ins, ("mT", qk, h))
            for qk in range(2):
                for h in range(H):
                    taken(pe, ("mT", qk, h))
            attention(1, lambda h, t: mT[0][:, h, t * P:(t + 1) * P], lambda h, n: mT[1][:, h, 0:n],
                      lambda h, j: kv[:, j, h, HD:], PR1, PT1, o1)
            for kind in (0, 1):
                for t in range(NT):
                    taken(pe, ("oT", kind, t))
            for n in range(2):
                project(("wout", n), lambda t: ("wout", n, t), CW)
            norm(1)
            for t in range(NT):
                hT_stands(1, t)
            for c in range(FB // 2):
                slot = arrived(("up", c))
                wv = ring[slot][:, :].rearrange("p (g k n) -> p g k n", g=2, k=KT)
                for b2 in range(2):
                    for gv in range(2):
                        b = acquire(("up", c, b2, gv))
                        for k in range(KT):
                            ins = mm(b[:, :], wv[:, gv, k, b2 * P:(b2 + 1) * P], hT[:, k, :], start=k == 0, stop=k == KT - 1)
                        publish(ins, ("up", c, b2, gv))
            pe.wait_ge(s_act, FB)
            for n in range(2):
                for j, (k0, kn) in enumerate(DK):
                    slot = arrived(("down", n, j))
                    wv = part(slot, 0, kn, CW)
                    for t in range(NT):
                        b = acquire(("down", n, t)) if j == 0 else bank[bank_of[("down", n, t)][0]]
                        for k in range(kn):
                            ins = mm(b[:, :], act[:, k0 + k, t * P:(t + 1) * P], wv[:, k, :], start=k0 + k == 0, stop=k0 + k == FB - 1)
                        if j == 2:
                            publish(ins, ("down", n, t))
                    if j < 2:
                        ins.then_inc(w_used, 1)
            norm(2)
            for c in range(7):
                project(("win2", c), lambda t: ("win2", c, t), CW, 2 if c == 0 else None)
                if c == 3:
                    for qk, src in enumerate((sbq, sbk)):
                        pe.wait_ge(s_nrm, 6 + qk)
                        pairs_T("sbT", qk, src)
            for qk, src in enumerate((rq, rk)):
                pe.wait_ge(s_nrm, 8 + qk)
                pairs_T("rT", qk, src)
            for qk in range(2):
                for t in range(NT):
                    taken(pe, ("sbT", qk, t))
            attention(2, lambda h, t: half(sbT[0], h, t * P, P), lambda h, n: half(sbT[1], h, 0, n),
                      lambda h, j: sbv[:, j, h * HD:(h + 1) * HD], PR2, PT2, o2)
            pe.wait_ge(s_kd, 1)
            pe.wait_ge(s_rqd, NT)
            for n in range(NT):
                c0 = n * P
                for j in range(2):
                    b = acquire(("rS", n, j))
                    for h in range(j, H, 2):
                        ins = mm(b[:, h // 2 * P:(h // 2 + 1) * P], half(rT[1], h, c0, P), half(rT[0], h, c0, P), start=True, stop=True)
                    publish(ins, ("rS", n, j))
                b = acquire(("rO", n))
                for j in range(2):
                    taken(pe, ("rS", n, j))
                if n:
                    pe.wait_ge(s_st, n)
                for pair in range(H // 2):
                    if n:
                        mm(b[:, pair * P:(pair + 1) * P], rqdT[:, pair, c0:c0 + P], state[:, pair, :], start=True, stop=False,
                           skip_group_check=True)
                    for h in (2 * pair, 2 * pair + 1):
                        ins = mm(b[:, h * HD:(h + 1) * HD], rS[:, h, :], rv[:, n, h * HD:(h + 1) * HD], start=n == 0, stop=True,
                                 skip_group_check=True)
                publish(ins, ("rO", n))
                if n < NT - 1:
                    b = acquire(("rkv", n))
                    for j in range(4):
                        ins = mm(b[:, j * P:(j + 1) * P], rk[:, n, j * P:(j + 1) * P], rv[:, n, j * P:(j + 1) * P], start=True, stop=True)
                    publish(ins, ("rkv", n))
                if n:
                    out_T(3, n - 1, o2)
            out_T(3, NT - 1, o2)
            for kind in (2, 3):
                for t in range(NT):
                    taken(pe, ("oT", kind, t))
            for n in range(2):
                project(("wout2", n), lambda t: ("wout2", n, t), CW)
            norm(3)
            pe.wait_ge(s_wrt, 32)
            b = acquire(("router",))
            for t in range(NT):
                hT_stands(3, t)
                for k in range(KT):
                    ins = mm(b[:, t * NE:(t + 1) * NE], hT[:, k, t * P:(t + 1) * P], wrt[:, k, :], start=k == 0, stop=k == KT - 1)
            publish(ins, ("router",))
            pe.wait_ge(s_ptok, 16)
            for t in range(NT):
                b = acquire(("pT", t))
                for j in range(2):
                    ins = tr(b[:, j * P:(j + 1) * P], ptok[:, t, j * P:(j + 1) * P])
                publish(ins, ("pT", t))
            pe.wait_ge(s_conc, 16)
            pe.wait_ge(s_route, 1)
            b = acquire(("rank",))
            for t in range(NT + 1):
                for j in range(min(t + 1, NT)):
                    ins = mm(b[:, t * NE:(t + 1) * NE], cc("tri") if j == t else ones[:, :], chosen[:, j, :], start=j == 0, stop=j == min(t, NT - 1))
            publish(ins, ("rank",))
            slot = arrived(("ple",))
            wv = part(slot, 0, 2, D)
            for t in range(NT):
                taken(pe, ("pT", t))
                for n in range(2):
                    b = acquire(("ple", t, n))
                    for k in range(2):
                        ins = mm(b[:, :], pT[:, k, t * P:(t + 1) * P], wv[:, k, n * CW:(n + 1) * CW], start=k == 0, stop=k == 1)
                    publish(ins, ("ple", t, n))

            def find(i, k7):
                pe.wait_ge(bank_taken[7], k7)
                pe.wait_ge(s_pick, i + 1)
                for t in range(NT):
                    ins = mm(bank[7][:, 0:2 + NE], pick[:, t, :], route[:, t, :], start=t == 0, stop=t == NT - 1)
                ins.then_inc(bank_full[7], 1)

            def turn(src, k6, k7):
                for b, k, j in ((6, k6, 0), (7, k7, 1)):
                    pe.wait_ge(bank_taken[b], k)
                    for m in range(4):
                        ins = tr(bank[b][:, m * P:(m + 1) * P], src[:, (4 * j + m) * P:(4 * j + m + 1) * P])
                    ins.then_inc(bank_full[b], 1)

            def weights(q, rounds):
                slot = q % RING_E
                pe.wait_ge(ring_in[slot], 16 * (fills[slot] + q // RING_E + 1) + 16 * rounds)
                return part(slot, 0, KT, CW)

            def fill(b, lhs, hot_, bcol, wv):
                mm(bank[b][:, :], hot_[:, :], bias3[:, bcol:bcol + CW], start=True, stop=False)
                for k in range(KT):
                    ins = mm(bank[b][:, :], lhs[:, k, :], wv[:, k, :], start=False, stop=k == KT - 1)
                ins.then_inc(bank_full[b], 1)

            def up(i, q0, rounds):
                pe.wait_ge(bank_taken[7], xe_taken(i)[1])
                pe.wait_ge(bank_taken[6], xe_taken(i)[0])
                pe.wait_ge(s_hotu, i + 1)
                for j, c in enumerate(UP_ORDER):
                    pe.wait_ge(bank_taken[c], TK[c] + i)
                    fill(c, xeT, hot[0], c * CW, weights(q0 + j, rounds))

            def down(i, q0, rounds, k6, k7):
                pe.wait_ge(bank_taken[6], k6)
                pe.wait_ge(bank_taken[7], k7)
                pe.wait_ge(s_hotd, i + 1)
                for n in range(2):
                    pe.wait_ge(bank_taken[4 + n], TK[4 + n] + i)
                    fill(4 + n, eaT, hot[1], 2 * D + n * CW, weights(q0 + n, rounds))

            def xe_taken(i):
                return 2 * i + (TK[6] + (1 if isinstance(i, int) and i == 0 else 0)), 3 * i + (TK[7] + (2 if isinstance(i, int) and i == 0 else 1))

            find(0, TK[7])
            pe.wait_ge(s_got, 16)
            turn(rows, TK[6], TK[7] + 1)
            find(1, TK[7] + 2)
            up(0, 0, 0)
            pe.wait_ge(s_got, 32)
            turn(rows, TK[6] + 1, TK[7] + 3)
            pe.wait_ge(s_slots, 1)
            nb = n_slots(pe)
            with pe.Fori(1, nb) as i:
                find(i + 1, 3 * i + (TK[7] + 1))
                pe.wait_ge(s_ea, 2 * i)
                turn(ea, 2 * i + TK[6], 3 * i + (TK[7] + 2))
                up(i, 4, i - 1)
                pe.wait_ge(s_got, 16 * i + 32)
                turn(rows, 2 * i + (TK[6] + 1), 3 * i + (TK[7] + 3))
                down(i - 1, 8, i - 1, 2 * i + (TK[6] + 1), 3 * i + (TK[7] + 3))
            pe.wait_ge(s_ea, 2 * nb)
            turn(ea, 2 * nb + TK[6], 3 * nb + (TK[7] + 1))
            down(nb - 1, 4, nb - 1, 2 * nb + (TK[6] + 1), 3 * nb + (TK[7] + 2))
            norm(4)
            for j in range(2):
                pe.wait_ge(ring_in[j], 16 * (fills[j] + 1) + 16 * nb)
            for t in range(NT):
                hT_stands(4, t)
                for n in range(2):
                    wv = part(n, 0, KT, CW)
                    b = acquire(("gate", t, n))
                    for k in range(KT):
                        ins = mm(b[:, :], hT[:, k, t * P:(t + 1) * P], wv[:, k, :], start=k == 0, stop=k == KT - 1)
                    publish(ins, ("gate", t, n))

        @block.vector
        def _(dve):
            link = Chain(dve, chain_v)
            ve = nc.vector
            tt, ts, stt = ve.tensor_tensor, ve.tensor_scalar, ve.scalar_tensor_tensor

            def norm(nz):
                def back(t):
                    label = ("xT", nz, t, 1)
                    b = full(dve, label)
                    if nz == 3:
                        take(ve.tensor_copy(hT[:, 4:8, t * P:(t + 1) * P], blk3(b[:, :])), label)
                        return
                    for k in range(4):
                        a, sh = norm_cols(nz, 4 + k)
                        ins = ts(hT[:, 4 + k, t * P:(t + 1) * P], b[:, k * P:(k + 1) * P], a, sh, ALU.mult,
                                 ALU.add if sh is not None else ALU.bypass)
                    take(ins, label)

                for t in range(NT):
                    k = nz * NT + t
                    dve.wait_ge(s_sq, k + 1)
                    link(ve.reciprocal(stat[:, 40 + k:41 + k], stat[:, 20 + k:21 + k]))
                    if t >= 2:
                        full(dve, ("xT", nz, t - 2, 1))
                        if nz == 3:
                            dve.wait_ge(s_hn[t % 2], 16 * (t // 2))
                    if nz == 3:
                        link(ts(xn[t % 2][:, :], x[:, t, :], stat[:, 40 + k:41 + k], None, ALU.mult))
                        tt(xn[t % 2][:, :], xn[t % 2][:, :], grow_f[:, :], ALU.mult).then_inc(s_xn, 1)
                    else:
                        ts(xn[t % 2][:, :], x[:, t, :], stat[:, 40 + k:41 + k], None, ALU.mult).then_inc(s_xn, 1)
                    if t:
                        back(t - 1)
                back(NT - 1)

            def mean_square(src, n, d, dst, scratch):
                link(tt(scratch, src, src, ALU.mult))
                link(ve.reduce_sum(dst, scratch, axis=AX))
                return ts(dst, dst, 1.0 / d, EPS, ALU.mult, ALU.add)

            def heads(r, src, scratch, after=None, scale=None):
                st = hs[:, r * 32:r * 32 + 32]
                a = src[:, :, :].rearrange("p t (h d) -> p (t h) d", d=HD)
                mean_square(a, 32, HD, st, scratch[:, :].rearrange("p (n d) -> p n d", d=HD)).then_inc(s_ms, 1)
                dve.wait_ge(s_rt, r + 1)
                link(ve.reciprocal(st, st))
                if scale is not None:
                    link(ts(st, st, scale, None, ALU.mult))
                return tt(a, a, bc(st, 2, [P, 32, HD]), ALU.mult)

            def rope(x1, x2, trig, j, scratch, shape):
                cos = bc(trig[:, j, 0, :], 1, shape)
                sin = bc(trig[:, j, 1, :], 1, shape)
                n = shape[1] * shape[2]
                a, b, c = (scratch[:, i * n:(i + 1) * n].rearrange("p (h d) -> p h d", h=shape[1]) for i in range(3))
                link(tt(a, x2, sin, ALU.mult))
                link(tt(b, x2, cos, ALU.mult))
                link(tt(c, x1, sin, ALU.mult))
                link(tt(x1, x1, cos, ALU.mult))
                link(tt(x1, x1, a, ALU.subtract))
                return tt(x2, b, c, ALU.add)

            def attention(kind, PR, PT, o):
                for s in range(4 * H + OT_LAG + 1):
                    if s < 4 * H:
                        t, h = divmod(s, H)
                        n = (t + 1) * P
                        c = soft[:, s % 8:s % 8 + 1]
                        if kind == 0:
                            L = PR[s % 3]
                            if s >= 3:
                                full(dve, ("T", 0, s - 3))
                            b = full(dve, ("S", 0, s))
                            lo = max(t - 1, 0) * P
                            if lo:
                                ts(L[:, 0:lo], b[:, 0:lo], SM_CA, farb[:, h:h + 1], ALU.mult, ALU.add)
                            take(stt(L[:, lo:n], b[:, lo:n], SM_CA, bias[:, h, (0 if t else P):2 * P], ALU.mult, ALU.add), ("S", 0, s))
                            taken(dve, ("S", 0, s))
                            ve.tensor_reduce(c, L[:, 0:n], AX, ALU.max, negate=True).then_inc(s_max, 1)
                        elif kind == 1:
                            b = full(dve, ("S", 1, s))
                            link(ve.memset(b[0:HD, n - HD:n], NEG))
                            link(ve.tensor_reduce(c, b[:, 0:n], AX, ALU.max, negate=True))
                            ts(c, c, SM_MLA, None, ALU.mult).then_inc(s_max, 1)
                        else:
                            W1, W2 = sbw[s % 2], sbw[2 + s % 2]
                            d0 = t * P
                            dve.wait_ge(s_ln, s + 1)
                            if s >= 2:
                                dve.wait_ge(s_P, 4 * H + s - 1)
                            b = full(dve, ("S", 2, s))
                            link(stt(W2[:, 0:n], b[:, 0:n], 0.0, W1[:, 0:n], ALU.max, ALU.add))
                            link(tt(W2[:, d0:n], W2[:, d0:n], cb("strict"), ALU.mult))
                            link(ve.tensor_tensor_scan(W1[:, 0:n][:, ::-1], one[:, 0:1].broadcast_to([P, n]), W2[:, 0:n][:, ::-1], 0.0, ALU.mult, ALU.add))
                            take(tt(W2[:, 0:n], b[:, 0:n], W1[:, 0:n], ALU.subtract), ("S", 2, s))
                            taken(dve, ("S", 2, s))
                            tt(W2[:, d0:n], W2[:, d0:n], cb("negm"), ALU.add).then_inc(s_arg, 1)
                    i = s - 2
                    if kind == 2 and 0 <= i < 4 * H:
                        b = full(dve, ("T", 2, i))
                        if i >= 2:
                            dve.wait_ge(s_pv, 8 * H + i - 1)
                        take(ve.tensor_copy(PT[i % 2][:, 0:i // H + 1, :], b[:, 0:(i // H + 1) * P].rearrange("p (a b) -> p a b", b=P)), ("T", 2, i))
                    i = s - 3
                    if 0 <= i < 4 * H and i % H == H - 1:
                        t = i // H
                        label = ("O", kind, t)
                        b = bank[bank_of[label][0]]
                        dve.wait_ge(s_pv, kind * 4 * H + i + 1)
                        if t >= 2:
                            full(dve, ("oT", kind, t - 2))
                        src = b[:, :].rearrange("p (h d) -> p h d", h=H)
                        if kind == 2:
                            take(ve.tensor_copy(o[t % 2][:, :, :], src), label)
                        else:
                            link(ve.reciprocal(den[:, :], soft[:, 16 + 8 * (t % 2):24 + 8 * (t % 2)]))
                            take(tt(o[t % 2][:, :, :], src, bc(den[:, :], 2, [P, H, HD]), ALU.mult), label)
                        taken(dve, label)
                        dve.nop().then_inc(s_o, 1)

            ve.memset(eps[:, :], EPS).then_inc(s_mset, 1)
            ve.memset(one[:, :], 1.0).then_inc(s_mset, 1)
            dve.wait_ge(s_con, 16)
            dve.wait_ge(s_pos, 32)
            link(ve.tensor_copy(posf[:, :, :], posi[:, :, :]))
            two_pi = 2 * np.pi
            c1 = 6.28125
            c2 = np.floor((two_pi - c1) * 2 ** 22) / 2 ** 22
            c3 = two_pi - c1 - c2
            for j, (a, inv, hw) in enumerate(((ang[0], inv1, ROPE // 2), (ang[1], inv2, HD // 2))):
                kk = angk[:, :, :, 0:hw]
                for m in range(2):
                    link(tt(a[:, :, m, :], bc(posf[:, j, :], 2, [P, NT, hw]), bc(inv, 1, [P, NT, hw]), ALU.mult))
                for m, turn in ((0, 0.25), (1, 0.0)):
                    link(ts(kk[:, :, m, :], a[:, :, m, :], 1.0 / two_pi, turn, ALU.mult, ALU.add))
                link(ts(kk, kk, 12582912.0, None, ALU.add))
                link(ts(kk, kk, -12582912.0, None, ALU.add))
                for m in range(2):
                    for cc_ in (c1, c2, c3):
                        link(stt(a[:, :, m, :], kk[:, :, m, :], -float(cc_), a[:, :, m, :], ALU.mult, ALU.add))
                link(ts(a[:, :, 0, :], a[:, :, 0, :], float(np.pi / 2), None, ALU.add))
                ts(a[:, :, :, :], a[:, :, :, :], 3.1415925, -3.1415925, ALU.min, ALU.max).then_inc(s_ang, 1)
            dve.wait_ge(s_silu, 1)
            ve.tensor_copy(srep[:, :, :], bc(cvec[:, :], 2, [P, KT, P])).then_inc(s_srep, 1)
            ts(qs[:, :], vec[:, VSQ:VSQ + 1], HD ** -0.5, None, ALU.mult).then_inc(s_qs, 1)

            def ada_row(c):
                b = full(dve, ("ada", c))
                if c >= 2:
                    full(dve, ("adaT", c - 2))
                take(ve.tensor_copy(modrow[c % 2][:, :], b[:, :]), ("ada", c))

            def ada_col(c):
                b = full(dve, ("adaT", c))
                take(tt(mod[:, 4 * c:4 * c + 4], blk3(b[:, :])[:, :, 0], vec[:, VBA + 4 * c:VBA + 4 * c + 4], ALU.add), ("adaT", c))

            for c in range(4):
                ada_row(c)
                if c:
                    ada_col(c - 1)
            ada_col(3)
            for c in range(4):
                taken(dve, ("adaT", c))
            stt(mod[:, 8:16], mod[:, 8:16], 1.0, vec[:, VGA:VGA + 8], ALU.add, ALU.mult).then_inc(s_mod, 1)
            norm(0)
            dve.wait_ge(s_biasr, 16)
            for h in range(H):
                link(ve.tensor_copy(bias[:, h, :], biasr[:, h, :][:, ::-1]))
            ve.memset(bias[0:HD, :, 2 * P - HD:], NEG).then_inc(s_bias, 1)
            for t in range(NT):
                taken(dve, ("win", 0, t))
            for j, (c0, n) in enumerate(((0, QR), (QR, KVR))):
                ins = mean_square(lat[:, :, c0:c0 + n], NT, n, hs[:, 4 * j:4 * j + 4], tmp[:, 0:NT * n].rearrange("p (t n) -> p t n", t=NT))
                if j == 0:
                    link(ins)
            link(ins)
            link(ve.tensor_copy(hs[:, 8:32], hs[:, 0:1].broadcast_to([P, 24])))
            link(ve.tensor_copy(krope[:, :, :], lat[:, :, QR + KVR:]))
            dve.nop().then_inc(s_ms, 1)
            dve.wait_ge(s_rt, 1)
            link(ve.reciprocal(hs[:, 0:8], hs[:, 0:8]))
            link(tt(lat[:, :, 0:QR], lat[:, :, 0:QR], bc(hs[:, 0:4], 2, [P, NT, QR]), ALU.mult))
            tt(lat[:, :, QR:QR + KVR], lat[:, :, QR:QR + KVR], bc(hs[:, 4:8], 2, [P, NT, KVR]), ALU.mult).then_inc(s_nrm, 1)
            for j, a in enumerate((caq, cak)):
                for t in range(NT):
                    taken(dve, ("win", 1 + j, t))
                heads(1 + j, a, tmp).then_inc(s_nrm, 1)
            dve.wait_ge(s_far, 16)
            attention(0, PR1, PT1, o1)
            full(dve, ("S", 0, 4 * H - 1))
            ve.tensor_copy(srep2[:, :, :], bc(cvec[:, :], 2, [P, KT, P])).then_inc(s_srep, 1)
            dve.wait_ge(s_rows1, 64)
            dve.wait_ge(s_trig, 2)
            for j, a in enumerate((mq, mk)):
                for t in range(NT):
                    if j == 0:
                        taken(dve, ("qup", t, 0))
                        taken(dve, ("qup", t, 1))
                    else:
                        taken(dve, ("kvup", t, 0))
                        taken(dve, ("kvup", t, 1))
                        link(ve.tensor_copy(mk[:, t, :, 0:NOPE], kv[:, t, :, 0:NOPE]))
                        link(ve.tensor_copy(mk[:, t, :, NOPE:], bc(krope[:, t, :], 1, [P, H, ROPE])))
                    link(mean_square(a[:, t, :, :], H, QK, hs[:, (3 + j) * 32 + t * H:(3 + j) * 32 + (t + 1) * H], tmpm[:, :, :]))
                dve.nop().then_inc(s_ms, 1)
                dve.wait_ge(s_rt, 4 + j)
                st = hs[:, (3 + j) * 32:(4 + j) * 32]
                link(ve.reciprocal(st, st))
                flat = a[:, :, :, :].rearrange("p t h d -> p (t h) d")
                link(tt(flat, flat, bc(st, 2, [P, 32, QK]), ALU.mult))
                link(tt(flat, flat, bc(grow1[:, j, :], 1, [P, 32, QK]), ALU.mult))
                for t in range(NT):
                    hw = ROPE // 2
                    ins = rope(a[:, t, :, NOPE:NOPE + hw], a[:, t, :, NOPE + hw:], trig1, t,
                               tmpm[:, :, :].rearrange("p h d -> p (h d)"), [P, H, hw])
                    if t < NT - 1:
                        link(ins)
                ins.then_inc(s_nrm, 1)
                dve.wait_ge(s_nrm, 4 + j)
            for h in range(H):
                label = ("mT", 1, h)
                b = full(dve, label)
                take(ve.tensor_copy(mT[1][:, h, :], b[0:QK, :]), label)
            attention(1, PR1, PT1, o1)
            dve.wait_ge(s_gb, 32)
            for c in (4, 5, 10, 11):
                taken(dve, ("ada", c))
            link(tt(gate_a[:, :], gate_a[:, :], gbias[:, 0, :], ALU.add))
            link(tt(gate_m[:, :], gate_m[:, :], gbias[:, 1, :], ALU.add))
            for c in ADAT:
                taken(dve, ("adaT", c))
            link(tt(mod[:, 24:40], mod[:, 24:40], vec[:, VBA + 24:VBA + 40], ALU.add))
            stt(mod[:, 32:40], mod[:, 32:40], 1.0, vec[:, VGM:VGM + 8], ALU.add, ALU.mult).then_inc(s_mod, 1)

            def residual(name, gate):
                for n in range(2):
                    for t in range(NT):
                        label = (name, n, t)
                        b = full(dve, label)
                        xs = x[:, t, n * CW:(n + 1) * CW]
                        if gate is None:
                            take(tt(xs, b[:, :], xs, ALU.add), label)
                            taken(dve, label)
                            if n:
                                dve.nop().then_inc(s_xr, 1)
                            continue
                        take(tt(tmpx[:, :], b[:, :], gate[:, n * CW:(n + 1) * CW], ALU.mult), label)
                        taken(dve, label)
                        ins = tt(xs, xs, tmpx[:, :], ALU.add)
                        if n:
                            ins.then_inc(s_xr, 1)
                            dve.wait_ge(s_xr, {"wout": NT, "down": 2 * NT}[name] + t + 1)
                        else:
                            link(ins)

            dve.nop().then_inc(s_xr, NT)
            residual("wout", gate_a)
            norm(1)
            for i in range(FB + 1):
                c, b2 = divmod(i, 2)
                if i < FB:
                    for gv, dst in ((0, cgate), (1, cval)):
                        label = ("up", c, b2, gv)
                        b = full(dve, label)
                        dve.wait_ge(s_conv, 2 * i + gv + 1)
                        d = dst[i % 2]
                        j = gv * FB + i
                        link(stt(d[:, 1:], b[:, 0:S - 1], vec[:, VEC1 + 2 * FB + j:VEC1 + 2 * FB + j + 1], d[:, 1:], ALU.mult, ALU.add))
                        take(stt(d[:, 2:], b[:, 0:S - 2], vec[:, VEC1 + j:VEC1 + j + 1], d[:, 2:], ALU.mult, ALU.add), label)
                    taken(dve, label)
                    dve.nop().then_inc(s_taps, 1)
                if i:
                    k = i - 1
                    dve.wait_ge(s_cg, k + 1)
                    tt(act[:, k, :], cgs[k % 2][:, :], cval[k % 2][:, :], ALU.mult).then_inc(s_act, 1)
            residual("down", gate_m)
            norm(2)
            dve.wait_ge(s_conb, 16)
            for j, (a, c) in enumerate(((sbq, 0), (sbk, 1))):
                for t in range(NT):
                    taken(dve, ("win2", c, t))
                heads(5 + j, a, tmpr).then_inc(s_nrm, 1)
                dve.wait_ge(s_nrm, 6 + j)
            for j, (a, c) in enumerate(((rq, 2), (rk, 3))):
                for t in range(NT):
                    taken(dve, ("win2", c, t))
                link(heads(7 + j, a, tmpr, scale=None if j == 0 else HD ** -0.5))
                flat = a[:, :, :].rearrange("p t (h d) -> p (t h) d", d=HD)
                link(tt(flat, flat, bc(grow2[:, j, :], 1, [P, 32, HD]), ALU.mult))
                for t in range(NT):
                    hw = HD // 2
                    a4 = a[:, t, :].rearrange("p (h d) -> p h d", h=H)
                    ins = rope(a4[:, :, 0:hw], a4[:, :, hw:], trig2, t, tmpr, [P, H, hw])
                    if t < NT - 1:
                        link(ins)
                ins.then_inc(s_nrm, 1)
                dve.wait_ge(s_nrm, 8 + j)
            for t in range(NT):
                full(dve, ("rT", 1, t))
            rk3 = rk[:, :, :].rearrange("p t (h d) -> p t h d", h=H)
            for t in range(NT):
                taken(dve, ("rT", 0, t))
                link(tt(rk3[:, t], rk3[:, t], bc(cb("kdec"), 2, [P, H, HD]), ALU.mult))
                tt(rqdT[:, :, t * P:(t + 1) * P], rT[0][:, :, t * P:(t + 1) * P], blk3(cb("qdec")), ALU.mult).then_inc(s_rqd, 1)
            dve.wait_ge(s_rqd, NT)
            dve.nop().then_inc(s_kd, 1)
            attention(2, PR2, PT2, o2)
            dve.wait_ge(s_gn, 32)
            dve.wait_ge(s_sg, 1)
            dmat = cb("dmat").rearrange("p (h i) -> p h i", h=H)
            for n in range(NT):
                for j in range(2):
                    label = ("rS", n, j)
                    b = full(dve, label)
                    if n:
                        full(dve, ("rO", n - 1))
                    else:
                        full(dve, ("T", 2, 4 * H - 1))
                    take(tt(rS[:, j::2, :], blk3(b[:, :]), dmat[:, j::2, :], ALU.mult), label)
                if n < NT - 1:
                    label = ("rkv", n)
                    b = full(dve, label)
                    for par in range(2):
                        hp = slice(par * HD, (par + 1) * HD)
                        src = blk3(b[:, :])[hp, :, par * HD:(par + 1) * HD]
                        own = state[hp, :, par * HD:(par + 1) * HD]
                        if n == 0:
                            link(ve.memset(state[hp, :, (1 - par) * HD:(2 - par) * HD], 0.0))
                            ins = ve.tensor_copy(own, src)
                        else:
                            link(tt(own, own, bc(cb("gch")[hp, :], 2, [HD, 4, HD]), ALU.mult))
                            ins = tt(own, src, own, ALU.add)
                        if par == 0:
                            link(ins)
                    take(ins, label)
                    taken(dve, label)
                    dve.nop().then_inc(s_st, 1)
                label = ("rO", n)
                b = full(dve, label)
                take(ve.tensor_copy(gy[:, :, :], b[:, :].rearrange("p (h d) -> p h d", h=H)), label)
                taken(dve, label)
                st = hs[:, (9 + n) * 32:(9 + n) * 32 + 8]
                link(ve.reduce_sum(st, gy[:, :, :], axis=AX))
                link(ts(st, st, 1.0 / HD, None, ALU.mult))
                link(tt(gy[:, :, :], gy[:, :, :], bc(st, 2, [P, H, HD]), ALU.subtract))
                link(mean_square(gy[:, :, :], H, HD, st, gsq[:, :, :]))
                ve.tensor_copy(hs[:, (9 + n) * 32 + 8:(9 + n) * 32 + 32], st[:, 0:1].broadcast_to([P, 24])).then_inc(s_ms, 1)
                dve.wait_ge(s_rt, 10 + n)
                link(ve.reciprocal(st, st))
                link(tt(gy[:, :, :], gy[:, :, :], bc(st, 2, [P, H, HD]), ALU.mult))
                gf = gy[:, :, :].rearrange("p h d -> p (h d)")
                link(tt(gf, gf, gnrow[:, 0, :], ALU.mult))
                link(tt(gf, gf, gnrow[:, 1, :], ALU.add))
                if n >= 2:
                    full(dve, ("oT", 3, n - 2))
                else:
                    full(dve, ("oT", 2, n + 2))
                tt(o2[n % 2][:, :, :].rearrange("p h d -> p (h d)"), gf, rg[:, n, :], ALU.mult).then_inc(s_o, 1)
            ve.memset(zero[:, :], 0.0).then_inc(s_zero, 1)
            residual("wout2", None)
            dve.wait_ge(s_grf, 16)
            norm(3)
            dve.wait_ge(s_wrt, 32)
            b = full(dve, ("router",))
            take(tt(logits[:, :, :], b[:, 0:NT * NE].rearrange("p (t e) -> p t e", t=NT), bc(brt[:, :], 1, [P, NT, NE]), ALU.add), ("router",))
            taken(dve, ("router",))
            for t in range(NT):
                link(ve.max(top8[:, t, :], logits[:, t, :]))
                link(ve.max_index(topi[:, t, :], top8[:, t, :], logits[:, t, :]))
            link(ve.tensor_copy(topf[:, :, :], topi[:, :, :]))
            tt(gate4[:, :, :], top8[:, :, 0:4], top8[:, :, 0:1].broadcast_to([P, NT, 4]), ALU.subtract).then_inc(s_top, 1)
            dve.wait_ge(s_ge, 1)
            link(ve.reduce_sum(den[:, 0:4], gate4[:, :, :], axis=AX))
            link(ve.reciprocal(den[:, 0:4], den[:, 0:4]))
            link(tt(gate4[:, :, :], gate4[:, :, :], bc(den[:, 0:4], 2, [P, NT, 4]), ALU.mult))
            dve.wait_ge(s_conc, 16)
            shape = [P, NT, NE]
            experts = bc(cc("iota")[:, 0:NE], 1, shape)
            link(ve.tensor_copy(route[:, :, 0], cc("tok")))
            link(ve.memset(route[:, :, 1], 1.0))
            for k in range(4):
                eq = chosen if k == 0 else eqk
                link(tt(eq[:, :, :], experts, topf[:, :, k:k + 1].broadcast_to(shape), ALU.is_equal))
                gk = gate4[:, :, k:k + 1].broadcast_to(shape)
                if k == 0:
                    link(tt(route[:, :, 2:], eq[:, :, :], gk, ALU.mult))
                else:
                    link(tt(chosen[:, :, :], chosen[:, :, :], eqk[:, :, :], ALU.add))
                    link(tt(eqk[:, :, :], eqk[:, :, :], gk, ALU.mult))
                    link(tt(route[:, :, 2:], route[:, :, 2:], eqk[:, :, :], ALU.add))
            link(ve.memset(ones[:, :], 1.0))
            dve.nop().then_inc(s_route, 1)
            b = full(dve, ("rank",))
            link(ve.tensor_copy(cntp[:, :], b[:, NT * NE:(NT + 1) * NE]))
            take(tt(rank[:, :, :], b[:, 0:NT * NE].rearrange("p (t e) -> p t e", t=NT), chosen[:, :, :], ALU.mult), ("rank",))
            taken(dve, ("rank",))
            link(ts(rank[:, :, :], rank[:, :, :], -1.0, None, ALU.add))
            for k in range(1, 4):
                link(ts(nblk[:, k, :], cntp[:, :], float(k * P), None, ALU.is_gt))
            link(tt(nblk[:, 0, :], nblk[:, 1, :], nblk[:, 2, :], ALU.add))
            link(tt(nblk[:, 0, :], nblk[:, 0, :], nblk[:, 3, :], ALU.add))
            link(ts(nblk[:, 0, :], nblk[:, 0, :], 1.0, None, ALU.add))
            link(ve.tensor_tensor_scan(ends[:, :], one[:, 0:1].broadcast_to([P, NE]), nblk[:, 0, :], 0.0, ALU.mult, ALU.add))
            shape = [P, MAXSLOT, NE]
            link(tt(cmp[:, :, :], bc(ends[:, :], 1, shape), bc(cc("slots"), 2, shape), ALU.is_le))
            link(ve.reduce_sum(slot_f[:, 0, :], cmp[:, :, :], axis=AX))
            link(ts(slot_f[:, 0, :], slot_f[:, 0, :], NE - 1.0, None, ALU.min))
            link(tt(cmp[:, :, :], cmp[:, :, :], bc(ends[:, :], 1, shape), ALU.mult))
            link(ve.tensor_reduce(slot_f[:, 1, :], cmp[:, :, :], AX, ALU.max))
            link(tt(slot_f[:, 2, :], cc("slots"), slot_f[:, 1, :], ALU.subtract))
            link(ts(slot_f[:, 2, :], slot_f[:, 2, :], float(P), None, ALU.mult))
            link(ve.tensor_copy(slot_i[:, :, :], slot_f[:, :, :]))
            ve.tensor_copy(nb_i[:, :], ends[:, NE - 1:NE]).then_inc(s_slots, 1)
            dve.wait_ge(s_bsum, 32)
            dve.wait_ge(s_acc, 16 * NT)
            for k in range(3):
                b3 = bias3[k * NE:(k + 1) * NE, :]
                src = bsum if k == 0 else brem
                if k:
                    link(tt(brem[:, :], src0[:, :], back3[:, :], ALU.subtract))
                link(ve.tensor_copy(b3, src[:, :]))
                if k < 2:
                    src0 = src
                    back3 = bsum if k else btmp
                    link(ve.tensor_copy(back3[:, :], b3))
            dve.nop().then_inc(s_b3, 1)

            def build(s_, i):
                e = slot_reg(dve, 0, s_, NE - 1)
                first = slot_reg(dve, 2, s_, 3 * P)
                for t in range(NT):
                    ins = ts(pick[:, t, :], cc("iota")[:, bass.ds(first, P)], rank[:, t, bass.ds(e, 1)], None, ALU.is_equal)
                ins.then_inc(s_pick, 1)

            def found(i, k):
                e = slot_reg(dve, 0, i, NE - 1)
                dve.wait_ge(bank_full[7], k)
                ve.tensor_copy(picked[:, :], bank[7][:, 0:2 + NE]).then_inc(bank_taken[7], 1)
                return e

            def index(i, e, k, got):
                dve.wait_ge(bank_taken[7], k)
                ts(idx_f[:, 0:1], picked[:, 1:2], -1.0, 1.0, ALU.mult, ALU.add).then_inc(s_empty, 1)
                dve.wait_ge(s_empty, i + 1)
                stt(idx_f[:, 1:2], idx_f[:, 0:1], cc("trash"), picked[:, 0:1], ALU.mult, ALU.add).then_inc(s_row, 1)
                ve.tensor_copy(gates[:, slot_at(i)], picked[:, bass.ds(e + 2, 1)]).then_inc(s_gate, 1)
                dve.wait_ge(s_row, i + 1)
                ve.tensor_copy(idx_all[:, slot_at(i)], idx_f[:, 1:2]).then_inc(s_gate, 1)
                if got is not None:
                    dve.wait_ge(s_got, got)
                ve.tensor_copy(idx_in[:, :], idx_f[:, 1:2]).then_inc(s_idx, 1)

            def activation(i):
                for j in range(2):
                    dve.wait_ge(bank_full[j], FU[j] + 1 + i)
                    ts(eg[j][:, :], bank[j][:, :], 7.0, None, ALU.min).then_inc(bank_taken[j], 1)
                    dve.wait_ge(bank_full[2 + j], FU[2 + j] + 1 + i)
                    ts(el[j][:, :], bank[2 + j][:, :], -7.0, 7.0, ALU.max, ALU.min).then_inc(bank_taken[2 + j], 1)
                    dve.wait_ge(bank_taken[2 + j], TK[2 + j] + 1 + i)
                    dve.wait_ge(s_sig, 2 * i + (j + 1))
                    stt(el[j][:, :], el[j][:, :], 1.0, es[j][:, :], ALU.add, ALU.mult).then_inc(s_lin, 1)
                    dve.wait_ge(s_lin, 2 * i + (j + 1))
                    tt(ea[:, j * CW:(j + 1) * CW], el[j][:, :], eg[j][:, :], ALU.mult).then_inc(s_ea, 1)

            def hot_row(dst, s_, s):
                ts(dst[:, :], cc("pmod")[0:3 * NE, :], slot_f[0:3 * NE, 0, slot_at(s_)], None, ALU.is_equal).then_inc(s, 1)

            dve.wait_ge(s_slots, 1)
            build(0, 0)
            e = found(0, FU[7] + 1)
            index(0, e, TK[7] + 1, None)
            build(1, 1)
            hot_row(hot[0], 0, s_hotu)
            e = found(1, FU[7] + 3)
            index(1, e, TK[7] + 3, 16)
            build(2, 2)
            activation(0)
            hot_row(hot[0], 1, s_hotu)
            nb = n_slots(dve)
            with dve.Fori(1, nb) as i:
                e = found(i + 1, 3 * i + (FU[7] + 2))
                index(i + 1, e, 3 * i + (TK[7] + 2), 16 * i + 16)
                build(i + 2, i + 2)
                dve.wait_ge(bank_full[5], i + (FU[5] - 1))
                hot_row(hot[1], i - 1, s_hotd)
                activation(i)
                hot_row(hot[0], i + 1, s_hotu)
                dve.wait_ge(s_scat, 16 * i)
                dve.wait_ge(s_gate, 2 * i)
                ve.tensor_copy(idx_out[:, :], idx_all[:, bass.ds(i - 1, 1)]).then_inc(s_ix, 1)
            dve.wait_ge(bank_full[5], nb + (FU[5] - 1))
            hot_row(hot[1], nb - 1, s_hotd)
            dve.wait_ge(s_scat, 16 * nb)
            ve.tensor_copy(idx_out[:, :], idx_all[:, bass.ds(nb - 1, 1)]).then_inc(s_ix, 1)
            norm(4)
            for t in range(NT):
                for n in range(2):
                    taken(dve, ("gate", t, n))
                if t >= 2:
                    dve.wait_ge(s_stored[t % 2], 16 * (t // 2))
                link(tt(xo[t % 2][:, :], pp[:, t, :], fgate[t % 2][:, :], ALU.mult))
                tt(xo[t % 2][:, :], xo[t % 2][:, :], x[:, t, :], ALU.add).then_inc(s_out, 1)


_INPUTS = ("x", "c", "positions", "w_ada", "b_ada", "g_attn_norm", "w_in", "g_q_latent", "g_kv_latent", "w_q_up", "w_kv_up",
           "g_mla_q", "g_mla_k", "g_ca_q", "g_ca_k", "rel_bias", "w_out", "g_mlp_norm", "w_up", "conv_w", "conv_b", "w_down",
           "p_2", "positions_2", "g_mix_norm_2", "w_in_2", "sb_q_gain_2", "sb_k_gain_2", "ret_q_gain_2", "ret_k_gain_2",
           "ret_gn_gain_2", "ret_gn_bias_2", "w_out_2", "g_ffn_norm_2", "w_router_2", "b_router_2", "w_up_gate_2",
           "b_up_gate_2", "w_down_2", "b_down_2", "g_ple_norm_2", "w_ple_gate_2", "w_ple_proj_2")


def kernel(**inputs):
    import concourse.bacc as bacc
    from concourse.bass_utils import run_bass_kernel_spmd

    nc = bacc.Bacc("TRN2", target_bir_lowering=False, num_devices=1)
    arrays = {f"in_{name}": np.ascontiguousarray(inputs[name]) for name in _INPUTS}
    arrays["in_consts"] = constants()[2]
    g = {name[3:]: nc.dram_tensor(name, a.shape, mybir.dt.from_np(a.dtype), kind="ExternalInput").ap() for name, a in arrays.items()}
    out = nc.dram_tensor("out", (1, S, D), FP, kind="ExternalOutput").ap()
    program(nc, g, out)
    r = run_bass_kernel_spmd(nc, [arrays], core_ids=[0])
    return r.results[0]["out"]
```

```python
import numpy as np
import concourse.bass as bass
from concourse import mybir

FP = mybir.dt.float32
BF = mybir.dt.bfloat16
FR = mybir.dt.float32r
I32 = mybir.dt.int32
U32 = mybir.dt.uint32
ALU = mybir.AluOpType
ACT = mybir.ActivationFunctionType
AX = mybir.AxisListType.X

P = 128
S = 512
NT = S // P
D = 1024
KT = D // P
H = 8
HD = 64
QK = 96
NOPE, ROPE = 64, 32
QR, KVR = 256, 128
LAT = QR + KVR + ROPE
FF = 2816
FB = FF // P
EPS = 1e-6
NEG = -1e30
NE = 32
MAXSLOT = 50
TRASH = S
CW = 512
CHUNK = KT * CW
RING_D = 4
CHUNKS_E = 6
HALVES = 2 * CHUNKS_E
STAGES = 4
PAIRS = 6
BY_POOL = (4, 9)

VC, VGA, VGM, VG2, VGF, VGP, VQL, VKL, VCQ, VCK, VSQ, VSK, VCB = 0, 8, 16, 24, 32, 40, 48, 50, 51, 52, 53, 54, 55
NV = VCB + 2 * FB
CWA = 2 * 2 * FB
VEC1, VEC2 = P, 256
VBA = VEC2 + 2 * FB


def constants():
    p = np.arange(P, dtype=np.float64)
    half1, half2 = ROPE // 2, HD // 2
    inv1 = 10000.0 ** (-np.arange(half1) / half1)
    inv2 = 10000.0 ** (-np.arange(half2) / half2)
    log_g = np.log(1.0 - 2.0 ** (-5.0 - np.arange(H)))
    diff = p[None, :] - p[:, None]
    dmat = np.where(diff[:, None] >= 0, np.exp(log_g[None, :, None] * np.maximum(diff, 0)[:, None]), 0.0)
    qdec = np.zeros((P, H // 2, P))
    gch = np.zeros((P, H // 2))
    for par in range(2):
        for pair in range(H // 2):
            qdec[par * HD:(par + 1) * HD, pair] = np.exp(log_g[2 * pair + par] * (p + 1.0))[None]
            gch[par * HD:(par + 1) * HD, pair] = np.exp(log_g[2 * pair + par] * P)
    kdec = np.exp(log_g[None, :] * (P - 1 - p)[:, None])
    parts = [
        ("a", [("ident", np.eye(P)), ("inv1", np.tile(inv1, (P, 1))), ("inv2", np.tile(inv2, (P, 1)))]),
        ("b", [("strict", (p[None, :] < p[:, None]) * 1.0), ("negm", np.where(p[None, :] < p[:, None], 0.0, NEG)),
               ("dmat", dmat.reshape(P, -1)), ("qdec", qdec.reshape(P, -1)), ("kdec", kdec), ("gch", gch)]),
        ("c", [("tri", (p[:, None] <= p[None, :]) * 1.0), ("iota", np.tile(np.arange(S), (P, 1))),
               ("slots", np.tile(np.arange(MAXSLOT), (P, 1))), ("tok", p[:, None] + P * np.arange(NT)[None, :]),
               ("trash", TRASH + p[:, None]), ("pmod", np.tile((p % 32)[:, None], (1, P)))]),
    ]
    where, cols, packs = {}, [], {}
    at = 0
    for pack, entries in parts:
        start = at
        for name, a in entries:
            where[name] = (at - start, a.shape[1])
            at += a.shape[1]
            cols.append(a)
        packs[pack] = (start, at - start)
    return where, packs, np.concatenate(cols, axis=1).astype(np.float32)


def program(nc, g, out):
    where, packs, _ = constants()

    BASE = 16512
    KB = 1024
    names = [0]

    def at(off, shape, dt=FP, name=None):
        names[0] += 1
        return nc.alloc_sbuf_tensor_at(f"{name or 't'}_{names[0]}", shape, dt, offset=BASE + int(off))

    ring = [at(s * 16 * KB, [P, CHUNK], name=f"ring{s}") for s in range(RING_D)]
    x = at(64 * KB, [P, NT, D], name="x")
    hT = at(80 * KB, [P, KT, S], name="hT")
    gate_a = at(96 * KB, [P, D], name="gate_a")
    gate_m = at(100 * KB, [P, D], name="gate_m")
    C = [104 * KB]

    def take_C(shape, dt=FP, name=None):
        t = at(C[0], shape, dt, name)
        C[0] += -(-int(np.prod(shape[1:])) * 4 // 32) * 32
        return t
    cona = take_C([P, packs["a"][1]], name="cona")
    vec = take_C([P, 352], name="vec")
    mod = take_C([P, 48], name="mod")
    stat = take_C([P, 96], name="stat")
    trig1 = take_C([P, NT, 2, ROPE // 2], name="trig1")
    trig2 = take_C([P, NT, 2, HD // 2], name="trig2")
    soft = take_C([P, 64], name="soft")
    hs = take_C([P, 416], name="hs")
    krope = take_C([P, NT, ROPE], name="krope")
    den = take_C([P, 8], name="den")
    cvec = take_C([P, 8], name="cvec")
    eps = take_C([P, 1], name="eps")
    one = take_C([P, 1], name="one")
    qs = take_C([P, 1], name="qs")
    assert C[0] <= 112 * KB, C[0]
    R = 112 * KB
    ident = cona[:, where["ident"][0]:where["ident"][0] + P]
    inv1 = cona[:, where["inv1"][0]:where["inv1"][0] + ROPE // 2]
    inv2 = cona[:, where["inv2"][0]:where["inv2"][0] + HD // 2]


    srep = at(R, [P, KT, P], name="srep")
    vrow = [at(R + 4 * KB, [NV, P], name="vrow0"), at(R + 5 * KB, [CWA, P], name="vrow1"),
            at(R + 6 * KB, [2 * FB + 48, P], name="vrow2")]
    modrow = [at(R + 8 * KB, [P, CW], name="modrow0"), at(R + 10 * KB, [P, CW], name="modrow1")]
    ang = [at(R + 16 * KB, [P, NT, 2, ROPE // 2], name="ang0"), at(R + 20 * KB, [P, NT, 2, HD // 2], name="ang1")]
    angk = at(R + 17 * KB, [P, NT, 2, HD // 2], name="angk")
    posi = at(R + 19 * KB, [P, 2, NT], I32, name="posi")
    posf = at(R + 19 * KB + 64, [P, 2, NT], name="posf")
    junk = at(R + 66 * KB, [P, D], name="junk")
    xn = [at(R + 70 * KB, [P, D], name="xn0"), at(R + 74 * KB, [P, D], name="xn1")]
    caq = at(R, [P, NT, CW], name="caq")
    cak = at(R + 8 * KB, [P, NT, CW], name="cak")
    caT = [at(R + 16 * KB, [P, NT, S], name="caqT"), at(R + 24 * KB, [P, NT, S], name="cakT")]
    cav = at(R + 32 * KB, [P, NT, CW], name="cav")
    bias = at(R + 40 * KB, [P, H, 2 * P], name="bias")
    biasr = at(R + 78 * KB, [P, H, 2 * P], name="biasr")
    lat = at(R + 48 * KB, [P, NT, LAT], name="lat")
    latT = at(R + 55 * KB, [P, 3, S], name="latT")
    kv = at(R + 62 * KB, [P, NT, H, 2 * HD], name="kv")
    tmp = at(R + 78 * KB, [P, NT * CW], name="tmp")
    mq = at(R, [P, NT, H, QK], name="mq")
    mk = at(R + 78 * KB, [P, NT, H, QK], name="mk")
    tmpm = at(R + 90 * KB, [P, H, QK], name="tmpm")
    mT = [at(R + 16 * KB, [QK, H, S], name="mqT"), at(R + 32 * KB, [QK, H, S], name="mkT")]
    PR1 = [at(R + (48 + 2 * i) * KB, [P, S], name=f"probs1_{i}") for i in range(3)]
    PT1 = [at(R + (54 + 2 * i) * KB, [P, NT, P], name=f"probsT1_{i}") for i in range(2)]
    o1 = [at(R + (58 + 2 * i) * KB, [P, H, HD], name=f"o1_{i}") for i in range(2)]
    farb = at(R + 94 * KB, [P, H], name="farb")
    grow1 = at(R + 94 * KB + 64, [P, 2, QK], name="grow1")
    grow2 = at(R + 94 * KB + 64 + 768, [P, 2, HD], name="grow2")
    modrow2 = [at(R + 12 * KB, [P, CW], name="modrow2"), at(R + 14 * KB, [P, CW], name="modrow3")]
    srep2 = at(R + 16 * KB, [P, KT, P], name="srep2")
    gbias = at(R, [P, 2, D], name="gbias")
    act = at(R, [P, FB, S], name="act")
    cgate = [at(R + (44 + 4 * i) * KB, [P, S], name=f"cgate{i}") for i in range(2)]
    cval = [at(R + (46 + 4 * i) * KB, [P, S], name=f"cval{i}") for i in range(2)]
    cgs = [at(R + (52 + 2 * i) * KB, [P, S], name=f"cgs{i}") for i in range(2)]
    hTs = [at(R + 78 * KB, [P, KT, S], FR, name="hT_hi"), at(R + 56 * KB, [P, KT, S], FR, name="hT_lo")]
    u_hi = [at(o, [P, KT, 2 * P], FR, name=f"up_hi{i}") for i, o in enumerate((48 * KB, 80 * KB))]
    u_lo = [at(o, [P, KT, 2 * P], FR, name=f"up_lo{i}") for i, o in enumerate((56 * KB, 88 * KB))]
    conb = at(96 * KB, [P, packs["b"][1]], name="conb")
    def cb(n):
        return conb[:, where[n][0]:where[n][0] + where[n][1]]
    sbq = at(R, [P, NT, CW], name="sbq")
    sbk = at(R + 8 * KB, [P, NT, CW], name="sbk")
    sbT = [at(R + 16 * KB, [P, NT, S], name="sbqT"), at(R + 24 * KB, [P, NT, S], name="sbkT")]
    sbv = at(R + 32 * KB, [P, NT, CW], name="sbv")
    rq = at(R + 40 * KB, [P, NT, CW], name="rq")
    rk = at(R + 48 * KB, [P, NT, CW], name="rk")
    rv = at(R + 56 * KB, [P, NT, CW], name="rv")
    rg = at(R + 64 * KB, [P, NT, CW], name="rg")
    rT = [at(R, [P, NT, S], name="rqT"), at(R + 8 * KB, [P, NT, S], name="rkT")]
    rqdT = at(R + 72 * KB, [P, NT, S], name="rqdT")
    tmp2 = at(R + 72 * KB, [P, NT * CW], name="tmp2")
    tmpr = at(R + 80 * KB, [P, NT * CW], name="tmpr")
    PR2 = [at((40 + 2 * i) * KB, [P, S], name=f"probs2_{i}") for i in range(4)]
    PT2 = [at(R + (86 + 2 * i) * KB, [P, NT, P], name=f"probsT2_{i}") for i in range(2)]
    o2 = [at(R + (90 + 2 * i) * KB, [P, H, HD], name=f"o2_{i}") for i in range(2)]
    sbl = [at((32 + 2 * i) * KB, [P, S], name=f"sbl{i}") for i in range(4)]
    sbw = [at((88 + 2 * i) * KB, [P, S], name=f"sbw{i}") for i in range(4)]
    rS = at(R + 80 * KB, [P, H, P], name="rS")
    state = at(R + 84 * KB, [P, H // 2, 2 * HD], name="state")
    gy = at(R + 86 * KB, [P, H, HD], name="gy")
    gsq = at(R + 88 * KB, [P, H, HD], name="gsq")
    gnrow = at(R + 16 * KB, [P, 2, CW], name="gnrow")
    wrt = at(R + 80 * KB, [P, KT, NE], name="wrt")
    ptok = at(R + 48 * KB, [P, NT, 256], name="ptok")
    pT = at(R + 52 * KB, [P, 2, S], name="pT")
    grow_f = at(R + 56 * KB, [P, D], name="grow_f")
    pp = at(R + 32 * KB, [P, NT, D], name="pp")
    bsum = at(R, [NE, 3 * D], name="bsum")
    brem = at(R + 12 * KB, [NE, 3 * D], name="brem")
    btmp = at(R + 24 * KB, [NE, D], name="btmp")
    tmpx = at(R + 62 * KB, [P, CW], name="tmpx")
    zero = at(R + 62 * KB, [P, D], name="zero")
    HALF = CHUNK // 2
    stage = [at((32 + 8 * i) * KB, [P, HALF], name=f"stage{i}") for i in range(STAGES)]
    pair_at = [0, 16 * KB, R, R + 16 * KB, 64 * KB, 80 * KB]
    w_hi = [at(o, [P, HALF], FR, name=f"w_hi{i}") for i, o in enumerate(pair_at)]
    w_lo = [at(o + 8 * KB, [P, HALF], FR, name=f"w_lo{i}") for i, o in enumerate(pair_at)]
    rows = at(R + 48 * KB, [P, D], name="rows")
    xeT = [at(R + 52 * KB, [P, KT, P], FR, name="xeT_hi"), at(R + 91 * KB + 512, [P, KT, P], FR, name="xeT_lo")]
    ea = at(R + 56 * KB, [P, D], name="ea")
    eaT = [at(R + 60 * KB, [P, KT, P], FR, name="eaT_hi"), at(R + 76 * KB, [P, KT, P], FR, name="eaT_lo")]
    ey = at(R + 64 * KB, [P, D], name="ey")
    eg = [at(R + (68 + 2 * i) * KB, [P, CW], name=f"eg{i}") for i in range(2)]
    el = [at(R + (72 + 2 * i) * KB, [P, CW], name=f"el{i}") for i in range(2)]
    pick = at(R + 80 * KB, [P, NT, P], name="pick")
    bias3 = at(R + 82 * KB, [3 * NE, 3 * D], BF, name="bias3")
    conc = at(R + 88 * KB, [P, packs["c"][1]], name="conc")
    def cc(n):
        return conc[:, where[n][0]:where[n][0] + where[n][1]]
    T = [96 * KB]

    def take_T(shape, dt=FP, name=None):
        t = at(T[0], shape, dt, name)
        T[0] += -(-int(np.prod(shape[1:])) * (2 if dt == BF else 4) // 32) * 32
        return t

    logits = take_T([P, NT, NE], name="logits")
    top8 = take_T([P, NT, 8], name="top8")
    topi = take_T([P, NT, 8], U32, name="topi")
    topf = take_T([P, NT, 8], name="topf")
    gate4 = take_T([P, NT, 4], name="gate4")
    chosen = take_T([P, NT, NE], name="chosen")
    route = take_T([P, NT, 2 + NE], name="route")
    rank = take_T([P, NT, NE], name="rank")
    eqk = take_T([P, NT, NE], name="eqk")
    nblk = take_T([P, 4, NE], name="nblk")
    ends = take_T([P, NE], name="ends")
    slot_f = take_T([P, 3, MAXSLOT], name="slot_f")
    slot_i = take_T([P, 3, MAXSLOT], I32, name="slot_i")
    cmp = at(R + 56 * KB, [P, MAXSLOT, NE], name="cmp")
    picked = take_T([P, 2 + NE], name="picked")
    gates = take_T([P, MAXSLOT], name="gates")
    idx_f = take_T([P, 4], name="idx_f")
    idx_all = take_T([P, MAXSLOT], I32, name="idx_all")
    idx_in = take_T([P, 1], I32, name="idx_in")
    idx_out = take_T([P, 1], I32, name="idx_out")
    hot = [take_T([3 * NE, P], BF, name=f"hot{i}") for i in range(2)]
    nb_i = take_T([P, 1], I32, name="nb_i")
    ones = take_T([P, P], name="ones")
    cntp = take_T([P, NE], name="cntp")
    brt = take_T([P, NE], name="brt")
    assert T[0] <= 104 * KB, T[0]

    bank = [nc.alloc_psum_tensor(f"bank{i}", [P, 512], FP) for i in range(8)]
    xo = [at(R + (48 + 4 * i) * KB, [P, D], name=f"xo{i}") for i in range(2)]
    fgate = [at(R + (56 + 4 * i) * KB, [P, D], name=f"fgate{i}") for i in range(2)]
    hn_d = nc.dram_tensor("hn_rows", [S + P, D], FP).ap()
    acc_d = nc.dram_tensor("moe_sum", [S + P, D], FP).ap()
    ext_d = nc.dram_tensor("rel_bias_ext", [H, 3 * P], FP).ap()

    def cols(w, c0, n, k0=0, kn=None):
        kn = kn or w.shape[0] // P
        return w[k0 * P:(k0 + kn) * P, c0:c0 + n].rearrange("(k p) n -> p k n", p=P)

    w = {n: g[n].rearrange("l a b -> (l a) b") for n in
         ("w_ada", "w_in", "w_q_up", "w_kv_up", "w_out", "w_up", "w_down", "w_in_2", "w_out_2", "w_router_2",
          "w_ple_gate_2", "w_ple_proj_2")}
    chunks = []

    def chunk(label, *parts):
        chunks.append((label, parts))

    for c in range(4):
        chunk(("ada", c), (0, KT, CW, cols(w["w_ada"], c * CW, CW)))
    for c, (c0, n) in enumerate([(0, LAT), (LAT, CW), (LAT + CW, CW), (LAT + 2 * CW, CW)]):
        chunk(("win", c), (0, KT, n, cols(w["w_in"], c0, n)))
    chunk(("mlaup",), (0, 2, H * QK, cols(w["w_q_up"], 0, H * QK)), (2 * H * QK, 1, H * 2 * HD, cols(w["w_kv_up"], 0, H * 2 * HD)))
    for c in range(4, 12):
        chunk(("ada", c), (0, KT, CW, cols(w["w_ada"], c * CW, CW)))
    for n in range(2):
        chunk(("wout", n), (0, KT, CW, cols(w["w_out"], n * CW, CW)))
    for c in range(FB // 2):
        chunk(("up", c), (0, KT, 2 * P, cols(w["w_up"], c * 2 * P, 2 * P)), (KT * 2 * P, KT, 2 * P, cols(w["w_up"], FF + c * 2 * P, 2 * P)))
    DK = [(0, 8), (8, 8), (16, 6)]
    for n in range(2):
        for j, (k0, kn) in enumerate(DK):
            chunk(("down", n, j), (0, kn, CW, cols(w["w_down"], n * CW, CW, k0, kn)))
    IN2 = [0, 1, 3, 4, 2, 5, 6]
    for c in range(7):
        chunk(("win2", c), (0, KT, CW, cols(w["w_in_2"], IN2[c] * CW, CW)))
    for n in range(2):
        chunk(("wout2", n), (0, KT, CW, cols(w["w_out_2"], n * CW, CW)))
    chunk(("ple",), (0, 2, D, cols(w["w_ple_proj_2"], 0, D)))
    number = {c[0]: i for i, c in enumerate(chunks)}
    ND = len(chunks)
    N_VROW = 9 + 8 + 3
    fills = [0] * RING_D
    arrives = {}
    UP0 = number[("up", 0)]
    place = [(i - UP0) % 3 if 0 <= i - UP0 < FB // 2 else i % RING_D for i in range(ND)]
    before = [max((j for j in range(i) if place[j] == place[i]), default=None) for i in range(ND)]
    before_split = max(j for j in range(UP0) if place[j] == 3)
    for i, (label, parts) in enumerate(chunks):
        fills[place[i]] += len(parts)
        arrives[label] = (place[i], 16 * fills[place[i]])

    def last_product(label):
        kind = label[0]
        if kind == "down":
            return ("down", label[1], NT - 1) if label[2] == 2 else 2 * label[1] + label[2] + 1
        return {"ada": label, "mlaup": ("kvup", NT - 1, 1), "ple": ("ple", NT - 1, 1)}.get(kind) or (*label, NT - 1)

    def part(slot, off, k, n):
        return ring[slot][:, off:off + k * n].rearrange("p (k n) -> p k n", k=k)

    order = []
    rot = [0]

    def product(label, b=None):
        if b is None:
            b = rot[0] % 8
            rot[0] += 1
        order.append((label, b))


    LAG = {0: 2, 1: 2, 2: 8}
    OT_LAG = {k: n + 4 for k, n in LAG.items()}

    def attention_order(kind):
        for s in range(4 * H + OT_LAG[kind] + 1):
            if s < 4 * H:
                product(("S", kind, s), (0, 1, 2, 6)[s % 4] if kind == 2 else s % 3)
            i = s - LAG[kind]
            if 0 <= i < 4 * H:
                product(("T", kind, i), 3 + i % 2)
            i -= 1
            if 0 <= i < 4 * H and i % H == 0:
                product(("O", kind, i // H), 5 if kind == 2 else 5 + i // H % 2)
            if s >= H + OT_LAG[kind] and (s - OT_LAG[kind]) % H == 0:
                product(("oT", kind, (s - OT_LAG[kind]) // H - 1), 7)

    def norm_order(nz):
        for t in range(NT):
            for j in range(2):
                product(("xT", nz, t, j))

    product(("vecs",))
    for c in range(4):
        product(("ada", c))
        if c:
            product(("adaT", c - 1))
    product(("adaT", 3))
    norm_order(0)
    for c in range(3):
        for t in range(NT):
            product(("win", c, t))
    for t in range(NT):
        product(("latT", t))
    for t in range(NT):
        product(("win", 3, t))
    for qk in range(2):
        for t in range(NT):
            product(("caT", qk, t))
    for t in range(NT):
        for n in range(2):
            product(("qup", t, n))
    for t in range(NT):
        for n in range(2):
            product(("kvup", t, n))
    attention_order(0)
    ADAT = (6, 7, 8, 9)
    for c in range(4, 12):
        product(("ada", c))
        if c - 1 in ADAT:
            product(("adaT", c - 1))
    for qk in range(2):
        for h in range(H):
            product(("mT", qk, h))
    attention_order(1)
    for n in range(2):
        for t in range(NT):
            product(("wout", n, t))
    norm_order(1)
    for c in range(FB // 2):
        for gv in range(2):
            for b in range(2):
                product(("up", c, b, gv))
    for n in range(2):
        for t in range(NT):
            product(("down", n, t))
    norm_order(2)
    for c in range(7):
        for t in range(NT):
            product(("win2", c, t))
        if c == 3:
            for qk in range(2):
                for t in range(NT):
                    product(("sbT", qk, t))
    for qk in range(2):
        for t in range(NT):
            product(("rT", qk, t))
    attention_order(2)
    for n in range(NT):
        product(("rS", n, 0), 0); product(("rS", n, 1), 1)
        product(("rO", n), 2 + n % 2)
        if n < NT - 1:
            product(("rkv", n), 4)
        if n:
            product(("oT", 3, n - 1), 7)
    product(("oT", 3, NT - 1), 7)
    for n in range(2):
        for t in range(NT):
            product(("wout2", n, t))
    for t in range(NT):
        product(("pT", t))
    for t in range(NT):
        for n in range(2):
            product(("ple", t, n))
        for j in range(2):
            product(("xT", 3, t, j))
    product(("router",))
    product(("rank",))
    uses = [0] * 8
    told = [0] * 8
    bank_of = {}
    for label, b in order:
        assert label not in bank_of, label
        uses[b] += 1
        told[b] += label[0] != "O"
        bank_of[label] = (b, uses[b], told[b])
    FU, TK = list(told), list(uses)
    late, late_uses = [], [0] * 8
    for t in range(NT):
        for j in range(2):
            late.append((("xT", 4, t, j), (2 * t + j) % 8))
    for t in range(NT):
        for n in range(2):
            late.append((("gate", t, n), (2 * t + n) % 8))
    for label, b in late:
        late_uses[b] += 1
        bank_of[label] = (b, late_uses[b], late_uses[b])
    late = {label for label, _ in late}

    sem = nc.alloc_semaphore
    ring_in = [sem(f"ring_in{i}") for i in range(RING_D)]
    stage_in = [sem(f"stage_in{i}") for i in range(STAGES)]
    s_uhi, s_ulo, s_thi, s_tlo = sem("up_weights_hi"), sem("up_weights_lo"), sem("hT_hi"), sem("hT_lo")
    s_hi, s_lo, s_lo_pool = sem("weights_hi"), sem("weights_lo"), sem("weights_lo_pool")
    s_first = sem("first_half_used")
    s_xhi = sem("expert_rows_hi")
    w_used = sem("w_used")
    bank_full = [sem(f"bank_full{i}") for i in range(8)]
    bank_taken = [sem(f"bank_taken{i}") for i in range(8)]
    s_lin, s_empty, s_row, s_gate = sem("linear_part"), sem("empty_places"), sem("row_numbers"), sem("gates_and_rows")
    late_full = [sem(f"late_full{i}") for i in range(8)]
    late_taken = [sem(f"late_taken{i}") for i in range(8)]
    s_mset, s_bias, s_taps, s_qs, s_top, s_ge, s_ix = (sem(n) for n in (
        "constants_set", "bias_windows", "conv_taps", "stick_q_gain", "top_values", "gate_exp", "scatter_index"))
    s_con, s_vrow, s_x, s_pos, s_rows1, s_ext, s_biasr, s_far = (sem(n) for n in (
        "consts_in", "vectors_in", "x_in", "positions_in", "gain_rows_in", "bias_ext_in", "bias_windows_in", "far_bias_in"))
    s_ext2, s_gb, s_conb, s_gn, s_grf, s_wrt, s_ptok, s_conc, s_bsum = (sem(n) for n in (
        "bias_ext_out", "gate_bias_in", "consts_b_in", "group_norm_rows_in", "ffn_gain_row_in", "router_in", "p_in",
        "consts_c_in", "expert_bias_in"))
    s_ang, s_trig, s_silu, s_srep = sem("angles"), sem("trig"), sem("silu_c"), sem("silu_c_rep")
    s_mod, s_sq, s_xn, s_hTv = sem("modulation"), sem("x_rms"), sem("x_normed"), sem("hT_vector")
    s_ms, s_rt, s_nrm = sem("head_mean_square"), sem("head_rms"), sem("head_normed")
    s_max, s_P, s_pv = sem("row_max"), sem("probs"), sem("pv_done")
    s_ln, s_arg, s_o = sem("log1p"), sem("log_weight"), sem("attention_out")
    s_conv, s_cg, s_act, s_xr = sem("conv_done"), sem("gate_silu"), sem("mlp_act"), sem("x_updated")
    s_rqd, s_kd, s_rS, s_st, s_sg = sem("rqd"), sem("k_decayed"), sem("ret_scores"), sem("ret_state"), sem("ret_gate")
    s_zero, s_zd, s_acc = sem("zeros"), sem("zeros_out"), sem("moe_sum_init")
    s_hn = [sem(f"hn_rows_out{i}") for i in range(2)]
    s_route, s_slots, s_b3 = sem("routes"), sem("slot_table"), sem("expert_bias_split")
    s_pick, s_idx, s_got, s_ea, s_hotu, s_hotd = (sem(n) for n in (
        "pick_built", "gather_index", "rows_gathered", "expert_act", "hot_up", "hot_down"))
    s_sig, s_scat, s_back = sem("glu_sigmoid"), sem("scattered"), sem("sum_back")
    s_out = sem("final_rows")
    s_held = sem("held")
    s_stored = [sem(f"out_stored{i}") for i in range(2)]
    chain_v, chain_a, chain_g = sem("vector_chain"), sem("scalar_chain"), sem("gpsimd_chain")

    def norm_cols(nz, k):
        if nz < 2:
            s0, s1 = ((0, 8), (24, 32))[nz]
            return mod[:, s1 + k:s1 + k + 1], mod[:, s0 + k:s0 + k + 1]
        v = {2: VG2, 4: VGP}[nz]
        return vec[:, v + k:v + k + 1], None

    SM_CA, SM_MLA = HD ** -0.5, QK ** -0.5
    UP_ORDER = (0, 2, 1, 3)

    class Chain:
        def __init__(self, eng, s):
            self.eng, self.s, self.n = eng, s, 0

        def __call__(self, ins):
            self.n += 1
            ins.then_inc(self.s, 1)
            self.eng.wait_ge(self.s, self.n)

    def full(eng, label):
        b, n, m = bank_of[label]
        eng.wait_ge((late_full if label in late else bank_full)[b], m)
        return bank[b]

    def taken(eng, label):
        b, n, m = bank_of[label]
        eng.wait_ge((late_taken if label in late else bank_taken)[b], n)

    def take(ins, label):
        ins.then_inc((late_taken if label in late else bank_taken)[bank_of[label][0]], 1)

    def win_dst(c, t):
        return lat[:, t, :] if c == 0 else (caq, cak, cav)[c - 1][:, t, :]

    def win2_dst(c, t):
        return (sbq, sbk, rq, rk, sbv, rv, rg)[c][:, t, :]

    def blk3(ap, n=4):
        return ap.rearrange("p (a b) -> p a b", a=n)

    def bc(ap, axis, shape):
        return ap.unsqueeze(axis).broadcast_to(shape)

    def row_bcast(ap1d, n, parts=P):
        return bass.AP(tensor=ap1d.tensor, offset=ap1d.offset, ap=[[0, parts], [1, n]])

    def slot_reg(eng, row, s, hi):
        return eng.value_load(slot_i[0:1, row, slot_at(s)],
                              min_val=0, max_val=hi)

    def up_half(c, gv):
        slot = arrives[("up", c)][0]
        return ring[slot][:, gv * KT * 2 * P:(gv + 1) * KT * 2 * P].rearrange("p (k n) -> p k n", k=KT)

    def half_in(eng, i, o):
        eng.wait_ge(stage_in[o % STAGES], 16 * (HALVES // STAGES) * i + 16 * (o // STAGES + 1))
        return stage[o % STAGES]

    def half_split(eng, i, o):
        r, c = o % HALVES, o // HALVES
        mine = [k for k in range(HALVES) if (k in BY_POOL) == (r in BY_POOL)]
        eng.wait_ge(s_lo_pool if r in BY_POOL else s_lo, len(mine) * i + (len(mine) * (c + 1) + mine.index(r) + 1))

    def half_used(eng, i, o):
        if o % 2 == 0:
            eng.wait_ge(s_first, CHUNKS_E * i + (CHUNKS_E + o // 2 + 1))
            return
        c, j = (o + 4) // HALVES, (o + 4) % HALVES // 2
        if j < 4:
            eng.wait_ge(bank_full[UP_ORDER[j]], i + (FU[UP_ORDER[j]] + c + 1))
        else:
            eng.wait_ge(bank_full[j], i + (FU[j] + c))

    def split_lo(eng, i, o, s_):
        eng.wait_ge(s_hi, HALVES * i + (o + 1))
        eng.tensor_tensor(w_lo[o % PAIRS][:, :], stage[o % STAGES][:, :], w_hi[o % PAIRS][:, :].bitcast(FP),
                          ALU.subtract).then_inc(s_, 1)

    def slot_at(i):
        return slice(i, i + 1) if isinstance(i, int) else bass.ds(i, 1)

    def n_slots(eng):
        return eng.value_load(nb_i[0:1, 0:1], min_val=NE, max_val=47)

    with nc.Block() as block:
        @block.sync
        def _(sp):
            v = g
            sp.dma_start(cona[:, :], v["consts"][:, packs["a"][0]:packs["a"][0] + packs["a"][1]]).then_inc(s_con, 16)
            packed = [("c", VC), ("g_attn_norm", VGA), ("g_mlp_norm", VGM), ("g_mix_norm_2", VG2), ("g_ffn_norm_2", VGF),
                      ("g_ple_norm_2", VGP), ("g_q_latent", VQL), ("g_kv_latent", VKL), ("conv_b", VCB)]
            for name, r0 in packed:
                n = v[name].shape[1] // P
                sp.dma_start(vrow[0][r0:r0 + n, :], v[name].rearrange("a (r p) -> (a r) p", p=P)).then_inc(s_vrow, 16)
            for name, r0 in (("g_ca_q", VCQ), ("g_ca_k", VCK), ("sb_q_gain_2", VSQ), ("sb_k_gain_2", VSK)):
                for half in range(2):
                    sp.dma_start(vrow[0][r0:r0 + 1, half * HD:(half + 1) * HD], v[name]).then_inc(s_vrow, 16)
            sp.dma_start(vrow[1][:, :], v["conv_w"][0, 0:2, :].rearrange("j (r p) -> (j r) p", p=P)).then_inc(s_vrow, 16)
            sp.dma_start(vrow[2][0:2 * FB, :], v["conv_w"][0, 2:3, :].rearrange("j (r p) -> (j r) p", p=P)).then_inc(s_vrow, 16)
            sp.dma_start(vrow[2][2 * FB:, :], v["b_ada"].rearrange("a (r p) -> (a r) p", p=P)).then_inc(s_vrow, 16)

            def used(i):
                if chunks[i][0][0] == "up":
                    sp.wait_ge(s_ulo, 2 * chunks[i][0][1] + 2)
                    return
                last = last_product(chunks[i][0])
                if isinstance(last, int):
                    sp.wait_ge(w_used, last)
                else:
                    full(sp, last)

            def load(i):
                label, parts = chunks[i]
                if before[i] is not None:
                    used(before[i])
                if place[i] == 3 and UP0 < i and place[i] not in place[UP0:i]:
                    full(sp, ("up", FB // 2 - 1, 1, 0))
                slot = place[i]
                for off, k, n, src in parts:
                    sp.dma_start(part(slot, off, k, n), src).then_inc(ring_in[slot], 16)

            for i in range(RING_D):
                load(i)
            for t in range(NT):
                sp.dma_start(x[:, t, :], v["x"][0, t * P:(t + 1) * P, :]).then_inc(s_x, 16)
            for i in range(RING_D, number[("wout", 0)]):
                load(i)
            full(sp, ("mT", 1, H - 1))
            for n, c in enumerate((2, 5)):
                src = v["b_ada"][0, c * D:(c + 1) * D]
                sp.dma_start(gbias[:, n, :], row_bcast(src, D)).then_inc(s_gb, 16)
            for i in range(number[("wout", 0)], number[("win2", 0)]):
                load(i)
            for i in range(number[("win2", 0)], number[("win2", 3)]):
                load(i)
            sp.wait_ge(s_xr, 3 * NT)
            sp.dma_start(conb[:, :], v["consts"][:, packs["b"][0]:packs["b"][0] + packs["b"][1]]).then_inc(s_conb, 16)
            for i in range(number[("win2", 3)], number[("wout2", 0)]):
                load(i)
            full(sp, ("S", 2, 4 * H - 1))
            sp.dma_start(gnrow[:, 0, :], row_bcast(v["ret_gn_gain_2"][0, :], CW)).then_inc(s_gn, 16)
            sp.dma_start(gnrow[:, 1, :], row_bcast(v["ret_gn_bias_2"][0, :], CW)).then_inc(s_gn, 16)
            for i in range(number[("wout2", 0)], ND):
                load(i)
            full(sp, ("oT", 3, NT - 1))
            sp.dma_start(grow_f[:, :], row_bcast(v["g_ffn_norm_2"][0, :], D)).then_inc(s_grf, 16)
            sp.dma_start(wrt[:, :, :], w["w_router_2"].rearrange("(k p) n -> p k n", p=P)).then_inc(s_wrt, 16)
            sp.dma_start(brt[:, :], row_bcast(v["b_router_2"][0, :], NE)).then_inc(s_wrt, 16)
            sp.dma_start(ptok[:, :, :], v["p_2"][0, 0].rearrange("(t p) n -> p t n", p=P)).then_inc(s_ptok, 16)
            sp.dma_start(conc[:, :], v["consts"][:, packs["c"][0]:packs["c"][0] + packs["c"][1]]).then_inc(s_conc, 16)
            sp.dma_start(bsum[:, 0:2 * D], v["b_up_gate_2"][0]).then_inc(s_bsum, 16)
            sp.dma_start(bsum[:, 2 * D:], v["b_down_2"][0]).then_inc(s_bsum, 16)

            def expert(i, o, e, down, c):
                k0 = o % 2 * (D // 2)
                if down:
                    src = v["w_down_2"][0, bass.ds(e, 1), k0:k0 + D // 2, c * CW:(c + 1) * CW]
                else:
                    src = v["w_up_gate_2"][0, bass.ds(e, 1), k0:k0 + D // 2, c * CW:(c + 1) * CW]
                src = src.rearrange("e (k p) n -> p (e k) n", p=P)
                place = stage[o % STAGES][:, :].rearrange("p (k n) -> p k n", k=KT // 2)
                if not isinstance(i, int) or o >= STAGES:
                    half_split(sp, i, o - STAGES)
                sp.dma_start(place, src).then_inc(stage_in[o % STAGES], 16)

            for o in range(8):
                if o % 2 == 0 and o < STAGES:
                    used(max(i for i in range(ND) if i % RING_D == 2 + o // 2))
                expert(0, o, 0, False, UP_ORDER[o // 2])
            sp.wait_ge(s_slots, 1)
            nb = n_slots(sp)
            with sp.Fori(1, nb) as i:
                e, d = slot_reg(sp, 0, i, NE - 1), slot_reg(sp, 0, i - 1, NE - 1)
                for j in range(HALVES):
                    expert(i, j - 4, e if j < 8 else d, j >= 8, UP_ORDER[j // 2] if j < 8 else j // 2 - 4)
            d = slot_reg(sp, 0, nb - 1, NE - 1)
            for j in range(4):
                expert(nb, j - 4, d, True, j // 2)
            for j in range(4):
                half_split(sp, nb, j - 4)
                src = cols(w["w_ple_gate_2"], j // 2 * CW, CW, j % 2 * (KT // 2), KT // 2)
                sp.dma_start(stage[j][:, :].rearrange("p (k n) -> p k n", k=KT // 2), src).then_inc(stage_in[j], 16)
            for t in range(NT):
                sp.wait_ge(s_out, t + 1)
                sp.dma_start(out[0, t * P:(t + 1) * P, :], xo[t % 2][:, :]).then_inc(s_stored[t % 2], 16)
            for parity in range(2):
                sp.wait_ge(s_stored[parity], 16 * NT // 2)

        @block.gpsimd
        def _(pool):
            link = Chain(pool, chain_g)
            v = g
            pool.nop().then_inc(s_lo_pool, len(BY_POOL))
            pool.dma_start(posi[:, 0, :].unsqueeze(2), v["positions"].rearrange("a (t p) -> p t a", p=P), allow_slow_non_contiguous=True).then_inc(s_pos, 16)
            pool.dma_start(posi[:, 1, :].unsqueeze(2), v["positions_2"].rearrange("a (t p) -> p t a", p=P), allow_slow_non_contiguous=True).then_inc(s_pos, 16)
            rb = v["rel_bias"]
            nrel = rb.shape[2]
            pool.dma_start(ext_d[:, 0:nrel], rb[0]).then_inc(s_ext, 16)
            last = bass.AP(tensor=rb.tensor, offset=rb.offset + nrel - 1, ap=[[nrel, H], [0, 3 * P - nrel], [1, 1]])
            pool.dma_start(ext_d[:, nrel:].unsqueeze(2), last, allow_slow_non_contiguous=True).then_inc(s_ext, 16)
            pool.wait_ge(s_ext, 32)
            window = bass.AP(tensor=ext_d.tensor, offset=ext_d.offset + 1, ap=[[1, P], [3 * P, H], [1, 2 * P]])
            pool.dma_start(biasr[:, :, :], window).then_inc(s_biasr, 16)
            far = bass.AP(tensor=rb.tensor, offset=rb.offset + nrel - 1, ap=[[0, P], [nrel, H], [1, 1]])
            pool.dma_start(farb[:, :].unsqueeze(2), far, allow_slow_non_contiguous=True).then_inc(s_far, 16)
            for j, name in enumerate(("g_mla_q", "g_mla_k")):
                pool.dma_start(grow1[:, j, :], row_bcast(v[name][0, :], QK)).then_inc(s_rows1, 16)
            for j, name in enumerate(("ret_q_gain_2", "ret_k_gain_2")):
                pool.dma_start(grow2[:, j, :], row_bcast(v[name][0, :], HD)).then_inc(s_rows1, 16)
            pool.wait_ge(s_zero, 1)
            pool.dma_start(hn_d[S:, :], zero[:, :]).then_inc(s_zd, 16)
            pool.dma_start(acc_d[S:, :], zero[:, :]).then_inc(s_scat, 16)
            for t in range(NT):
                pool.wait_ge(s_xr, 3 * NT + t + 1)
                pool.dma_start(acc_d[t * P:(t + 1) * P, :], x[:, t, :]).then_inc(s_acc, 16)
            for t in range(NT):
                pool.wait_ge(s_xn, 3 * NT + t + 1)
                pool.dma_start(hn_d[t * P:(t + 1) * P, :], xn[t % 2][:, :]).then_inc(s_hn[t % 2], 16)
            pool.wait_ge(s_zd, 16)
            pool.wait_ge(s_scat, 16)
            for parity in range(2):
                pool.wait_ge(s_hn[parity], 16 * NT // 2)
            pool.wait_ge(s_acc, 16 * NT)

            def gather():
                pool.indirect_dma_start(out=rows[:, :], out_offset=None, in_=hn_d[:, :],
                                        in_offset=bass.IndirectOffsetOnAxis(ap=idx_in[:, 0:1], axis=0)).then_inc(s_got, 16)

            def scatter():
                pool.indirect_dma_start(out=acc_d[:, :], out_offset=bass.IndirectOffsetOnAxis(ap=idx_out[:, 0:1], axis=0),
                                        in_=ey[:, :], in_offset=None, compute_op=ALU.add).then_inc(s_scat, 16)

            def output_stands(i):
                pool.wait_ge(bank_taken[4], TK[4] + 1 + i)
                pool.wait_ge(bank_taken[5], TK[5] + 1 + i)
                pool.wait_ge(s_ix, i + 1)
                pool.nop().then_inc(s_held, 1)

            split_lo(nc.gpsimd, 0, 4, s_lo_pool)
            for i in range(2):
                pool.wait_ge(s_idx, i + 1)
                gather()
            split_lo(nc.gpsimd, 0, 9, s_lo_pool)
            pool.wait_ge(s_slots, 1)
            nb = n_slots(pool)
            with pool.Fori(1, nb) as i:
                pool.wait_ge(s_idx, i + 2)
                pool.nop().then_inc(s_held, 1)
                gather()
                split_lo(nc.gpsimd, i, 4, s_lo_pool)
                split_lo(nc.gpsimd, i, 9, s_lo_pool)
                output_stands(i - 1)
                scatter()
            output_stands(nb - 1)
            scatter()
            pool.wait_ge(s_scat, nb * 16 + 16)
            pool.nop().then_inc(s_held, 1)
            for t in range(NT):
                pool.dma_start(x[:, t, :], acc_d[t * P:(t + 1) * P, :]).then_inc(s_back, 16)
            pool.wait_ge(s_back, 16 * NT)

        @block.scalar
        def _(act_e):
            link = Chain(act_e, chain_a)
            fn = nc.scalar.activation

            def copy_out(dst, label, src=None, scale=None):
                b = full(act_e, label)
                src = b[:, 0:dst.shape[-1]] if src is None else src(b)
                if scale is None:
                    take(fn(dst, src, ACT.Copy), label)
                else:
                    take(fn(dst, src, ACT.Copy, scale=scale), label)

            def norm(nz, between=None):
                for t in range(NT):
                    if nz == 0:
                        act_e.wait_ge(s_x, 16 * NT)
                    elif nz == 4:
                        act_e.wait_ge(s_back, 16 * NT)
                    else:
                        act_e.wait_ge(s_xr, nz * NT + t + 1)
                    k = nz * NT + t
                    link(fn(junk[:, :], x[:, t, :], ACT.Square, accum_out=stat[:, k:k + 1]))
                    fn(stat[:, 20 + k:21 + k], stat[:, k:k + 1], ACT.Sqrt, scale=1.0 / D, bias=eps[:, 0:1]).then_inc(s_sq, 1)
                for t in range(NT):
                    if between:
                        between(t)
                    label = ("xT", nz, t, 0)
                    b = full(act_e, label)
                    if nz == 3:
                        take(fn(hT[:, 0:4, t * P:(t + 1) * P], blk3(b[:, :]), ACT.Copy), label)
                        continue
                    for k in range(4):
                        a, sh = norm_cols(nz, k)
                        o, i = hT[:, k, t * P:(t + 1) * P], b[:, k * P:(k + 1) * P]
                        ins = fn(o, i, ACT.Identity, scale=a, bias=sh) if sh is not None else fn(o, i, ACT.Copy, scale=a)
                    take(ins, label)

            def roots(r):
                act_e.wait_ge(s_ms, r + 1)
                fn(hs[:, r * 32:r * 32 + 32], hs[:, r * 32:r * 32 + 32], ACT.Sqrt).then_inc(s_rt, 1)

            def attention(kind, PR, PT):
                base = {0: 0, 1: 1, 2: 0}[kind] * 4 * H
                for s in range(4 * H + OT_LAG[kind] + 1):
                    if s < 4 * H:
                        t, h = divmod(s, H)
                        n = (t + 1) * P
                        if kind < 2:
                            i = kind * 4 * H + s
                            if t >= 2 and h == 0:
                                act_e.wait_ge(s_o, kind * NT + t - 1)
                            act_e.wait_ge(s_max, i + 1)
                            c = soft[:, s % 8:s % 8 + 1]
                            total = soft[:, 16 + 8 * (t % 2) + h:17 + 8 * (t % 2) + h]
                            Pb = PR[s % 3]
                            if kind == 0:
                                fn(Pb[:, 0:n], Pb[:, 0:n], ACT.Exp, bias=c, accum_out=total).then_inc(s_P, 1)
                            else:
                                if s >= 3:
                                    full(act_e, ("T", 1, s - 3))
                                b = full(act_e, ("S", 1, s))
                                take(fn(Pb[:, 0:n], b[:, 0:n], ACT.Exp, bias=c, scale=SM_MLA, accum_out=total), ("S", 1, s))
                    if kind == 2 and s % 2 and s < 4 * H + 4:
                        new = (s - 1, s) if s < 4 * H else ()
                        for i in new:
                            n = (i // H + 1) * P
                            W1 = sbl[i % 4]
                            b = full(act_e, ("S", 2, i))
                            if i >= 4:
                                taken(act_e, ("S", 2, i - 4))
                            link(fn(W1[:, 0:n], b[:, 0:n], ACT.Abs))
                            link(fn(W1[:, 0:n], W1[:, 0:n], ACT.Exp, scale=-1.0))
                        for i in (s - 5, s - 4):
                            if i < 0:
                                continue
                            n = (i // H + 1) * P
                            act_e.wait_ge(s_arg, i + 1)
                            if i >= 4:
                                full(act_e, ("T", 2, i - 4))
                            fn(PR[i % 4][:, 0:n], sbw[i % 4][:, 0:n], ACT.Exp).then_inc(s_P, 1)
                        for i in new:
                            n = (i // H + 1) * P
                            W1 = sbl[i % 4]
                            fn(W1[:, 0:n], W1[:, 0:n], ACT.Ln, bias=one[:, 0:1]).then_inc(s_ln, 1)
                    i = s - 2
                    if kind < 2 and 0 <= i < 4 * H:
                        n = (i // H + 1) * P
                        b = full(act_e, ("T", kind, i))
                        if i >= 2:
                            act_e.wait_ge(s_pv, kind * 4 * H + i - 1)
                        take(fn(PT[i % 2][:, 0:i // H + 1, :], b[:, 0:n].rearrange("p (a b) -> p a b", b=P), ACT.Copy), ("T", kind, i))
                    if s >= H + OT_LAG[kind] and (s - OT_LAG[kind]) % H == 0:
                        t = (s - OT_LAG[kind]) // H - 1
                        out_T(kind, t)

            def out_T(kind, t):
                label = ("oT", kind, t)
                k0 = {0: 4, 1: 0, 2: 0, 3: 4}[kind]
                b = full(act_e, label)
                take(fn(hT[:, k0:k0 + 4, t * P:(t + 1) * P], blk3(b[:, :]), ACT.Copy), label)

            act_e.wait_ge(s_mset, 2)
            b = full(act_e, ("vecs",))
            link(fn(vec[:, 0:NV], b[:, 0:NV], ACT.Copy))
            link(fn(vec[:, VEC1:VEC1 + CWA], b[:, VEC1:VEC1 + CWA], ACT.Copy))
            take(fn(vec[:, VEC2:VEC2 + 2 * FB + 48], b[:, VEC2:VEC2 + 2 * FB + 48], ACT.Copy), ("vecs",))
            taken(act_e, ("vecs",))
            fn(cvec[:, :], vec[:, VC:VC + 8], ACT.Silu).then_inc(s_silu, 1)
            for j, (a, dst) in enumerate(zip(ang, (trig1, trig2))):
                act_e.wait_ge(s_ang, j + 1)
                fn(dst[:, :, :, :], a[:, :, :, :], ACT.Sin).then_inc(s_trig, 1)
            norm(0)
            for c in range(3):
                for t in range(NT):
                    copy_out(win_dst(c, t), ("win", c, t))
                if c == 0:
                    roots(0)
            for t in range(NT):
                label = ("latT", t)
                b = full(act_e, label)
                for j in range(3):
                    ins = fn(latT[:, j, t * P:(t + 1) * P], b[:, j * P:(j + 1) * P], ACT.Copy, scale=vec[:, VQL + j:VQL + j + 1])
                take(ins, label)
            for t in range(NT):
                copy_out(win_dst(3, t), ("win", 3, t))
                if t < 2:
                    roots(1 + t)
            for qk in range(2):
                for t in range(NT):
                    copy_out(caT[qk][:, :, t * P:(t + 1) * P], ("caT", qk, t), lambda b: blk3(b[:, :]), vec[:, VCQ + qk:VCQ + qk + 1])
            for t in range(NT):
                for n in range(2):
                    copy_out(mq[:, t, 4 * n:4 * n + 4, :], ("qup", t, n), lambda b: blk3(b[:, 0:4 * QK]))
            act_e.wait_ge(s_bias, 1)
            for t in range(NT):
                for n in range(2):
                    copy_out(kv[:, t, 4 * n:4 * n + 4, :], ("kvup", t, n), lambda b: blk3(b[:, :]))
            attention(0, PR1, PT1)
            for c in range(4, 12):
                dst = {4: gate_a, 5: gate_a, 10: gate_m, 11: gate_m}.get(c)
                if dst is not None:
                    copy_out(dst[:, c % 2 * CW:(c % 2 + 1) * CW], ("ada", c))
                else:
                    if c == 8 or c == 9:
                        full(act_e, ("adaT", c - 2))
                    copy_out(modrow2[c % 2][:, :], ("ada", c))
                if c in (5, 7):
                    roots(3 + (c - 5) // 2)
                if c - 1 in ADAT:
                    copy_out(mod[:, 4 * (c - 1):4 * c], ("adaT", c - 1), lambda b: blk3(b[:, :])[:, :, 0])
            for h in range(H):
                copy_out(mT[0][:, h, :], ("mT", 0, h), lambda b: b[0:QK, :])
            attention(1, PR1, PT1)
            norm(1)
            for t in range(NT):
                taken(act_e, ("xT", 1, t, 1))
                taken(act_e, ("xT", 1, t, 0))
                fn(hTs[0][:, :, t * P:(t + 1) * P], hT[:, :, t * P:(t + 1) * P], ACT.Copy).then_inc(s_thi, 1)

            def up_hi(c, gv):
                act_e.wait_ge(ring_in[arrives[("up", c)][0]], arrives[("up", c)][1])
                if c:
                    full(act_e, ("up", c - 1, 1, gv))
                elif gv == 0:
                    full(act_e, last_product(chunks[before_split][0]))
                else:
                    act_e.wait_ge(s_tlo, NT)
                fn(u_hi[gv][:, :, :], up_half(c, gv), ACT.Copy).then_inc(s_uhi, 1)

            up_hi(0, 0)
            up_hi(0, 1)
            for i in range(FB + 1):
                c, b2 = divmod(i, 2)
                if i < FB:
                    for gv, dst in ((0, cgate), (1, cval)):
                        label = ("up", c, b2, gv)
                        b = full(act_e, label)
                        j = gv * FB + i
                        if gv == 0 and i >= 2:
                            act_e.wait_ge(s_act, i - 1)
                        fn(dst[i % 2][:, :], b[:, :], ACT.Identity, scale=vec[:, VEC2 + j:VEC2 + j + 1],
                           bias=vec[:, VCB + j:VCB + j + 1]).then_inc(s_conv, 1)
                        if c < FB // 2 - 1 and b2 == gv:
                            up_hi(c + 1, gv)
                if i >= 1:
                    k = i - 1
                    act_e.wait_ge(s_taps, k + 1)
                    fn(cgs[k % 2][:, :], cgate[k % 2][:, :], ACT.Silu).then_inc(s_cg, 1)
            norm(2)
            for c in range(7):
                for t in range(NT):
                    copy_out(win2_dst(c, t), ("win2", c, t))
                if c in (1, 2):
                    roots(4 + c)
                if c == 3:
                    act_e.wait_ge(s_qs, 1)
                    for qk in range(2):
                        for t in range(NT):
                            copy_out(sbT[qk][:, :, t * P:(t + 1) * P], ("sbT", qk, t), lambda b: blk3(b[:, :]),
                                     qs[:, 0:1] if qk == 0 else vec[:, VSK:VSK + 1])
                if c in (4, 5):
                    roots(3 + c)
            for qk in range(2):
                for t in range(NT):
                    copy_out(rT[qk][:, :, t * P:(t + 1) * P], ("rT", qk, t), lambda b: blk3(b[:, :]))
            fn(rg[:, :, :], rg[:, :, :], ACT.Silu).then_inc(s_sg, 1)
            attention(2, PR2, PT2)
            for n in range(NT):
                roots(9 + n)
                if n:
                    out_T(3, n - 1)
            out_T(3, NT - 1)

            def embedding(t):
                for u in range(NT) if t == 0 else ():
                    label = ("pT", u)
                    b = full(act_e, label)
                    take(fn(pT[:, :, u * P:(u + 1) * P], blk3(b[:, 0:2 * P], 2), ACT.Copy), label)
                for n in range(2):
                    copy_out(pp[:, t, n * CW:(n + 1) * CW], ("ple", t, n))

            norm(3, embedding)
            def tiles_T(dst, k6, k7):
                for j, (b, k) in enumerate(((6, k6), (7, k7))):
                    act_e.wait_ge(bank_full[b], k)
                    fn(dst[0][:, 4 * j:4 * j + 4, :], blk3(bank[b][:, :]), ACT.Copy).then_inc(s_xhi, 1)

            def split_hi(i, *os):
                for o in os:
                    src = half_in(act_e, i, o)
                    if not isinstance(i, int) or o >= PAIRS:
                        half_used(act_e, i, o - PAIRS)
                    fn(w_hi[o % PAIRS][:, :], src[:, :], ACT.Copy).then_inc(s_hi, 1)

            def sigmoid(i, j):
                act_e.wait_ge(bank_taken[j], TK[j] + 1 + i)
                fn(ea[:, j * CW:(j + 1) * CW], eg[j][:, :], ACT.Sigmoid, scale=1.702).then_inc(s_sig, 1)

            def output(i, n, scattered=None):
                if n == 0:
                    act_e.wait_ge(s_scat, scattered)
                    act_e.wait_ge(s_gate, 2 * i + 2)
                act_e.wait_ge(bank_full[4 + n], FU[4 + n] + 1 + i)
                act_e.nop().then_inc(s_held, 1)
                fn(ey[:, n * CW:(n + 1) * CW], bank[4 + n][:, :], ACT.Copy,
                   scale=gates[:, bass.ds(i, 1)]).then_inc(bank_taken[4 + n], 1)

            full(act_e, last_product(chunks[max(i for i in range(ND) if i % RING_D == 0)][0]))
            full(act_e, last_product(chunks[max(i for i in range(ND) if i % RING_D == 1)][0]))
            act_e.wait_ge(s_b3, 1)
            act_e.wait_ge(s_acc, 16 * NT)
            split_hi(0, 0, 1, 2, 3)
            act_e.wait_ge(s_top, 1)
            fn(gate4[:, :, :], gate4[:, :, :], ACT.Exp).then_inc(s_ge, 1)
            full(act_e, ("router",))
            split_hi(0, 4, 5)
            tiles_T(xeT, FU[6] + 1, FU[7] + 2)
            split_hi(0, 6, 7)
            sigmoid(0, 0)
            split_hi(0, 8, 9, 10, 11)
            sigmoid(0, 1)
            split_hi(0, 12)
            tiles_T(xeT, FU[6] + 2, FU[7] + 4)
            act_e.wait_ge(s_slots, 1)
            nb = n_slots(act_e)
            with act_e.Fori(1, nb) as i:
                tiles_T(eaT, 2 * i + (FU[6] + 1), 3 * i + (FU[7] + 3))
                split_hi(i, 1, 2, 3)
                sigmoid(i, 0)
                split_hi(i, 4, 5, 6, 7)
                sigmoid(i, 1)
                split_hi(i, 8, 9)
                tiles_T(xeT, 2 * i + (FU[6] + 2), 3 * i + (FU[7] + 4))
                split_hi(i, 10)
                output(i - 1, 0, 16 * i)
                split_hi(i, 11, 12)
                output(i - 1, 1)
            tiles_T(eaT, 2 * nb + (FU[6] + 1), 3 * nb + (FU[7] + 2))
            output(nb - 1, 0, 16 * nb)
            output(nb - 1, 1)
            norm(4)
            for t in range(NT):
                for n in range(2):
                    label = ("gate", t, n)
                    b = full(act_e, label)
                    if t >= 2 and n == 0:
                        act_e.wait_ge(s_out, t - 1)
                    take(fn(fgate[t % 2][:, n * CW:(n + 1) * CW], b[:, :], ACT.Sigmoid), label)


        @block.tensor
        def _(pe):
            mm = nc.tensor.matmul

            def acquire(label):
                b, n, m = bank_of[label]
                if n > 1:
                    pe.wait_ge((late_taken if label in late else bank_taken)[b], n - 1)
                return bank[b]

            def publish(ins, label):
                ins.then_inc((late_full if label in late else bank_full)[bank_of[label][0]], 1)

            def arrived(label):
                slot, value = arrives[label]
                pe.wait_ge(ring_in[slot], value)
                return slot

            def tr(dst, src):
                return nc.tensor.transpose(dst, src, ident)

            def norm(nz, between=None):
                for t in range(NT):
                    if between:
                        between(t)
                    pe.wait_ge(s_xn, nz * NT + t + 1)
                    for j in range(2):
                        b = acquire(("xT", nz, t, j))
                        for k in range(4):
                            ins = tr(b[:, k * P:(k + 1) * P], xn[t % 2][:, (4 * j + k) * P:(4 * j + k + 1) * P])
                        publish(ins, ("xT", nz, t, j))

            def hT_stands(nz, t):
                taken(pe, ("xT", nz, t, 0))
                taken(pe, ("xT", nz, t, 1))

            def project(chunk_label, label, n, nz=None):
                slot = arrived(chunk_label)
                wv = part(slot, 0, KT, n)
                for t in range(NT):
                    if nz is not None:
                        hT_stands(nz, t)
                    b = acquire(label(t))
                    for k in range(KT):
                        ins = mm(b[:, 0:n], hT[:, k, t * P:(t + 1) * P], wv[:, k, :], start=k == 0, stop=k == KT - 1)
                    publish(ins, label(t))

            def ada(c):
                slot = arrived(("ada", c))
                wv = part(slot, 0, KT, CW)
                b = acquire(("ada", c))
                for k in range(KT):
                    ins = mm(b[:, :], srep[:, k, :] if c < 4 else srep2[:, k, :], wv[:, k, :], start=k == 0, stop=k == KT - 1)
                publish(ins, ("ada", c))

            def ada_T(c, rows_):
                taken(pe, ("ada", c))
                b = acquire(("adaT", c))
                for j in range(4):
                    ins = tr(b[:, j * P:(j + 1) * P], rows_[c % 2][:, j * P:(j + 1) * P])
                publish(ins, ("adaT", c))

            def pairs_T(name, qk, src):
                for t in range(NT):
                    b = acquire((name, qk, t))
                    for j in range(4):
                        ins = tr(b[:, j * P:(j + 1) * P], src[:, t, j * P:(j + 1) * P])
                    publish(ins, (name, qk, t))

            def out_T(kind, t, o):
                pe.wait_ge(s_o, kind * NT + t + 1)
                b = acquire(("oT", kind, t))
                for j in range(4):
                    ins = tr(b[:, j * P:(j + 1) * P], o[t % 2][:, 2 * j:2 * j + 2, :].rearrange("p a b -> p (a b)"))
                publish(ins, ("oT", kind, t))

            def attention(kind, q_of, k_of, v_of, PR, PT, o):
                for s in range(4 * H + OT_LAG[kind] + 1):
                    if s < 4 * H:
                        t, h = divmod(s, H)
                        n = (t + 1) * P
                        b = acquire(("S", kind, s))
                        publish(mm(b[:, 0:n], q_of(h, t), k_of(h, n), start=True, stop=True), ("S", kind, s))
                    i = s - LAG[kind]
                    if 0 <= i < 4 * H:
                        t = i // H
                        if kind == 1:
                            taken(pe, ("S", 1, i))
                        else:
                            pe.wait_ge(s_P, (0 if kind == 0 else 4 * H) + i + 1)
                        b = acquire(("T", kind, i))
                        for j in range(t + 1):
                            ins = tr(b[:, j * P:(j + 1) * P], PR[i % len(PR)][:, j * P:(j + 1) * P])
                        publish(ins, ("T", kind, i))
                    i -= 1
                    if 0 <= i < 4 * H:
                        t, h = divmod(i, H)
                        taken(pe, ("T", kind, i))
                        b = acquire(("O", kind, t)) if h == 0 else bank[bank_of[("O", kind, t)][0]]
                        for j in range(t + 1):
                            ins = mm(b[:, h * HD:(h + 1) * HD], PT[i % 2][:, j, :], v_of(h, j), start=j == 0, stop=j == t)
                        ins.then_inc(s_pv, 1)
                    if s >= H + OT_LAG[kind] and (s - OT_LAG[kind]) % H == 0:
                        out_T(kind, (s - OT_LAG[kind]) // H - 1, o)

            pe.nop().then_inc(s_first, CHUNKS_E)
            pe.wait_ge(s_con, 16)
            pe.wait_ge(s_vrow, 16 * N_VROW)
            b = acquire(("vecs",))
            nc.tensor.transpose(b[:, 0:NV], vrow[0][:, :], cona[0:NV, 0:NV])
            nc.tensor.transpose(b[:, VEC1:VEC1 + CWA], vrow[1][:, :], cona[0:CWA, 0:CWA])
            n = 2 * FB + 48
            publish(nc.tensor.transpose(b[:, VEC2:VEC2 + n], vrow[2][:, :], cona[0:n, 0:n]), ("vecs",))
            pe.wait_ge(s_srep, 1)
            for c in range(4):
                ada(c)
                if c:
                    ada_T(c - 1, modrow)
            ada_T(3, modrow)
            norm(0)
            for c in range(3):
                project(("win", c), lambda t: ("win", c, t), LAT if c == 0 else CW, 0 if c == 0 else None)
            pe.wait_ge(s_nrm, 1)
            for t in range(NT):
                b = acquire(("latT", t))
                for j in range(3):
                    ins = tr(b[:, j * P:(j + 1) * P], lat[:, t, j * P:(j + 1) * P])
                publish(ins, ("latT", t))
            project(("win", 3), lambda t: ("win", 3, t), CW)
            for qk, src in enumerate((caq, cak)):
                pe.wait_ge(s_nrm, 2 + qk)
                pairs_T("caT", qk, src)
            slot = arrived(("mlaup",))
            wq = part(slot, 0, 2, H * QK)
            wkv = ring[slot][:, 2 * H * QK:2 * H * QK + H * 2 * HD]
            for t in range(NT):
                taken(pe, ("latT", t))
                for n in range(2):
                    b = acquire(("qup", t, n))
                    for k in range(2):
                        ins = mm(b[:, 0:4 * QK], latT[:, k, t * P:(t + 1) * P], wq[:, k, n * 4 * QK:(n + 1) * 4 * QK], start=k == 0, stop=k == 1)
                    publish(ins, ("qup", t, n))
            for t in range(NT):
                for n in range(2):
                    b = acquire(("kvup", t, n))
                    publish(mm(b[:, :], latT[:, 2, t * P:(t + 1) * P], wkv[:, n * CW:(n + 1) * CW], start=True, stop=True), ("kvup", t, n))
            for qk in range(2):
                for t in range(NT):
                    taken(pe, ("caT", qk, t))

            def half(a, h, c0, n):
                return a[h % 2 * HD:(h % 2 + 1) * HD, h // 2, c0:c0 + n]

            attention(0, lambda h, t: half(caT[0], h, t * P, P), lambda h, n: half(caT[1], h, 0, n),
                      lambda h, j: cav[:, j, h * HD:(h + 1) * HD], PR1, PT1, o1)
            pe.wait_ge(s_srep, 2)
            for c in range(4, 12):
                ada(c)
                if c - 1 in ADAT:
                    ada_T(c - 1, modrow2)
            for qk, src in enumerate((mq, mk)):
                pe.wait_ge(s_nrm, 4 + qk)
                for h in range(H):
                    b = acquire(("mT", qk, h))
                    for t in range(NT):
                        ins = tr(b[0:QK, t * P:(t + 1) * P], src[:, t, h, :])
                    publish(ins, ("mT", qk, h))
            for qk in range(2):
                for h in range(H):
                    taken(pe, ("mT", qk, h))
            attention(1, lambda h, t: mT[0][:, h, t * P:(t + 1) * P], lambda h, n: mT[1][:, h, 0:n],
                      lambda h, j: kv[:, j, h, HD:], PR1, PT1, o1)
            for kind in (0, 1):
                for t in range(NT):
                    taken(pe, ("oT", kind, t))
            for n in range(2):
                project(("wout", n), lambda t: ("wout", n, t), CW)
            norm(1)
            pe.wait_ge(s_tlo, NT)
            for c in range(FB // 2):
                for gv in range(2):
                    pe.wait_ge(s_ulo, 2 * c + gv + 1)
                    for b2 in range(2):
                        b = acquire(("up", c, b2, gv))
                        for k in range(KT):
                            wh, wl = (a[gv][:, k, b2 * P:(b2 + 1) * P] for a in (u_hi, u_lo))
                            mm(b[:, :], wh, hTs[0][:, k, :], start=k == 0, stop=False)
                            mm(b[:, :], wh, hTs[1][:, k, :], start=False, stop=False)
                            ins = mm(b[:, :], wl, hTs[0][:, k, :], start=False, stop=k == KT - 1)
                        publish(ins, ("up", c, b2, gv))
            pe.wait_ge(s_act, FB)
            for n in range(2):
                for j, (k0, kn) in enumerate(DK):
                    slot = arrived(("down", n, j))
                    wv = part(slot, 0, kn, CW)
                    for t in range(NT):
                        b = acquire(("down", n, t)) if j == 0 else bank[bank_of[("down", n, t)][0]]
                        for k in range(kn):
                            ins = mm(b[:, :], act[:, k0 + k, t * P:(t + 1) * P], wv[:, k, :], start=k0 + k == 0, stop=k0 + k == FB - 1)
                        if j == 2:
                            publish(ins, ("down", n, t))
                    if j < 2:
                        ins.then_inc(w_used, 1)
            norm(2)
            for c in range(7):
                project(("win2", c), lambda t: ("win2", c, t), CW, 2 if c == 0 else None)
                if c == 3:
                    for qk, src in enumerate((sbq, sbk)):
                        pe.wait_ge(s_nrm, 6 + qk)
                        pairs_T("sbT", qk, src)
            for qk, src in enumerate((rq, rk)):
                pe.wait_ge(s_nrm, 8 + qk)
                pairs_T("rT", qk, src)
            for qk in range(2):
                for t in range(NT):
                    taken(pe, ("sbT", qk, t))
            attention(2, lambda h, t: half(sbT[0], h, t * P, P), lambda h, n: half(sbT[1], h, 0, n),
                      lambda h, j: sbv[:, j, h * HD:(h + 1) * HD], PR2, PT2, o2)
            pe.wait_ge(s_kd, 1)
            pe.wait_ge(s_rqd, NT)
            for n in range(NT):
                c0 = n * P
                for j in range(2):
                    b = acquire(("rS", n, j))
                    for h in range(j, H, 2):
                        ins = mm(b[:, h // 2 * P:(h // 2 + 1) * P], half(rT[1], h, c0, P), half(rT[0], h, c0, P), start=True, stop=True)
                    publish(ins, ("rS", n, j))
                b = acquire(("rO", n))
                for j in range(2):
                    taken(pe, ("rS", n, j))
                if n:
                    pe.wait_ge(s_st, n)
                for pair in range(H // 2):
                    if n:
                        mm(b[:, pair * P:(pair + 1) * P], rqdT[:, pair, c0:c0 + P], state[:, pair, :], start=True, stop=False,
                           skip_group_check=True)
                    for h in (2 * pair, 2 * pair + 1):
                        ins = mm(b[:, h * HD:(h + 1) * HD], rS[:, h, :], rv[:, n, h * HD:(h + 1) * HD], start=n == 0, stop=True,
                                 skip_group_check=True)
                publish(ins, ("rO", n))
                if n < NT - 1:
                    b = acquire(("rkv", n))
                    for j in range(4):
                        ins = mm(b[:, j * P:(j + 1) * P], rk[:, n, j * P:(j + 1) * P], rv[:, n, j * P:(j + 1) * P], start=True, stop=True)
                    publish(ins, ("rkv", n))
                if n:
                    out_T(3, n - 1, o2)
            out_T(3, NT - 1, o2)
            for kind in (2, 3):
                for t in range(NT):
                    taken(pe, ("oT", kind, t))
            for n in range(2):
                project(("wout2", n), lambda t: ("wout2", n, t), CW)
            slot = arrived(("ple",))
            w_ple = part(slot, 0, 2, D)

            def embedding(t):
                taken(pe, ("pT", t))
                for n in range(2):
                    b = acquire(("ple", t, n))
                    for k in range(2):
                        ins = mm(b[:, :], pT[:, k, t * P:(t + 1) * P], w_ple[:, k, n * CW:(n + 1) * CW], start=k == 0, stop=k == 1)
                    publish(ins, ("ple", t, n))

            pe.wait_ge(s_ptok, 16)
            for t in range(NT):
                b = acquire(("pT", t))
                for j in range(2):
                    ins = tr(b[:, j * P:(j + 1) * P], ptok[:, t, j * P:(j + 1) * P])
                publish(ins, ("pT", t))
            norm(3, embedding)
            pe.wait_ge(s_wrt, 32)
            b = acquire(("router",))
            for t in range(NT):
                hT_stands(3, t)
                for k in range(KT):
                    ins = mm(b[:, t * NE:(t + 1) * NE], hT[:, k, t * P:(t + 1) * P], wrt[:, k, :], start=k == 0, stop=k == KT - 1)
            publish(ins, ("router",))
            pe.wait_ge(s_conc, 16)
            pe.wait_ge(s_route, 1)
            b = acquire(("rank",))
            for t in range(NT + 1):
                for j in range(min(t + 1, NT)):
                    ins = mm(b[:, t * NE:(t + 1) * NE], cc("tri") if j == t else ones[:, :], chosen[:, j, :], start=j == 0, stop=j == min(t, NT - 1))
            publish(ins, ("rank",))

            def find(i, k7):
                pe.wait_ge(bank_taken[7], k7)
                pe.wait_ge(s_pick, i + 1)
                for t in range(NT):
                    ins = mm(bank[7][:, 0:2 + NE], pick[:, t, :], route[:, t, :], start=t == 0, stop=t == NT - 1)
                ins.then_inc(bank_full[7], 1)

            def turn(src, k6, k7):
                for b, k, j in ((6, k6, 0), (7, k7, 1)):
                    pe.wait_ge(bank_taken[b], k)
                    for m in range(4):
                        ins = tr(bank[b][:, m * P:(m + 1) * P], src[:, (4 * j + m) * P:(4 * j + m + 1) * P])
                    ins.then_inc(bank_full[b], 1)

            def fill(b, lhs, hot_, bcol, i, o):
                hi, lo = lhs
                mm(bank[b][:, :], hot_[:, :], bias3[:, bcol:bcol + CW], start=True, stop=False)
                for half_ in (o, o + 1):
                    half_split(pe, i, half_)
                    wh, wl = (a[half_ % PAIRS][:, :].rearrange("p (k n) -> p k n", k=KT // 2) for a in (w_hi, w_lo))
                    for k in range(KT // 2):
                        kk = half_ % 2 * (KT // 2) + k
                        mm(bank[b][:, :], hi[:, kk, :], wh[:, k, :], start=False, stop=False)
                        mm(bank[b][:, :], hi[:, kk, :], wl[:, k, :], start=False, stop=False)
                        ins = mm(bank[b][:, :], lo[:, kk, :], wh[:, k, :], start=False, stop=kk == KT - 1)
                    ins.then_inc(s_first if half_ == o else bank_full[b], 1)

            def up(i, o):
                pe.wait_ge(bank_taken[7], xe_taken(i)[1])
                pe.wait_ge(bank_taken[6], xe_taken(i)[0])
                pe.wait_ge(s_hotu, i + 1)
                for j, c in enumerate(UP_ORDER):
                    pe.wait_ge(bank_taken[c], TK[c] + i)
                    fill(c, xeT, hot[0], c * CW, i, o + 2 * j)

            def down(i, at_, o, k6, k7):
                pe.wait_ge(bank_taken[6], k6)
                pe.wait_ge(bank_taken[7], k7)
                pe.wait_ge(s_hotd, i + 1)
                for n in range(2):
                    pe.wait_ge(bank_taken[4 + n], TK[4 + n] + i)
                    fill(4 + n, eaT, hot[1], 2 * D + n * CW, at_, o + 2 * n)

            def xe_taken(i):
                return 2 * i + (TK[6] + (1 if isinstance(i, int) and i == 0 else 0)), 3 * i + (TK[7] + (2 if isinstance(i, int) and i == 0 else 1))

            find(0, TK[7])
            pe.wait_ge(s_got, 16)
            turn(rows, TK[6], TK[7] + 1)
            find(1, TK[7] + 2)
            up(0, 0)
            pe.wait_ge(s_got, 32)
            turn(rows, TK[6] + 1, TK[7] + 3)
            pe.wait_ge(s_slots, 1)
            nb = n_slots(pe)
            with pe.Fori(1, nb) as i:
                find(i + 1, 3 * i + (TK[7] + 1))
                pe.wait_ge(s_ea, 2 * i)
                turn(ea, 2 * i + TK[6], 3 * i + (TK[7] + 2))
                up(i, -4)
                pe.wait_ge(s_got, 16 * i + 32)
                turn(rows, 2 * i + (TK[6] + 1), 3 * i + (TK[7] + 3))
                down(i - 1, i, 4, 2 * i + (TK[6] + 1), 3 * i + (TK[7] + 3))
            pe.wait_ge(s_ea, 2 * nb)
            turn(ea, 2 * nb + TK[6], 3 * nb + (TK[7] + 1))
            down(nb - 1, nb, -4, 2 * nb + (TK[6] + 1), 3 * nb + (TK[7] + 2))
            norm(4)
            for j in range(4):
                half_in(pe, nb, j)
            for t in range(NT):
                hT_stands(4, t)
                for n in range(2):
                    b = acquire(("gate", t, n))
                    for k in range(KT):
                        wv = stage[2 * n + k // 4][:, k % 4 * CW:(k % 4 + 1) * CW]
                        ins = mm(b[:, :], hT[:, k, t * P:(t + 1) * P], wv, start=k == 0, stop=k == KT - 1)
                    publish(ins, ("gate", t, n))

        @block.vector
        def _(dve):
            link = Chain(dve, chain_v)
            ve = nc.vector
            dve.nop().then_inc(s_lo, HALVES - len(BY_POOL))
            tt, ts, stt = ve.tensor_tensor, ve.tensor_scalar, ve.scalar_tensor_tensor

            def norm(nz):
                def back(t):
                    label = ("xT", nz, t, 1)
                    b = full(dve, label)
                    if nz == 3:
                        take(ve.tensor_copy(hT[:, 4:8, t * P:(t + 1) * P], blk3(b[:, :])), label)
                        return
                    for k in range(4):
                        a, sh = norm_cols(nz, 4 + k)
                        ins = ts(hT[:, 4 + k, t * P:(t + 1) * P], b[:, k * P:(k + 1) * P], a, sh, ALU.mult,
                                 ALU.add if sh is not None else ALU.bypass)
                    take(ins, label)

                for t in range(NT):
                    k = nz * NT + t
                    dve.wait_ge(s_sq, k + 1)
                    link(ve.reciprocal(stat[:, 40 + k:41 + k], stat[:, 20 + k:21 + k]))
                    if t >= 2:
                        full(dve, ("xT", nz, t - 2, 1))
                        if nz == 3:
                            dve.wait_ge(s_hn[t % 2], 16 * (t // 2))
                    if nz == 3:
                        link(ts(xn[t % 2][:, :], x[:, t, :], stat[:, 40 + k:41 + k], None, ALU.mult))
                        tt(xn[t % 2][:, :], xn[t % 2][:, :], grow_f[:, :], ALU.mult).then_inc(s_xn, 1)
                    else:
                        ts(xn[t % 2][:, :], x[:, t, :], stat[:, 40 + k:41 + k], None, ALU.mult).then_inc(s_xn, 1)
                    if t:
                        back(t - 1)
                back(NT - 1)

            def mean_square(src, n, d, dst, scratch):
                link(tt(scratch, src, src, ALU.mult))
                link(ve.reduce_sum(dst, scratch, axis=AX))
                return ts(dst, dst, 1.0 / d, EPS, ALU.mult, ALU.add)

            def heads(r, src, scratch, after=None, scale=None):
                st = hs[:, r * 32:r * 32 + 32]
                a = src[:, :, :].rearrange("p t (h d) -> p (t h) d", d=HD)
                mean_square(a, 32, HD, st, scratch[:, :].rearrange("p (n d) -> p n d", d=HD)).then_inc(s_ms, 1)
                dve.wait_ge(s_rt, r + 1)
                link(ve.reciprocal(st, st))
                if scale is not None:
                    link(ts(st, st, scale, None, ALU.mult))
                return tt(a, a, bc(st, 2, [P, 32, HD]), ALU.mult)

            def rope(x1, x2, trig, j, scratch, shape):
                cos = bc(trig[:, j, 0, :], 1, shape)
                sin = bc(trig[:, j, 1, :], 1, shape)
                n = shape[1] * shape[2]
                a, b, c = (scratch[:, i * n:(i + 1) * n].rearrange("p (h d) -> p h d", h=shape[1]) for i in range(3))
                link(tt(a, x2, sin, ALU.mult))
                link(tt(b, x2, cos, ALU.mult))
                link(tt(c, x1, sin, ALU.mult))
                link(tt(x1, x1, cos, ALU.mult))
                link(tt(x1, x1, a, ALU.subtract))
                return tt(x2, b, c, ALU.add)

            def stick(s):
                t = s // H
                n = (t + 1) * P
                W1, W2 = sbl[s % 4], sbw[s % 4]
                d0 = t * P
                dve.wait_ge(s_ln, s + 1)
                if s >= 4:
                    dve.wait_ge(s_P, 4 * H + s - 3)
                b = full(dve, ("S", 2, s))
                link(stt(W2[:, 0:n], b[:, 0:n], 0.0, W1[:, 0:n], ALU.max, ALU.add))
                link(tt(W2[:, d0:n], W2[:, d0:n], cb("strict"), ALU.mult))
                link(ve.tensor_tensor_scan(W1[:, 0:n][:, ::-1], one[:, 0:1].broadcast_to([P, n]), W2[:, 0:n][:, ::-1], 0.0, ALU.mult, ALU.add))
                take(tt(W2[:, 0:n], b[:, 0:n], W1[:, 0:n], ALU.subtract), ("S", 2, s))
                taken(dve, ("S", 2, s))
                tt(W2[:, d0:n], W2[:, d0:n], cb("negm"), ALU.add).then_inc(s_arg, 1)

            def attention(kind, PR, PT, o):
                for s in range(4 * H + OT_LAG[kind] + 1):
                    if s < 4 * H:
                        t, h = divmod(s, H)
                        n = (t + 1) * P
                        c = soft[:, s % 8:s % 8 + 1]
                        if kind == 0:
                            L = PR[s % 3]
                            if s >= 3:
                                full(dve, ("T", 0, s - 3))
                            b = full(dve, ("S", 0, s))
                            lo = max(t - 1, 0) * P
                            if lo:
                                ts(L[:, 0:lo], b[:, 0:lo], SM_CA, farb[:, h:h + 1], ALU.mult, ALU.add)
                            take(stt(L[:, lo:n], b[:, lo:n], SM_CA, bias[:, h, (0 if t else P):2 * P], ALU.mult, ALU.add), ("S", 0, s))
                            taken(dve, ("S", 0, s))
                            ve.tensor_reduce(c, L[:, 0:n], AX, ALU.max, negate=True).then_inc(s_max, 1)
                        elif kind == 1:
                            b = full(dve, ("S", 1, s))
                            link(ve.memset(b[0:HD, n - HD:n], NEG))
                            link(ve.tensor_reduce(c, b[:, 0:n], AX, ALU.max, negate=True))
                            ts(c, c, SM_MLA, None, ALU.mult).then_inc(s_max, 1)
                    i = s - LAG[kind]
                    if kind == 2 and 0 <= i < 4 * H:
                        b = full(dve, ("T", 2, i))
                        if i >= 2:
                            dve.wait_ge(s_pv, 8 * H + i - 1)
                        take(ve.tensor_copy(PT[i % 2][:, 0:i // H + 1, :], b[:, 0:(i // H + 1) * P].rearrange("p (a b) -> p a b", b=P)), ("T", 2, i))
                    if kind == 2 and 0 <= s - 2 < 4 * H:
                        stick(s - 2)
                    i -= 1
                    if 0 <= i < 4 * H and i % H == H - 1:
                        t = i // H
                        label = ("O", kind, t)
                        b = bank[bank_of[label][0]]
                        dve.wait_ge(s_pv, kind * 4 * H + i + 1)
                        if t >= 2:
                            full(dve, ("oT", kind, t - 2))
                        src = b[:, :].rearrange("p (h d) -> p h d", h=H)
                        if kind == 2:
                            take(ve.tensor_copy(o[t % 2][:, :, :], src), label)
                        else:
                            link(ve.reciprocal(den[:, :], soft[:, 16 + 8 * (t % 2):24 + 8 * (t % 2)]))
                            take(tt(o[t % 2][:, :, :], src, bc(den[:, :], 2, [P, H, HD]), ALU.mult), label)
                        taken(dve, label)
                        dve.nop().then_inc(s_o, 1)

            ve.memset(eps[:, :], EPS).then_inc(s_mset, 1)
            ve.memset(one[:, :], 1.0).then_inc(s_mset, 1)
            dve.wait_ge(s_con, 16)
            dve.wait_ge(s_pos, 32)
            link(ve.tensor_copy(posf[:, :, :], posi[:, :, :]))
            two_pi = 2 * np.pi
            c1 = 6.28125
            c2 = np.floor((two_pi - c1) * 2 ** 22) / 2 ** 22
            c3 = two_pi - c1 - c2
            for j, (a, inv, hw) in enumerate(((ang[0], inv1, ROPE // 2), (ang[1], inv2, HD // 2))):
                kk = angk[:, :, :, 0:hw]
                for m in range(2):
                    link(tt(a[:, :, m, :], bc(posf[:, j, :], 2, [P, NT, hw]), bc(inv, 1, [P, NT, hw]), ALU.mult))
                for m, turn in ((0, 0.25), (1, 0.0)):
                    link(ts(kk[:, :, m, :], a[:, :, m, :], 1.0 / two_pi, turn, ALU.mult, ALU.add))
                link(ts(kk, kk, 12582912.0, None, ALU.add))
                link(ts(kk, kk, -12582912.0, None, ALU.add))
                for m in range(2):
                    for cc_ in (c1, c2, c3):
                        link(stt(a[:, :, m, :], kk[:, :, m, :], -float(cc_), a[:, :, m, :], ALU.mult, ALU.add))
                link(ts(a[:, :, 0, :], a[:, :, 0, :], float(np.pi / 2), None, ALU.add))
                ts(a[:, :, :, :], a[:, :, :, :], 3.1415925, -3.1415925, ALU.min, ALU.max).then_inc(s_ang, 1)
            dve.wait_ge(s_silu, 1)
            ve.tensor_copy(srep[:, :, :], bc(cvec[:, :], 2, [P, KT, P])).then_inc(s_srep, 1)
            ts(qs[:, :], vec[:, VSQ:VSQ + 1], HD ** -0.5, None, ALU.mult).then_inc(s_qs, 1)

            def ada_row(c):
                b = full(dve, ("ada", c))
                if c >= 2:
                    full(dve, ("adaT", c - 2))
                take(ve.tensor_copy(modrow[c % 2][:, :], b[:, :]), ("ada", c))

            def ada_col(c):
                b = full(dve, ("adaT", c))
                take(tt(mod[:, 4 * c:4 * c + 4], blk3(b[:, :])[:, :, 0], vec[:, VBA + 4 * c:VBA + 4 * c + 4], ALU.add), ("adaT", c))

            for c in range(4):
                ada_row(c)
                if c:
                    ada_col(c - 1)
            ada_col(3)
            for c in range(4):
                taken(dve, ("adaT", c))
            stt(mod[:, 8:16], mod[:, 8:16], 1.0, vec[:, VGA:VGA + 8], ALU.add, ALU.mult).then_inc(s_mod, 1)
            norm(0)
            dve.wait_ge(s_biasr, 16)
            for h in range(H):
                link(ve.tensor_copy(bias[:, h, :], biasr[:, h, :][:, ::-1]))
            ve.memset(bias[0:HD, :, 2 * P - HD:], NEG).then_inc(s_bias, 1)
            for t in range(NT):
                taken(dve, ("win", 0, t))
            for j, (c0, n) in enumerate(((0, QR), (QR, KVR))):
                ins = mean_square(lat[:, :, c0:c0 + n], NT, n, hs[:, 4 * j:4 * j + 4], tmp[:, 0:NT * n].rearrange("p (t n) -> p t n", t=NT))
                if j == 0:
                    link(ins)
            link(ins)
            link(ve.tensor_copy(hs[:, 8:32], hs[:, 0:1].broadcast_to([P, 24])))
            link(ve.tensor_copy(krope[:, :, :], lat[:, :, QR + KVR:]))
            dve.nop().then_inc(s_ms, 1)
            dve.wait_ge(s_rt, 1)
            link(ve.reciprocal(hs[:, 0:8], hs[:, 0:8]))
            link(tt(lat[:, :, 0:QR], lat[:, :, 0:QR], bc(hs[:, 0:4], 2, [P, NT, QR]), ALU.mult))
            tt(lat[:, :, QR:QR + KVR], lat[:, :, QR:QR + KVR], bc(hs[:, 4:8], 2, [P, NT, KVR]), ALU.mult).then_inc(s_nrm, 1)
            for j, a in enumerate((caq, cak)):
                for t in range(NT):
                    taken(dve, ("win", 1 + j, t))
                heads(1 + j, a, tmp).then_inc(s_nrm, 1)
            dve.wait_ge(s_far, 16)
            attention(0, PR1, PT1, o1)
            full(dve, ("S", 0, 4 * H - 1))
            ve.tensor_copy(srep2[:, :, :], bc(cvec[:, :], 2, [P, KT, P])).then_inc(s_srep, 1)
            dve.wait_ge(s_rows1, 64)
            dve.wait_ge(s_trig, 2)
            for j, a in enumerate((mq, mk)):
                for t in range(NT):
                    if j == 0:
                        taken(dve, ("qup", t, 0))
                        taken(dve, ("qup", t, 1))
                    else:
                        taken(dve, ("kvup", t, 0))
                        taken(dve, ("kvup", t, 1))
                        link(ve.tensor_copy(mk[:, t, :, 0:NOPE], kv[:, t, :, 0:NOPE]))
                        link(ve.tensor_copy(mk[:, t, :, NOPE:], bc(krope[:, t, :], 1, [P, H, ROPE])))
                    link(mean_square(a[:, t, :, :], H, QK, hs[:, (3 + j) * 32 + t * H:(3 + j) * 32 + (t + 1) * H], tmpm[:, :, :]))
                dve.nop().then_inc(s_ms, 1)
                dve.wait_ge(s_rt, 4 + j)
                st = hs[:, (3 + j) * 32:(4 + j) * 32]
                link(ve.reciprocal(st, st))
                flat = a[:, :, :, :].rearrange("p t h d -> p (t h) d")
                link(tt(flat, flat, bc(st, 2, [P, 32, QK]), ALU.mult))
                link(tt(flat, flat, bc(grow1[:, j, :], 1, [P, 32, QK]), ALU.mult))
                for t in range(NT):
                    hw = ROPE // 2
                    ins = rope(a[:, t, :, NOPE:NOPE + hw], a[:, t, :, NOPE + hw:], trig1, t,
                               tmpm[:, :, :].rearrange("p h d -> p (h d)"), [P, H, hw])
                    if t < NT - 1:
                        link(ins)
                ins.then_inc(s_nrm, 1)
                dve.wait_ge(s_nrm, 4 + j)
            for h in range(H):
                label = ("mT", 1, h)
                b = full(dve, label)
                take(ve.tensor_copy(mT[1][:, h, :], b[0:QK, :]), label)
            attention(1, PR1, PT1, o1)
            dve.wait_ge(s_gb, 32)
            for c in (4, 5, 10, 11):
                taken(dve, ("ada", c))
            link(tt(gate_a[:, :], gate_a[:, :], gbias[:, 0, :], ALU.add))
            link(tt(gate_m[:, :], gate_m[:, :], gbias[:, 1, :], ALU.add))
            for c in ADAT:
                taken(dve, ("adaT", c))
            link(tt(mod[:, 24:40], mod[:, 24:40], vec[:, VBA + 24:VBA + 40], ALU.add))
            stt(mod[:, 32:40], mod[:, 32:40], 1.0, vec[:, VGM:VGM + 8], ALU.add, ALU.mult).then_inc(s_mod, 1)

            def residual(name, gate):
                for n in range(2):
                    for t in range(NT):
                        label = (name, n, t)
                        b = full(dve, label)
                        xs = x[:, t, n * CW:(n + 1) * CW]
                        if gate is None:
                            take(tt(xs, b[:, :], xs, ALU.add), label)
                            taken(dve, label)
                            if n:
                                dve.nop().then_inc(s_xr, 1)
                            continue
                        take(tt(tmpx[:, :], b[:, :], gate[:, n * CW:(n + 1) * CW], ALU.mult), label)
                        taken(dve, label)
                        ins = tt(xs, xs, tmpx[:, :], ALU.add)
                        if n:
                            ins.then_inc(s_xr, 1)
                            dve.wait_ge(s_xr, {"wout": NT, "down": 2 * NT}[name] + t + 1)
                        else:
                            link(ins)

            dve.nop().then_inc(s_xr, NT)
            residual("wout", gate_a)
            norm(1)
            def up_lo(c, gv):
                dve.wait_ge(s_uhi, 2 * c + gv + 1)
                tt(u_lo[gv][:, :, :], up_half(c, gv), u_hi[gv][:, :, :].bitcast(FP), ALU.subtract).then_inc(s_ulo, 1)

            full(dve, ("xT", 1, NT - 1, 1))
            for t in range(NT):
                dve.wait_ge(s_thi, t + 1)
                cols_t = slice(t * P, (t + 1) * P)
                tt(hTs[1][:, :, cols_t], hT[:, :, cols_t], hTs[0][:, :, cols_t].bitcast(FP), ALU.subtract).then_inc(s_tlo, 1)
            up_lo(0, 0)
            up_lo(0, 1)
            for i in range(FB + 1):
                c, b2 = divmod(i, 2)
                if i < FB:
                    for gv, dst in ((0, cgate), (1, cval)):
                        label = ("up", c, b2, gv)
                        b = full(dve, label)
                        dve.wait_ge(s_conv, 2 * i + gv + 1)
                        d = dst[i % 2]
                        j = gv * FB + i
                        link(stt(d[:, 1:], b[:, 0:S - 1], vec[:, VEC1 + 2 * FB + j:VEC1 + 2 * FB + j + 1], d[:, 1:], ALU.mult, ALU.add))
                        take(stt(d[:, 2:], b[:, 0:S - 2], vec[:, VEC1 + j:VEC1 + j + 1], d[:, 2:], ALU.mult, ALU.add), label)
                        if c < FB // 2 - 1 and b2 == gv:
                            up_lo(c + 1, gv)
                    taken(dve, ("up", c, b2, 0))
                    taken(dve, ("up", c, b2, 1))
                    dve.nop().then_inc(s_taps, 1)
                if i:
                    k = i - 1
                    dve.wait_ge(s_cg, k + 1)
                    tt(act[:, k, :], cgs[k % 2][:, :], cval[k % 2][:, :], ALU.mult).then_inc(s_act, 1)
            residual("down", gate_m)
            norm(2)
            dve.wait_ge(s_conb, 16)
            for j, (a, c) in enumerate(((sbq, 0), (sbk, 1))):
                for t in range(NT):
                    taken(dve, ("win2", c, t))
                heads(5 + j, a, tmpr).then_inc(s_nrm, 1)
                dve.wait_ge(s_nrm, 6 + j)
            for j, (a, c) in enumerate(((rq, 2), (rk, 3))):
                for t in range(NT):
                    taken(dve, ("win2", c, t))
                link(heads(7 + j, a, tmpr, scale=None if j == 0 else HD ** -0.5))
                flat = a[:, :, :].rearrange("p t (h d) -> p (t h) d", d=HD)
                link(tt(flat, flat, bc(grow2[:, j, :], 1, [P, 32, HD]), ALU.mult))
                for t in range(NT):
                    hw = HD // 2
                    a4 = a[:, t, :].rearrange("p (h d) -> p h d", h=H)
                    ins = rope(a4[:, :, 0:hw], a4[:, :, hw:], trig2, t, tmpr, [P, H, hw])
                    if t < NT - 1:
                        link(ins)
                ins.then_inc(s_nrm, 1)
                dve.wait_ge(s_nrm, 8 + j)
            for t in range(NT):
                full(dve, ("rT", 1, t))
            rk3 = rk[:, :, :].rearrange("p t (h d) -> p t h d", h=H)
            for t in range(NT):
                taken(dve, ("rT", 0, t))
                link(tt(rk3[:, t], rk3[:, t], bc(cb("kdec"), 2, [P, H, HD]), ALU.mult))
                tt(rqdT[:, :, t * P:(t + 1) * P], rT[0][:, :, t * P:(t + 1) * P], blk3(cb("qdec")), ALU.mult).then_inc(s_rqd, 1)
            dve.wait_ge(s_rqd, NT)
            dve.nop().then_inc(s_kd, 1)
            attention(2, PR2, PT2, o2)
            dve.wait_ge(s_gn, 32)
            dve.wait_ge(s_sg, 1)
            dmat = cb("dmat").rearrange("p (h i) -> p h i", h=H)
            for n in range(NT):
                for j in range(2):
                    label = ("rS", n, j)
                    b = full(dve, label)
                    if n:
                        full(dve, ("rO", n - 1))
                    else:
                        full(dve, ("T", 2, 4 * H - 1))
                    take(tt(rS[:, j::2, :], blk3(b[:, :]), dmat[:, j::2, :], ALU.mult), label)
                if n < NT - 1:
                    label = ("rkv", n)
                    b = full(dve, label)
                    for par in range(2):
                        hp = slice(par * HD, (par + 1) * HD)
                        src = blk3(b[:, :])[hp, :, par * HD:(par + 1) * HD]
                        own = state[hp, :, par * HD:(par + 1) * HD]
                        if n == 0:
                            link(ve.memset(state[hp, :, (1 - par) * HD:(2 - par) * HD], 0.0))
                            ins = ve.tensor_copy(own, src)
                        else:
                            link(tt(own, own, bc(cb("gch")[hp, :], 2, [HD, 4, HD]), ALU.mult))
                            ins = tt(own, src, own, ALU.add)
                        if par == 0:
                            link(ins)
                    take(ins, label)
                    taken(dve, label)
                    dve.nop().then_inc(s_st, 1)
                label = ("rO", n)
                b = full(dve, label)
                take(ve.tensor_copy(gy[:, :, :], b[:, :].rearrange("p (h d) -> p h d", h=H)), label)
                taken(dve, label)
                st = hs[:, (9 + n) * 32:(9 + n) * 32 + 8]
                link(ve.reduce_sum(st, gy[:, :, :], axis=AX))
                link(ts(st, st, 1.0 / HD, None, ALU.mult))
                link(tt(gy[:, :, :], gy[:, :, :], bc(st, 2, [P, H, HD]), ALU.subtract))
                link(mean_square(gy[:, :, :], H, HD, st, gsq[:, :, :]))
                ve.tensor_copy(hs[:, (9 + n) * 32 + 8:(9 + n) * 32 + 32], st[:, 0:1].broadcast_to([P, 24])).then_inc(s_ms, 1)
                dve.wait_ge(s_rt, 10 + n)
                link(ve.reciprocal(st, st))
                link(tt(gy[:, :, :], gy[:, :, :], bc(st, 2, [P, H, HD]), ALU.mult))
                gf = gy[:, :, :].rearrange("p h d -> p (h d)")
                link(tt(gf, gf, gnrow[:, 0, :], ALU.mult))
                link(tt(gf, gf, gnrow[:, 1, :], ALU.add))
                if n >= 2:
                    full(dve, ("oT", 3, n - 2))
                else:
                    full(dve, ("oT", 2, n + 2))
                tt(o2[n % 2][:, :, :].rearrange("p h d -> p (h d)"), gf, rg[:, n, :], ALU.mult).then_inc(s_o, 1)
            ve.memset(zero[:, :], 0.0).then_inc(s_zero, 1)
            dve.wait_ge(s_bsum, 32)
            for c in range(3):
                part_ = slice(c * D, (c + 1) * D)
                for k in range(3):
                    b3 = bias3[k * NE:(k + 1) * NE, part_]
                    if k:
                        left, before = (bsum, btmp) if k == 1 else (brem, bsum)
                        back3 = before[:, :] if k == 1 else before[:, part_]
                        link(ve.tensor_tensor(brem[:, part_], left[:, part_], back3, ALU.subtract))
                    link(ve.tensor_copy(b3, (brem if k else bsum)[:, part_]))
                    if k < 2:
                        link(ve.tensor_copy(bsum[:, part_] if k else btmp[:, :], b3))
            dve.nop().then_inc(s_b3, 1)
            residual("wout2", None)
            dve.wait_ge(s_grf, 16)
            norm(3)
            def split(i, *os):
                for o in os:
                    split_lo(ve, i, o, s_lo)

            split(0, 0, 1, 2)
            dve.wait_ge(s_wrt, 32)
            b = full(dve, ("router",))
            take(tt(logits[:, :, :], b[:, 0:NT * NE].rearrange("p (t e) -> p t e", t=NT), bc(brt[:, :], 1, [P, NT, NE]), ALU.add), ("router",))
            taken(dve, ("router",))
            for t in range(NT):
                link(ve.max(top8[:, t, :], logits[:, t, :]))
                link(ve.max_index(topi[:, t, :], top8[:, t, :], logits[:, t, :]))
            link(ve.tensor_copy(topf[:, :, :], topi[:, :, :]))
            tt(gate4[:, :, :], top8[:, :, 0:4], top8[:, :, 0:1].broadcast_to([P, NT, 4]), ALU.subtract).then_inc(s_top, 1)
            split(0, 3)
            dve.wait_ge(s_ge, 1)
            link(ve.reduce_sum(den[:, 0:4], gate4[:, :, :], axis=AX))
            link(ve.reciprocal(den[:, 0:4], den[:, 0:4]))
            link(tt(gate4[:, :, :], gate4[:, :, :], bc(den[:, 0:4], 2, [P, NT, 4]), ALU.mult))
            dve.wait_ge(s_conc, 16)
            shape = [P, NT, NE]
            experts = bc(cc("iota")[:, 0:NE], 1, shape)
            link(ve.tensor_copy(route[:, :, 0], cc("tok")))
            link(ve.memset(route[:, :, 1], 1.0))
            for k in range(4):
                eq = chosen if k == 0 else eqk
                link(tt(eq[:, :, :], experts, topf[:, :, k:k + 1].broadcast_to(shape), ALU.is_equal))
                gk = gate4[:, :, k:k + 1].broadcast_to(shape)
                if k == 0:
                    link(tt(route[:, :, 2:], eq[:, :, :], gk, ALU.mult))
                else:
                    link(tt(chosen[:, :, :], chosen[:, :, :], eqk[:, :, :], ALU.add))
                    link(tt(eqk[:, :, :], eqk[:, :, :], gk, ALU.mult))
                    link(tt(route[:, :, 2:], route[:, :, 2:], eqk[:, :, :], ALU.add))
            link(ve.memset(ones[:, :], 1.0))
            dve.nop().then_inc(s_route, 1)
            def build(s_, i):
                if s_ is None:
                    e = first = 0
                else:
                    e = slot_reg(dve, 0, s_, NE - 1)
                    first = slot_reg(dve, 2, s_, 3 * P)
                for t in range(NT):
                    ins = ts(pick[:, t, :], cc("iota")[:, bass.ds(first, P)], rank[:, t, bass.ds(e, 1)], None, ALU.is_equal)
                ins.then_inc(s_pick, 1)

            def found(i, k):
                e = 0 if isinstance(i, int) and i == 0 else slot_reg(dve, 0, i, NE - 1)
                dve.wait_ge(bank_full[7], k)
                ve.tensor_copy(picked[:, :], bank[7][:, 0:2 + NE]).then_inc(bank_taken[7], 1)
                return e

            def index(i, e, k, got):
                dve.wait_ge(bank_taken[7], k)
                ts(idx_f[:, 0:1], picked[:, 1:2], -1.0, 1.0, ALU.mult, ALU.add).then_inc(s_empty, 1)
                dve.wait_ge(s_empty, i + 1)
                stt(idx_f[:, 1:2], idx_f[:, 0:1], cc("trash"), picked[:, 0:1], ALU.mult, ALU.add).then_inc(s_row, 1)
                ve.tensor_copy(gates[:, slot_at(i)], picked[:, bass.ds(e + 2, 1)]).then_inc(s_gate, 1)
                dve.wait_ge(s_row, i + 1)
                ve.tensor_copy(idx_all[:, slot_at(i)], idx_f[:, 1:2]).then_inc(s_gate, 1)
                if got is not None:
                    dve.wait_ge(s_got, got)
                ve.tensor_copy(idx_in[:, :], idx_f[:, 1:2]).then_inc(s_idx, 1)

            b = full(dve, ("rank",))
            link(ve.tensor_copy(cntp[:, :], b[:, NT * NE:(NT + 1) * NE]))
            take(tt(rank[:, :, :], b[:, 0:NT * NE].rearrange("p (t e) -> p t e", t=NT), chosen[:, :, :], ALU.mult), ("rank",))
            taken(dve, ("rank",))
            link(ts(rank[:, :, :], rank[:, :, :], -1.0, None, ALU.add))
            build(None, 0)
            for k in range(1, 4):
                link(ts(nblk[:, k, :], cntp[:, :], float(k * P), None, ALU.is_gt))
            link(tt(nblk[:, 0, :], nblk[:, 1, :], nblk[:, 2, :], ALU.add))
            link(tt(nblk[:, 0, :], nblk[:, 0, :], nblk[:, 3, :], ALU.add))
            link(ts(nblk[:, 0, :], nblk[:, 0, :], 1.0, None, ALU.add))
            link(ve.tensor_tensor_scan(ends[:, :], one[:, 0:1].broadcast_to([P, NE]), nblk[:, 0, :], 0.0, ALU.mult, ALU.add))
            e = found(0, FU[7] + 1)
            index(0, e, TK[7] + 1, None)
            shape = [P, MAXSLOT, NE]
            link(tt(cmp[:, :, :], bc(ends[:, :], 1, shape), bc(cc("slots"), 2, shape), ALU.is_le))
            link(ve.reduce_sum(slot_f[:, 0, :], cmp[:, :, :], axis=AX))
            link(ts(slot_f[:, 0, :], slot_f[:, 0, :], NE - 1.0, None, ALU.min))
            link(tt(cmp[:, :, :], cmp[:, :, :], bc(ends[:, :], 1, shape), ALU.mult))
            link(ve.tensor_reduce(slot_f[:, 1, :], cmp[:, :, :], AX, ALU.max))
            link(tt(slot_f[:, 2, :], cc("slots"), slot_f[:, 1, :], ALU.subtract))
            link(ts(slot_f[:, 2, :], slot_f[:, 2, :], float(P), None, ALU.mult))
            link(ve.tensor_copy(slot_i[:, :, :], slot_f[:, :, :]))
            ve.tensor_copy(nb_i[:, :], ends[:, NE - 1:NE]).then_inc(s_slots, 1)

            def gate_part(i, j):
                dve.wait_ge(bank_full[j], FU[j] + 1 + i)
                ts(eg[j][:, :], bank[j][:, :], 7.0, None, ALU.min).then_inc(bank_taken[j], 1)

            def linear_part(i, j):
                dve.wait_ge(bank_full[2 + j], FU[2 + j] + 1 + i)
                ts(el[j][:, :], bank[2 + j][:, :], -7.0, 7.0, ALU.max, ALU.min).then_inc(bank_taken[2 + j], 1)
                dve.wait_ge(bank_taken[2 + j], TK[2 + j] + 1 + i)
                dve.wait_ge(s_sig, 2 * i + (j + 1))
                e_ = ea[:, j * CW:(j + 1) * CW]
                stt(el[j][:, :], el[j][:, :], 1.0, e_, ALU.add, ALU.mult).then_inc(s_lin, 1)
                dve.wait_ge(s_lin, 2 * i + (j + 1))
                tt(e_, el[j][:, :], eg[j][:, :], ALU.mult).then_inc(s_ea, 1)

            def rest_T(dst, n):
                for j, b in enumerate((6, 7)):
                    dve.wait_ge(s_xhi, n + j + 1)
                    k = slice(4 * j, 4 * j + 4)
                    tt(dst[1][:, k, :], blk3(bank[b][:, :]), dst[0][:, k, :].bitcast(FP), ALU.subtract).then_inc(bank_taken[b], 1)

            def hot_row(dst, s_, s):
                ts(dst[:, :], cc("pmod")[0:3 * NE, :], slot_f[0:3 * NE, 0, slot_at(s_)], None, ALU.is_equal).then_inc(s, 1)

            dve.wait_ge(s_slots, 1)
            build(1, 1)
            hot_row(hot[0], 0, s_hotu)
            rest_T(xeT, 0)
            split(0, 5)
            e = found(1, FU[7] + 3)
            index(1, e, TK[7] + 3, 16)
            build(2, 2)
            split(0, 6, 7)
            gate_part(0, 0)
            split(0, 8)
            linear_part(0, 0)
            split(0, 10)
            gate_part(0, 1)
            split(0, 11)
            linear_part(0, 1)
            hot_row(hot[0], 1, s_hotu)
            rest_T(xeT, 2)
            nb = n_slots(dve)
            with dve.Fori(1, nb) as i:
                e = found(i + 1, 3 * i + (FU[7] + 2))
                index(i + 1, e, 3 * i + (TK[7] + 2), 16 * i + 16)
                rest_T(eaT, 4 * i)
                dve.wait_ge(bank_full[5], i + (FU[5] - 1))
                hot_row(hot[1], i - 1, s_hotd)
                split(i, 0, 1, 2)
                gate_part(i, 0)
                split(i, 3)
                build(i + 2, i + 2)
                split(i, 5)
                linear_part(i, 0)
                split(i, 6)
                gate_part(i, 1)
                split(i, 7, 8)
                linear_part(i, 1)
                hot_row(hot[0], i + 1, s_hotu)
                rest_T(xeT, 4 * i + 2)
                dve.wait_ge(s_scat, 16 * i)
                dve.wait_ge(s_gate, 2 * i)
                ve.tensor_copy(idx_out[:, :], idx_all[:, bass.ds(i - 1, 1)]).then_inc(s_ix, 1)
                split(i, 10, 11)
            rest_T(eaT, 4 * nb)
            dve.wait_ge(bank_full[5], nb + (FU[5] - 1))
            hot_row(hot[1], nb - 1, s_hotd)
            dve.wait_ge(s_scat, 16 * nb)
            ve.tensor_copy(idx_out[:, :], idx_all[:, bass.ds(nb - 1, 1)]).then_inc(s_ix, 1)
            norm(4)
            for t in range(NT):
                for n in range(2):
                    taken(dve, ("gate", t, n))
                if t >= 2:
                    dve.wait_ge(s_stored[t % 2], 16 * (t // 2))
                link(tt(xo[t % 2][:, :], pp[:, t, :], fgate[t % 2][:, :], ALU.mult))
                tt(xo[t % 2][:, :], xo[t % 2][:, :], x[:, t, :], ALU.add).then_inc(s_out, 1)


_INPUTS = ("x", "c", "positions", "w_ada", "b_ada", "g_attn_norm", "w_in", "g_q_latent", "g_kv_latent", "w_q_up", "w_kv_up",
           "g_mla_q", "g_mla_k", "g_ca_q", "g_ca_k", "rel_bias", "w_out", "g_mlp_norm", "w_up", "conv_w", "conv_b", "w_down",
           "p_2", "positions_2", "g_mix_norm_2", "w_in_2", "sb_q_gain_2", "sb_k_gain_2", "ret_q_gain_2", "ret_k_gain_2",
           "ret_gn_gain_2", "ret_gn_bias_2", "w_out_2", "g_ffn_norm_2", "w_router_2", "b_router_2", "w_up_gate_2",
           "b_up_gate_2", "w_down_2", "b_down_2", "g_ple_norm_2", "w_ple_gate_2", "w_ple_proj_2")


def kernel(**inputs):
    import concourse.bacc as bacc
    from concourse.bass_utils import run_bass_kernel_spmd

    nc = bacc.Bacc("TRN2", target_bir_lowering=False, num_devices=1)
    arrays = {f"in_{name}": np.ascontiguousarray(inputs[name]) for name in _INPUTS}
    arrays["in_consts"] = constants()[2]
    g = {name[3:]: nc.dram_tensor(name, a.shape, mybir.dt.from_np(a.dtype), kind="ExternalInput").ap() for name, a in arrays.items()}
    out = nc.dram_tensor("out", (1, S, D), FP, kind="ExternalOutput").ap()
    program(nc, g, out)
    r = run_bass_kernel_spmd(nc, [arrays], core_ids=[0])
    return r.results[0]["out"]
```
